# Optimizing a Trainium2 kernel written in Bass

```python
import math
import jax
import jax.numpy as jnp
from jax import lax
import numpy as np

D_MODEL = 1024
BATCH = 1
SEQ = 256
DEPTH = 1

N_HEADS_DIL = 6
N_HEADS_MOBA = 6
N_HEADS_MEM = 4
N_HEADS_MIX = N_HEADS_DIL + N_HEADS_MOBA + N_HEADS_MEM
HEAD_DIM = D_MODEL // N_HEADS_MIX
W_DIL = N_HEADS_DIL * HEAD_DIM
W_MOBA = N_HEADS_MOBA * HEAD_DIM
W_MEM = N_HEADS_MEM * HEAD_DIM
MIX_WIDTH = W_DIL + W_MOBA + W_MEM
IN_WIDTH = 3 * W_DIL + 3 * W_MOBA + W_MEM
DIL_CONFIGS = ((128, 1), (512, 4), (2048, 16))
BAND_BLOCK = 128
MOBA_BLOCK = 256
MOBA_TOPK = 3
MOBA_QBLOCK = 128
MEM_LEN = 256
PEER_HEADS = 8
PEER_NKEYS = 128
PEER_EXPERTS = PEER_NKEYS * PEER_NKEYS
PEER_TOPK = 16
PEER_DKEY = 256
PEER_CHUNK = 128
RMS_EPS = 1e-6
NEG_INF = -1e30


def rms_norm(a, g):
    af = a.astype(jnp.float32)
    y = af * lax.rsqrt(jnp.mean(af * af, axis=-1, keepdims=True) + RMS_EPS)
    return (y * g.astype(jnp.float32)).astype(a.dtype)

def split_heads(a, n_heads):
    b, s, _ = a.shape
    return a.reshape(b, s, n_heads, HEAD_DIM).transpose(0, 2, 1, 3)

def merge_heads(a):
    b, h, s, dh = a.shape
    return a.transpose(0, 2, 1, 3).reshape(b, s, h * dh)

def alibi_slopes(n):
    return jnp.exp2(-8.0 * jnp.arange(1, n + 1, dtype=jnp.float32) / n)

def dilated_branch(q, k, v, slopes, window, dilation):
    B, H, S, Dh = q.shape
    L = S // dilation
    n_blk = -(-L // BAND_BLOCK)
    Lp = n_blk * BAND_BLOCK
    reach = window // dilation

    def split(a):
        a = a.reshape(B, H, L, dilation, Dh).transpose(0, 1, 3, 2, 4)
        a = jnp.pad(a, ((0, 0), (0, 0), (0, 0), (0, Lp - L), (0, 0)))
        return a.reshape(B, H, dilation, n_blk, BAND_BLOCK, Dh)

    def with_prev(a):
        prev = jnp.pad(a, ((0, 0), (0, 0), (0, 0), (1, 0), (0, 0), (0, 0)))[:, :, :, :-1]
        return jnp.concatenate([prev, a], axis=4)

    qb = split(q)
    kc = with_prev(split(k))
    vc = with_prev(split(v))
    s = jnp.einsum('bhrnqd,bhrnkd->bhrnqk', qb, kc).astype(jnp.float32) * (1.0 / math.sqrt(Dh))
    ql = jnp.arange(BAND_BLOCK)[:, None]
    kl = jnp.arange(2 * BAND_BLOCK)[None, :]
    delta = BAND_BLOCK + ql - kl
    blk = jnp.arange(n_blk)[:, None, None]
    valid = (delta >= 0) & (delta <= reach) & (blk * BAND_BLOCK - BAND_BLOCK + kl[None] >= 0)
    bias = -slopes[:, None, None, None, None] * (delta * dilation).astype(jnp.float32)
    s = jnp.where(valid, s + bias, NEG_INF)
    m = jnp.max(s, axis=-1, keepdims=True)
    p = jnp.exp(s - m)
    den = jnp.sum(p, axis=-1, keepdims=True)
    lse = m[..., 0] + jnp.log(den[..., 0])
    o = jnp.einsum('bhrnqk,bhrnkd->bhrnqd', p.astype(v.dtype), vc) / den.astype(v.dtype)

    def merge(a):
        tail = a.shape[5:]
        a = a.reshape((B, H, dilation, Lp) + tail)[:, :, :, :L]
        a = jnp.moveaxis(a, 2, 3)
        return a.reshape((B, H, S) + tail)

    return merge(o), merge(lse)

def dilated_mixture(q, k, v, slopes):
    outs, lses = [], []
    for window, dilation in DIL_CONFIGS:
        o, l = dilated_branch(q, k, v, slopes, window, dilation)
        outs.append(o)
        lses.append(l)
    wts = jax.nn.softmax(jnp.stack(lses, axis=0), axis=0).astype(q.dtype)
    return jnp.einsum('cbhs,cbhsd->bhsd', wts, jnp.stack(outs, axis=0))

def moba_attention(q, k, v, slopes):
    B, H, S, Dh = q.shape
    n_blk = -(-S // MOBA_BLOCK)
    Sp = n_blk * MOBA_BLOCK
    pad = ((0, 0), (0, 0), (0, Sp - S), (0, 0))
    kb = jnp.pad(k, pad).reshape(B, H, n_blk, MOBA_BLOCK, Dh)
    vb = jnp.pad(v, pad).reshape(B, H, n_blk, MOBA_BLOCK, Dh)
    k_mean = jnp.mean(kb.astype(jnp.float32), axis=3).astype(k.dtype)
    gate = jnp.einsum('bhsd,bhnd->bhsn', q, k_mean).astype(jnp.float32)
    n_past = jnp.arange(S) // MOBA_BLOCK
    past = jnp.arange(n_blk)[None, :] < n_past[:, None]
    gate = jnp.where(past, gate, NEG_INF)
    k_sel = min(MOBA_TOPK, n_blk)
    _, sel = lax.top_k(gate, k_sel)

    n_qb = S // MOBA_QBLOCK
    qq = q.reshape(B, H, n_qb, MOBA_QBLOCK, Dh).transpose(0, 2, 1, 3, 4).reshape(B * n_qb, H, MOBA_QBLOCK, Dh)
    ss = sel.reshape(B, H, n_qb, MOBA_QBLOCK, k_sel).transpose(0, 2, 1, 3, 4).reshape(B * n_qb, H, MOBA_QBLOCK, k_sel)
    b_ids = jnp.repeat(jnp.arange(B, dtype=jnp.int32), n_qb)
    n_ids = jnp.tile(jnp.arange(n_qb, dtype=jnp.int32), B)
    head = jnp.arange(H)[:, None, None]
    scale = 1.0 / math.sqrt(Dh)
    n_sel_keys = k_sel * MOBA_BLOCK

    def step(args):
        q_blk, sel_blk, b, n = args
        kb_b = lax.dynamic_index_in_dim(kb, b, axis=0, keepdims=False)
        vb_b = lax.dynamic_index_in_dim(vb, b, axis=0, keepdims=False)
        t_q = n * MOBA_QBLOCK + jnp.arange(MOBA_QBLOCK)
        k_g = kb_b[head, sel_blk]
        v_g = vb_b[head, sel_blk]
        s_sel = jnp.einsum('hqd,hqjkd->hqjk', q_blk, k_g).astype(jnp.float32) * scale
        s_pos = sel_blk[..., None] * MOBA_BLOCK + jnp.arange(MOBA_BLOCK)
        ok = jnp.arange(k_sel)[None, :] < (t_q // MOBA_BLOCK)[:, None]
        dist_sel = (t_q[None, :, None, None] - s_pos).astype(jnp.float32)
        s_sel = jnp.where(ok[None, :, :, None], s_sel - slopes[:, None, None, None] * dist_sel, NEG_INF)
        own = (n * MOBA_QBLOCK) // MOBA_BLOCK
        k_own = lax.dynamic_index_in_dim(kb_b, own, axis=1, keepdims=False)
        v_own = lax.dynamic_index_in_dim(vb_b, own, axis=1, keepdims=False)
        o_pos = own * MOBA_BLOCK + jnp.arange(MOBA_BLOCK)
        dist_own = t_q[:, None] - o_pos[None, :]
        s_own = jnp.einsum('hqd,hkd->hqk', q_blk, k_own).astype(jnp.float32) * scale
        s_own = jnp.where(dist_own >= 0, s_own - slopes[:, None, None] * dist_own.astype(jnp.float32), NEG_INF)
        s_all = jnp.concatenate([s_sel.reshape(H, MOBA_QBLOCK, n_sel_keys), s_own], axis=-1)
        p = jax.nn.softmax(s_all, axis=-1).astype(v.dtype)
        p_sel = p[..., :n_sel_keys].reshape(H, MOBA_QBLOCK, k_sel, MOBA_BLOCK)
        p_own = p[..., n_sel_keys:]
        return (jnp.einsum('hqjk,hqjkd->hqd', p_sel, v_g)
                + jnp.einsum('hqk,hkd->hqd', p_own, v_own))

    out = lax.map(step, (qq, ss, b_ids, n_ids))
    return out.reshape(B, n_qb, H, MOBA_QBLOCK, Dh).transpose(0, 2, 1, 3, 4).reshape(B, H, S, Dh)

def memory_attention(q, k, v):
    s = jnp.einsum('bhsd,bhmd->bhsm', q, k).astype(jnp.float32) * (1.0 / math.sqrt(q.shape[-1]))
    p = jax.nn.softmax(s, axis=-1).astype(v.dtype)
    return jnp.einsum('bhsm,bhmd->bhsd', p, v)

def peer_ffn(h, w_q, sub1, sub2, u, v):
    B, S, D = h.shape
    half = PEER_DKEY // 2
    qry = (h @ w_q).reshape(B, S, PEER_HEADS, PEER_DKEY)
    s1 = jnp.einsum('bshd,hkd->bshk', qry[..., :half], sub1).astype(jnp.float32)
    s2 = jnp.einsum('bshd,hkd->bshk', qry[..., half:], sub2).astype(jnp.float32)
    v1, i1 = lax.top_k(s1, PEER_TOPK)
    v2, i2 = lax.top_k(s2, PEER_TOPK)
    cand = (v1[..., :, None] + v2[..., None, :]).reshape(B, S, PEER_HEADS, PEER_TOPK * PEER_TOPK)
    cand_idx = (i1[..., :, None] * PEER_NKEYS + i2[..., None, :]).reshape(B, S, PEER_HEADS, PEER_TOPK * PEER_TOPK)
    top_s, pos = lax.top_k(cand, PEER_TOPK)
    expert = jnp.take_along_axis(cand_idx, pos, axis=-1)
    gate = jax.nn.softmax(top_s, axis=-1)
    T = B * S
    E = PEER_HEADS * PEER_TOPK
    n_chunk = T // PEER_CHUNK
    hx = h.reshape(n_chunk, PEER_CHUNK, D)
    ex = expert.reshape(n_chunk, PEER_CHUNK, E)
    gx = gate.reshape(n_chunk, PEER_CHUNK, E).astype(h.dtype)

    def step(args):
        x_c, e_c, g_c = args
        a = jnp.einsum('cd,ced->ce', x_c, u[e_c])
        w = jax.nn.gelu(a.astype(jnp.float32), approximate=False).astype(x_c.dtype) * g_c
        return jnp.einsum('ce,ced->cd', w, v[e_c])

    return lax.map(step, (hx, ex, gx)).reshape(B, S, D)

def hybrid_layer(x, mem, g_mix, w_in, qg_dil, kg_dil, qg_moba, kg_moba, qg_mem, kg_mem, g_memtok, w_mem_kv,
                 og_dil, og_moba, og_mem, w_out, g_ffn, w_peer_q, sub1, sub2, peer_u, peer_v):
    slopes = alibi_slopes(N_HEADS_DIL + N_HEADS_MOBA)
    sl_dil, sl_moba = slopes[0::2], slopes[1::2]
    hn = rms_norm(x, g_mix)
    proj = hn @ w_in
    cuts = [W_DIL, 2 * W_DIL, 3 * W_DIL, 3 * W_DIL + W_MOBA, 3 * W_DIL + 2 * W_MOBA, 3 * W_DIL + 3 * W_MOBA]
    q_d, k_d, v_d, q_b, k_b, v_b, q_m = jnp.split(proj, cuts, axis=-1)
    q_d = rms_norm(split_heads(q_d, N_HEADS_DIL), qg_dil)
    k_d = rms_norm(split_heads(k_d, N_HEADS_DIL), kg_dil)
    o_dil = dilated_mixture(q_d, k_d, split_heads(v_d, N_HEADS_DIL), sl_dil)
    q_b = rms_norm(split_heads(q_b, N_HEADS_MOBA), qg_moba)
    k_b = rms_norm(split_heads(k_b, N_HEADS_MOBA), kg_moba)
    o_moba = moba_attention(q_b, k_b, split_heads(v_b, N_HEADS_MOBA), sl_moba)
    kv = rms_norm(mem, g_memtok) @ w_mem_kv
    k_m, v_m = jnp.split(kv, 2, axis=-1)
    q_m = rms_norm(split_heads(q_m, N_HEADS_MEM), qg_mem)
    k_m = rms_norm(split_heads(k_m, N_HEADS_MEM), kg_mem)
    o_mem = memory_attention(q_m, k_m, split_heads(v_m, N_HEADS_MEM))
    y = jnp.concatenate([rms_norm(merge_heads(o_dil), og_dil),
                         rms_norm(merge_heads(o_moba), og_moba),
                         rms_norm(merge_heads(o_mem), og_mem)], axis=-1) @ w_out
    x = x + y
    x = x + peer_ffn(rms_norm(x, g_ffn), w_peer_q, sub1, sub2, peer_u, peer_v)
    return x

def first_inputs(seed: int = 0) -> dict:
    key = jax.random.key(seed)
    ks = jax.random.split(key, 24)

    def nrm(k, shape, scale):
        return jax.random.normal(k, shape, jnp.float32) * scale

    def gain(k, n):
        return 1.0 + 0.02 * jax.random.normal(k, (DEPTH, n), jnp.float32)

    return {
        'x': nrm(ks[0], (BATCH, SEQ, D_MODEL), 1.0),
        'mem': nrm(ks[1], (BATCH, MEM_LEN, D_MODEL), 1.0),
        'g_mix': gain(ks[2], D_MODEL),
        'w_in': nrm(ks[3], (DEPTH, D_MODEL, IN_WIDTH), D_MODEL ** -0.5),
        'qg_dil': gain(ks[4], HEAD_DIM),
        'kg_dil': gain(ks[5], HEAD_DIM),
        'qg_moba': gain(ks[6], HEAD_DIM),
        'kg_moba': gain(ks[7], HEAD_DIM),
        'qg_mem': gain(ks[8], HEAD_DIM),
        'kg_mem': gain(ks[9], HEAD_DIM),
        'g_memtok': gain(ks[10], D_MODEL),
        'w_mem_kv': nrm(ks[11], (DEPTH, D_MODEL, 2 * W_MEM), D_MODEL ** -0.5),
        'og_dil': gain(ks[12], W_DIL),
        'og_moba': gain(ks[13], W_MOBA),
        'og_mem': gain(ks[14], W_MEM),
        'w_out': nrm(ks[15], (DEPTH, MIX_WIDTH, D_MODEL), MIX_WIDTH ** -0.5),
        'g_ffn': gain(ks[16], D_MODEL),
        'w_peer_q': nrm(ks[17], (DEPTH, D_MODEL, PEER_HEADS * PEER_DKEY), D_MODEL ** -0.5),
        'peer_subkeys_1': nrm(ks[18], (DEPTH, PEER_HEADS, PEER_NKEYS, PEER_DKEY // 2), (PEER_DKEY // 2) ** -0.5),
        'peer_subkeys_2': nrm(ks[19], (DEPTH, PEER_HEADS, PEER_NKEYS, PEER_DKEY // 2), (PEER_DKEY // 2) ** -0.5),
        'peer_u': nrm(ks[20], (DEPTH, PEER_EXPERTS, D_MODEL), D_MODEL ** -0.5),
        'peer_v': nrm(ks[21], (DEPTH, PEER_EXPERTS, D_MODEL), PEER_HEADS ** -0.5),
    }

def first_block(x, mem, g_mix, w_in, qg_dil, kg_dil, qg_moba, kg_moba, qg_mem, kg_mem, g_memtok, w_mem_kv,
              og_dil, og_moba, og_mem, w_out, g_ffn, w_peer_q, peer_subkeys_1, peer_subkeys_2, peer_u, peer_v):
    h = x
    for layer in range(DEPTH):
        h = hybrid_layer(h, mem, g_mix[layer], w_in[layer], qg_dil[layer], kg_dil[layer], qg_moba[layer],
                         kg_moba[layer], qg_mem[layer], kg_mem[layer], g_memtok[layer], w_mem_kv[layer],
                         og_dil[layer], og_moba[layer], og_mem[layer], w_out[layer], g_ffn[layer],
                         w_peer_q[layer], peer_subkeys_1[layer], peer_subkeys_2[layer], peer_u[layer],
                         peer_v[layer])
    return h


DEPTH_2 = 2

RW_HEADS = 8
RW_HEAD = 64
RW_DIM = RW_HEADS * RW_HEAD
RW_LORA_W = 64
RW_LORA_A = 64
RW_LORA_G = 128
RW_SPLITS = [RW_DIM, 2 * RW_DIM, 3 * RW_DIM, 3 * RW_DIM + RW_LORA_W,
             3 * RW_DIM + RW_LORA_W + RW_LORA_A]
SG_GROUPS = 4
SG_CHUNK = 128
SG_GROUP_DIM = 128
SG_DIM = SG_GROUPS * SG_GROUP_DIM
AB_SHIFT_DIM = 3 * RW_DIM + RW_LORA_W + RW_LORA_A + RW_LORA_G
AB_IN_DIM = AB_SHIFT_DIM + 2 * SG_DIM
AB_MIX_DIM = RW_DIM + SG_DIM

MLA_HEADS = 16
MLA_Q_RANK = 256
MLA_KV_RANK = 256
MLA_NOPE = 64
MLA_ROPE = 32
MLA_V = 64
MLA_QK = MLA_NOPE + MLA_ROPE
MLA_IN_DIM = MLA_Q_RANK + MLA_KV_RANK + MLA_ROPE
MLA_MIX_DIM = MLA_HEADS * MLA_V
ROPE_THETA = 10000.0
Q_BLOCK = 128

XA_HEADS = 4
XA_HEAD = D_MODEL // XA_HEADS

MOE_GROUPS = 4
MOE_PER_GROUP = 8
MOE_EXPERTS = MOE_GROUPS * MOE_PER_GROUP
MOE_TOPK = 2
MOE_FF = 512
MOE_BLOCK = 128

DN_ALPHA = (2 * DEPTH_2) ** 0.25
DN_BETA = (8 * DEPTH_2) ** -0.25
LN_EPS = 1e-5
RW_GN_EPS = 64e-5
N_EVEN = (DEPTH_2 + 1) // 2
N_ODD = DEPTH_2 // 2


def _standardize(x, eps):
    xf = x.astype(jnp.float32)
    mu = jnp.mean(xf, -1, keepdims=True)
    var = jnp.mean(jnp.square(xf - mu), -1, keepdims=True)
    return ((xf - mu) * lax.rsqrt(var + eps)).astype(x.dtype)

def layer_norm(x, g, b, eps=LN_EPS):
    return _standardize(x, eps) * g + b

def rms_norm_2(x, g, eps=RMS_EPS):
    xf = x.astype(jnp.float32)
    return (xf * lax.rsqrt(jnp.mean(xf * xf, -1, keepdims=True) + eps)).astype(x.dtype) * g

def token_shift(p):
    return jnp.pad(p, ((0, 0), (1, 0), (0, 0)))[:, :-1]

def rwkv7_recurrence(r, w, k, v, kk, a):
    B, S, H, N = r.shape

    def step(state, inp):
        r_t, w_t, k_t, v_t, kk_t, a_t = inp
        sa = jnp.einsum('bhvk,bhk->bhv', state, -kk_t)
        state = (state * w_t[:, :, None, :]
                 + sa[..., None] * (kk_t * a_t)[:, :, None, :]
                 + v_t[..., None] * k_t[:, :, None, :])
        return state, jnp.einsum('bhvk,bhk->bhv', state, r_t)

    xs = tuple(jnp.moveaxis(t.astype(jnp.float32), 1, 0) for t in (r, w, k, v, kk, a))
    state0 = jnp.zeros((B, H, N, N), jnp.float32)
    _, y = lax.scan(step, state0, xs)
    return jnp.moveaxis(y, 0, 1)

def rwkv7_mix(p, w0, w2, a0, a2, g2, k_k, k_a, r_k, gn_g, gn_b):
    B, S, _ = p.shape
    heads = lambda t: t.reshape(B, S, RW_HEADS, RW_HEAD)
    r, k, v, w_lo, a_lo, g_lo = jnp.split(p, RW_SPLITS, axis=-1)
    w_log = -jax.nn.softplus(-(w0 + jnp.tanh(w_lo) @ w2)) - 0.5
    decay = jnp.exp(-jnp.exp(w_log.astype(jnp.float32)))
    a = jax.nn.sigmoid(a0 + a_lo @ a2)
    g = jax.nn.sigmoid(g_lo) @ g2
    kk = heads(k * k_k).astype(jnp.float32)
    kk = kk / jnp.maximum(jnp.sqrt(jnp.sum(kk * kk, -1, keepdims=True)), 1e-12)
    k = k * (1.0 + (a - 1.0) * k_a)
    r_h, k_h, v_h = heads(r), heads(k), heads(v)
    y = rwkv7_recurrence(r_h, heads(decay), k_h, v_h, kk, heads(a))
    y = _standardize(y, RW_GN_EPS).astype(p.dtype).reshape(B, S, RW_DIM) * gn_g + gn_b
    bonus = jnp.sum(r_h * k_h * r_k, -1, keepdims=True) * v_h
    return (y + bonus.reshape(B, S, RW_DIM)) * g

def spatial_gating(pu, pv, ln_g, ln_b, ws, bs):
    B, S, _ = pu.shape
    n_chunk = S // SG_CHUNK
    u = jax.nn.gelu(pu)
    z = jax.nn.gelu(pv).reshape(B, n_chunk, SG_CHUNK, SG_GROUPS, SG_GROUP_DIM)
    z = layer_norm(z, ln_g, ln_b)
    causal = jnp.tril(jnp.ones((SG_CHUNK, SG_CHUNK), dtype=bool))
    wm = jnp.where(causal, ws, jnp.zeros_like(ws))
    zs = jnp.einsum('gts,bcsgd->bctgd', wm, z) + bs.T[:, :, None]
    return u * zs.reshape(B, S, SG_DIM)

def mixer_ab(x, w_in, mu, w0, w2, a0, a2, g2, k_k, k_a, r_k, gn_g, gn_b,
             ln_g, ln_b, ws, bs, w_out):
    p = x @ w_in
    ps = p[..., :AB_SHIFT_DIM]
    pu = p[..., AB_SHIFT_DIM:AB_SHIFT_DIM + SG_DIM]
    pv = p[..., AB_SHIFT_DIM + SG_DIM:]
    ps = ps + (token_shift(ps) - ps) * mu
    ya = rwkv7_mix(ps, w0, w2, a0, a2, g2, k_k, k_a, r_k, gn_g, gn_b)
    yb = spatial_gating(pu, pv, ln_g, ln_b, ws, bs)
    return jnp.concatenate([ya, yb], axis=-1) @ w_out

def rope(x):
    S = x.shape[1]
    half = x.shape[-1] // 2
    inv = ROPE_THETA ** (-jnp.arange(half, dtype=jnp.float32) / half)
    ang = jnp.arange(S, dtype=jnp.float32)[:, None] * inv[None, :]
    cos = jnp.cos(ang)[None, :, None, :]
    sin = jnp.sin(ang)[None, :, None, :]
    xf = x.astype(jnp.float32)
    x1, x2 = xf[..., :half], xf[..., half:]
    return jnp.concatenate([x1 * cos - x2 * sin, x1 * sin + x2 * cos], -1).astype(x.dtype)

def causal_block_attention(q, k, v):
    B, S, H, Dk = q.shape
    n_blk = S // Q_BLOCK
    scale = Dk ** -0.5
    qb = jnp.moveaxis(q.reshape(B, n_blk, Q_BLOCK, H, Dk), 1, 0)
    k_idx = jnp.arange(S)

    def one_block(args):
        q_blk, i = args
        s = jnp.einsum('bqhd,bkhd->bhqk', q_blk, k).astype(jnp.float32) * scale
        q_idx = i * Q_BLOCK + jnp.arange(Q_BLOCK)
        s = jnp.where(k_idx[None, :] <= q_idx[:, None], s, -jnp.inf)
        pr = jax.nn.softmax(s, axis=-1).astype(v.dtype)
        return jnp.einsum('bhqk,bkhd->bqhd', pr, v)

    o = lax.map(one_block, (qb, jnp.arange(n_blk)))
    return jnp.moveaxis(o, 0, 1).reshape(B, S, H, v.shape[-1])

def mla(x, w_in, q_norm, kv_norm, wq_b, wkv_b, w_out):
    B, S, _ = x.shape
    p = x @ w_in
    cq = p[..., :MLA_Q_RANK]
    ckv = p[..., MLA_Q_RANK:MLA_Q_RANK + MLA_KV_RANK]
    k_pe = p[..., MLA_Q_RANK + MLA_KV_RANK:]
    q = (rms_norm_2(cq, q_norm) @ wq_b).reshape(B, S, MLA_HEADS, MLA_QK)
    kv = (rms_norm_2(ckv, kv_norm) @ wkv_b).reshape(B, S, MLA_HEADS, MLA_NOPE + MLA_V)
    q_nope, q_pe = q[..., :MLA_NOPE], rope(q[..., MLA_NOPE:])
    k_nope, v = kv[..., :MLA_NOPE], kv[..., MLA_NOPE:]
    k_pe = rope(k_pe[:, :, None, :])
    qf = jnp.concatenate([q_nope, q_pe], -1)
    kf = jnp.concatenate([k_nope, jnp.broadcast_to(k_pe, (B, S, MLA_HEADS, MLA_ROPE))], -1)
    o = causal_block_attention(qf, kf, v)
    return o.reshape(B, S, MLA_MIX_DIM) @ w_out

def mem_cross_attention(x, mem, wq, wkv, wo):
    B, S, D = x.shape
    M = mem.shape[1]
    q = (x @ wq).reshape(B, S, XA_HEADS, XA_HEAD)
    kv = (mem @ wkv).reshape(B, M, 2, XA_HEADS, XA_HEAD)
    k, v = kv[:, :, 0], kv[:, :, 1]
    s = jnp.einsum('bqhd,bmhd->bhqm', q, k).astype(jnp.float32) * (XA_HEAD ** -0.5)
    pr = jax.nn.softmax(s, axis=-1).astype(v.dtype)
    o = jnp.einsum('bhqm,bmhd->bqhd', pr, v)
    return o.reshape(B, S, D) @ wo

def grouped_experts(xf, expert, gate, w_gate, w_up, w_down):
    T, D = xf.shape
    A = T * MOE_TOPK
    n_blk = -(-A // MOE_BLOCK) + MOE_EXPERTS
    L = n_blk * MOE_BLOCK
    flat_e = expert.reshape(-1)
    order = jnp.argsort(flat_e)
    sorted_e = flat_e[order]
    tok = (order // MOE_TOPK).astype(jnp.int32)
    counts = jnp.bincount(flat_e, length=MOE_EXPERTS)
    padded = (counts + MOE_BLOCK - 1) // MOE_BLOCK * MOE_BLOCK
    pad_end = jnp.cumsum(padded)
    pad_start = pad_end - padded
    start = jnp.cumsum(counts) - counts
    dest = (pad_start[sorted_e] + jnp.arange(A) - start[sorted_e]).astype(jnp.int32)
    row_tok = jnp.full((L,), T, dtype=jnp.int32).at[dest].set(tok)
    blk_expert = jnp.minimum(
        jnp.searchsorted(pad_end, jnp.arange(n_blk) * MOE_BLOCK, side='right'),
        MOE_EXPERTS - 1)
    x_rows = jnp.concatenate([xf, jnp.zeros((1, D), xf.dtype)], 0)[row_tok]
    x_rows = x_rows.reshape(n_blk, MOE_BLOCK, D)

    def expert_block(args):
        xb, e = args
        h = jax.nn.silu(xb @ w_gate[e]) * (xb @ w_up[e])
        return h @ w_down[e]

    y_rows = lax.map(expert_block, (x_rows, blk_expert)).reshape(L, D)
    y_assign = y_rows[dest] * gate.reshape(-1)[order][:, None]
    return jax.ops.segment_sum(y_assign, tok, num_segments=T)

def hier_moe(x, w_group, b_group, w_expert, b_expert, w_gate, w_up, w_down):
    B, S, D = x.shape
    xf = x.reshape(-1, D)
    T = xf.shape[0]
    g_logits = (xf @ w_group).astype(jnp.float32) + b_group
    g_prob = jax.nn.softmax(g_logits, axis=-1)
    grp = jnp.argmax(g_logits, axis=-1)
    p_grp = jnp.take_along_axis(g_prob, grp[:, None], axis=-1)
    e_logits = ((xf @ w_expert).astype(jnp.float32) + b_expert).reshape(
        T, MOE_GROUPS, MOE_PER_GROUP)
    e_logits = jnp.take_along_axis(e_logits, grp[:, None, None], axis=1)[:, 0]
    top_v, top_i = lax.top_k(e_logits, MOE_TOPK)
    gate = (jax.nn.softmax(top_v, axis=-1) * p_grp).astype(x.dtype)
    expert = (grp[:, None] * MOE_PER_GROUP + top_i).astype(jnp.int32)
    y = grouped_experts(xf, expert, gate, w_gate, w_up, w_down)
    return y.reshape(B, S, D)

def second_inputs(seed: int = 0) -> dict:
    key = jax.random.key(seed)
    ks = iter(jax.random.split(key, 48))

    def normal(shape, scale):
        return jax.random.normal(next(ks), shape, jnp.float32) * scale

    def gain(shape):
        return 1.0 + normal(shape, 0.02)

    D = D_MODEL
    NE, NO, L = N_EVEN, N_ODD, DEPTH_2
    return {
        'x': normal((BATCH, SEQ, D), 1.0),
        'mem': normal((BATCH, MEM_LEN, D), 1.0),
        'ab_w_in': normal((NE, D, AB_IN_DIM), D ** -0.5),
        'ab_mu': jax.random.uniform(next(ks), (NE, AB_SHIFT_DIM), jnp.float32),
        'rw_w0': jax.random.uniform(next(ks), (NE, RW_DIM), jnp.float32, -6.5, -1.5),
        'rw_w2': normal((NE, RW_LORA_W, RW_DIM), 0.5 * RW_LORA_W ** -0.5),
        'rw_a0': normal((NE, RW_DIM), 0.3),
        'rw_a2': normal((NE, RW_LORA_A, RW_DIM), RW_LORA_A ** -0.5),
        'rw_g2': normal((NE, RW_LORA_G, RW_DIM), RW_LORA_G ** -0.5),
        'rw_k_k': 0.85 + normal((NE, RW_DIM), 0.05),
        'rw_k_a': 1.0 + normal((NE, RW_DIM), 0.05),
        'rw_r_k': normal((NE, RW_HEADS, RW_HEAD), 0.1),
        'rw_gn_g': gain((NE, RW_DIM)),
        'rw_gn_b': normal((NE, RW_DIM), 0.02),
        'sg_ln_g': gain((NE, SG_GROUPS, SG_GROUP_DIM)),
        'sg_ln_b': normal((NE, SG_GROUPS, SG_GROUP_DIM), 0.02),
        'sg_ws': normal((NE, SG_GROUPS, SG_CHUNK, SG_CHUNK), 0.5 * SG_CHUNK ** -0.5),
        'sg_b': 1.0 + normal((NE, SG_GROUPS, SG_CHUNK), 0.1),
        'ab_w_out': normal((NE, AB_MIX_DIM, D), DN_BETA * AB_MIX_DIM ** -0.5),
        'mla_w_in': normal((NO, D, MLA_IN_DIM), D ** -0.5),
        'mla_q_norm': gain((NO, MLA_Q_RANK)),
        'mla_kv_norm': gain((NO, MLA_KV_RANK)),
        'mla_wq_b': normal((NO, MLA_Q_RANK, MLA_HEADS * MLA_QK), MLA_Q_RANK ** -0.5),
        'mla_wkv_b': normal((NO, MLA_KV_RANK, MLA_HEADS * (MLA_NOPE + MLA_V)), MLA_KV_RANK ** -0.5),
        'mla_w_out': normal((NO, MLA_MIX_DIM, D), DN_BETA * MLA_MIX_DIM ** -0.5),
        'ln1_g': gain((L, D)),
        'ln1_b': normal((L, D), 0.02),
        'xa_wq': normal((L, D, D), D ** -0.5),
        'xa_wkv': normal((L, D, 2 * D), D ** -0.5),
        'xa_wo': normal((L, D, D), DN_BETA * D ** -0.5),
        'ln2_g': gain((L, D)),
        'ln2_b': normal((L, D), 0.02),
        'moe_w_group': normal((L, D, MOE_GROUPS), D ** -0.5),
        'moe_b_group': normal((L, MOE_GROUPS), 0.01),
        'moe_w_expert': normal((L, D, MOE_EXPERTS), D ** -0.5),
        'moe_b_expert': normal((L, MOE_EXPERTS), 0.01),
        'moe_w_gate': normal((L, MOE_EXPERTS, D, MOE_FF), D ** -0.5),
        'moe_w_up': normal((L, MOE_EXPERTS, D, MOE_FF), D ** -0.5),
        'moe_w_down': normal((L, MOE_EXPERTS, MOE_FF, D), DN_BETA * MOE_FF ** -0.5),
        'ln3_g': gain((L, D)),
        'ln3_b': normal((L, D), 0.02),
    }

def second_block(x, mem, ab_w_in, ab_mu, rw_w0, rw_w2, rw_a0, rw_a2, rw_g2, rw_k_k,
              rw_k_a, rw_r_k, rw_gn_g, rw_gn_b, sg_ln_g, sg_ln_b, sg_ws, sg_b,
              ab_w_out, mla_w_in, mla_q_norm, mla_kv_norm, mla_wq_b, mla_wkv_b,
              mla_w_out, ln1_g, ln1_b, xa_wq, xa_wkv, xa_wo, ln2_g, ln2_b,
              moe_w_group, moe_b_group, moe_w_expert, moe_b_expert, moe_w_gate,
              moe_w_up, moe_w_down, ln3_g, ln3_b):
    h = x
    for layer in range(DEPTH_2):
        j = layer // 2
        if layer % 2 == 0:
            mix = mixer_ab(h, ab_w_in[j], ab_mu[j], rw_w0[j], rw_w2[j], rw_a0[j],
                           rw_a2[j], rw_g2[j], rw_k_k[j], rw_k_a[j], rw_r_k[j],
                           rw_gn_g[j], rw_gn_b[j], sg_ln_g[j], sg_ln_b[j], sg_ws[j],
                           sg_b[j], ab_w_out[j])
        else:
            mix = mla(h, mla_w_in[j], mla_q_norm[j], mla_kv_norm[j], mla_wq_b[j],
                      mla_wkv_b[j], mla_w_out[j])
        h = layer_norm(DN_ALPHA * h + mix, ln1_g[layer], ln1_b[layer])
        xa = mem_cross_attention(h, mem, xa_wq[layer], xa_wkv[layer], xa_wo[layer])
        h = layer_norm(DN_ALPHA * h + xa, ln2_g[layer], ln2_b[layer])
        ff = hier_moe(h, moe_w_group[layer], moe_b_group[layer], moe_w_expert[layer],
                      moe_b_expert[layer], moe_w_gate[layer], moe_w_up[layer],
                      moe_w_down[layer])
        h = layer_norm(DN_ALPHA * h + ff, ln3_g[layer], ln3_b[layer])
    return h


def setup_inputs(seed=0):
    out = dict(first_inputs(seed))
    for name, value in second_inputs(seed + 1).items():
        if name != "x":
            out[name + "_2"] = value
    return out


def reference(
    x, mem, g_mix, w_in, qg_dil, kg_dil, qg_moba, kg_moba, qg_mem, kg_mem, g_memtok, w_mem_kv,
    og_dil, og_moba, og_mem, w_out, g_ffn, w_peer_q, peer_subkeys_1, peer_subkeys_2, peer_u,
    peer_v, mem_2, ab_w_in_2, ab_mu_2, rw_w0_2, rw_w2_2, rw_a0_2, rw_a2_2, rw_g2_2, rw_k_k_2,
    rw_k_a_2, rw_r_k_2, rw_gn_g_2, rw_gn_b_2, sg_ln_g_2, sg_ln_b_2, sg_ws_2, sg_b_2, ab_w_out_2,
    mla_w_in_2, mla_q_norm_2, mla_kv_norm_2, mla_wq_b_2, mla_wkv_b_2, mla_w_out_2, ln1_g_2,
    ln1_b_2, xa_wq_2, xa_wkv_2, xa_wo_2, ln2_g_2, ln2_b_2, moe_w_group_2, moe_b_group_2,
    moe_w_expert_2, moe_b_expert_2, moe_w_gate_2, moe_w_up_2, moe_w_down_2, ln3_g_2, ln3_b_2,
):
    x = first_block(
        x, mem, g_mix, w_in, qg_dil, kg_dil, qg_moba, kg_moba, qg_mem, kg_mem, g_memtok,
        w_mem_kv, og_dil, og_moba, og_mem, w_out, g_ffn, w_peer_q, peer_subkeys_1,
        peer_subkeys_2, peer_u, peer_v,
    )
    return second_block(
        x, mem_2, ab_w_in_2, ab_mu_2, rw_w0_2, rw_w2_2, rw_a0_2, rw_a2_2, rw_g2_2, rw_k_k_2,
        rw_k_a_2, rw_r_k_2, rw_gn_g_2, rw_gn_b_2, sg_ln_g_2, sg_ln_b_2, sg_ws_2, sg_b_2,
        ab_w_out_2, mla_w_in_2, mla_q_norm_2, mla_kv_norm_2, mla_wq_b_2, mla_wkv_b_2,
        mla_w_out_2, ln1_g_2, ln1_b_2, xa_wq_2, xa_wkv_2, xa_wo_2, ln2_g_2, ln2_b_2,
        moe_w_group_2, moe_b_group_2, moe_w_expert_2, moe_b_expert_2, moe_w_gate_2, moe_w_up_2,
        moe_w_down_2, ln3_g_2, ln3_b_2,
    )


_drawn_inputs = setup_inputs


def setup_inputs(seed=0):
    import zlib

    import numpy as np

    out = dict(_drawn_inputs(seed))
    spreads = {}
    factors = {'qg_dil': 3.283,
     'kg_dil': 3.652,
     'qg_moba': 3.013,
     'kg_moba': 2.864,
     'qg_mem': 2.923,
     'kg_mem': 2.816,
     'og_dil': 2.992,
     'og_moba': 2.738,
     'og_mem': 3.03,
     'rw_w2_2': 5.317,
     'rw_a0_2': 3.235,
     'rw_k_k_2': 4.996,
     'rw_k_a_2': 4.716,
     'rw_gn_g_2': 8.0,
     'rw_gn_b_2': 8.0,
     'sg_ln_g_2': 8.0,
     'sg_ln_b_2': 8.0,
     'mla_q_norm_2': 8.0,
     'mla_kv_norm_2': 8.0,
     'moe_b_group_2': 4.831,
     'moe_b_expert_2': 8.0}
    for name, (base, spread) in spreads.items():
        noise = np.random.default_rng([zlib.crc32(name.encode()), seed]).standard_normal(out[name].shape)
        drawn = base * np.exp(spread * noise) if base else spread * noise
        out[name] = jnp.asarray(drawn.astype(out[name].dtype))
    for name, factor in factors.items():
        out[name] = (out[name] * factor).astype(out[name].dtype)
    return out
```

```python
from contextlib import ExitStack, contextmanager
import math

import numpy as np
import concourse.bass as bass
from concourse import mybir

ALU = mybir.AluOpType
ACT = mybir.ActivationFunctionType
F32 = mybir.dt.float32
U32 = mybir.dt.uint32
AX = mybir.AxisListType.X

P = 128
S = 256
NT = S // P
D = 1024
DC = D // P
MASKED = -1e32

HD = 64
H_DIL, H_MOBA, H_MEM = 6, 6, 4
H_MIX = H_DIL + H_MOBA + H_MEM
IN_W = 3 * HD * (H_DIL + H_MOBA) + HD * H_MEM
N_ALIBI = H_DIL + H_MOBA
SLOPES = [2.0 ** (-8.0 * (i + 1) / N_ALIBI) for i in range(N_ALIBI)]

PH, PK, TOPK = 8, 128, 16
RW_H, RW_N, CH = 8, 64, 64
NCH = S // CH
SG = 4
MLA_H, MLA_NOPE, MLA_ROPE, MLA_V = 16, 64, 32, 64
MLA_QK = MLA_NOPE + MLA_ROPE
XA_H, XA_D = 4, 256
NG, NPG = 4, 8
NE = NG * NPG
FF = 512
ALPHA = 4.0 ** 0.25
SLOT = 4096
SLOTS = 4

def shape_constants():
    t = np.arange(S)
    dist = (t[:, None] - t[None, :]).astype(np.float32)
    causal = dist >= 0
    idist = dist.astype(np.int64)
    count = ((causal & (idist <= 128)).astype(np.float32) + (causal & (idist % 4 == 0))
             + (causal & (idist % 16 == 0))).astype(np.float32)
    rows = lambda m: m.reshape(NT, P, S).transpose(1, 0, 2).reshape(P, NT * S)
    c = {}
    c["ident"] = np.eye(P, dtype=np.float32)
    c["iota"] = np.tile(np.arange(P, dtype=np.float32), (P, 1))
    c["ones"] = np.ones((P, 64), np.float32)
    c["dist_moba"] = rows(np.where(causal, -dist, MASKED))
    c["dist_dil"] = rows(np.where(count > 0, -dist, MASKED))
    c["count"] = rows(count)
    c["causal"] = rows(np.where(causal, 0.0, MASKED))
    half = MLA_ROPE // 2
    inv = 10000.0 ** (-np.arange(half, dtype=np.float32) / half)
    ang = (t[:, None].astype(np.float32) * inv[None, :]).astype(np.float32)
    pack = lambda m: m.reshape(NT, P, half).transpose(1, 0, 2).reshape(P, NT * half)
    c["cos"], c["sin"] = pack(np.cos(ang)), pack(np.sin(ang))
    s64, t64 = np.arange(CH)[:, None], np.arange(CH)[None, :]
    pad = lambda m: np.concatenate([m.reshape(CH, -1), np.zeros((P - CH, m.size // CH))], 0)
    c["tri"] = pad(np.concatenate([s64 < t64, s64 <= t64], 1))
    lev = [((s64 // (2 * b) == t64 // (2 * b)) & (s64 % (2 * b) < b) & (t64 % (2 * b) >= b))
           for b in (1, 2, 4, 8, 16, 32)]
    c["levels"] = pad(np.stack(lev, 1))
    c["reset"] = np.tile((np.arange(RW_H * S) % CH != 0).astype(np.float32), (P, 1))
    at, parts, n = {}, [], 0
    for k, v in c.items():
        v = np.ascontiguousarray(v, dtype=np.float32)
        at[k] = (n, v.shape[1])
        n += v.shape[1]
        parts.append(v)
    return at, np.concatenate(parts, 1)

def vector_columns():
    return [("g_mix", "g_mix", P, DC), ("g_memtok", "g_memtok", P, DC), ("g_ffn", "g_ffn", P, DC),
            ("qg_dil", "qg_dil", HD, 1), ("kg_dil", "kg_dil", HD, 1), ("qg_moba", "qg_moba", HD, 1),
            ("kg_moba", "kg_moba", HD, 1), ("qg_mem", "qg_mem", HD, 1), ("kg_mem", "kg_mem", HD, 1),
            ("og_dil", "og_dil", P, 3), ("og_moba", "og_moba", P, 3), ("og_mem", "og_mem", P, 2),
            ("mu_rkv", "ab_mu_2", 64, 28), ("w0", "rw_w0_2", 64, 8), ("a0", "rw_a0_2", 64, 8),
            ("k_k", "rw_k_k_2", 64, 8), ("k_a", "rw_k_a_2", 64, 8), ("r_k", "rw_r_k_2", 64, 8),
            ("mu_g", "ab_mu_2", P, 14), ("sg_b", "sg_b_2", P, SG),
            ("q_norm", "mla_q_norm_2", P, 2), ("kv_norm", "mla_kv_norm_2", P, 2)]

def column_places():
    at, n = {}, 0
    for name, _, _, cols in vector_columns():
        at[name] = (n, cols)
        n += cols
    return at, n

class Signal:

    def __init__(self, nc, name):
        self.sem = nc.alloc_semaphore(name=name)
        self.count = self.start = 0

    def up(self, n=1):
        self.count += n
        return self.sem

    def at(self, n):
        return self.start + n

    def repeated(self, times, each):
        self.count += (times - 1) * each

class WeightStream:

    def __init__(self, k):
        self.k = k
        self.sources = []
        self.issued = 0
        self.landed = [Signal(k.nc, f"weights_landed_{i}") for i in range(SLOTS)]

    def add(self, aps):
        first = len(self.sources)
        self.sources += aps
        return first

    def view(self, n, kc, cols):
        return self.k.ring[:, n % SLOTS, 0:kc * cols].rearrange("p (k n) -> p k n", k=kc)

    def load(self, sp, n):
        src = self.sources[n]
        kc, cols = src.shape[1], src.shape[2]
        sp.dma_start(self.view(n, kc, cols), src).then_inc(self.landed[n % SLOTS].up(16), 16)

    def wait_landed(self, pe, n):
        pe.wait_ge(self.landed[n % SLOTS].sem, 16 * (n // SLOTS + 1))

    def prefetch(self, sp, end, first, freed):
        while self.issued < min(end + SLOTS, len(self.sources)):
            old = self.issued - SLOTS
            if old >= first:
                sp.wait_ge(self.k.products.sem, self.k.products.at(freed[old]))
            self.load(sp, self.issued)
            self.issued += 1

class Kernel:
    def __init__(self, nc, dram, ctx):
        self.nc, self.dram, self.ctx, self.allocated = nc, dram, ctx, 0
        self.signals = []

        def signal(name):
            self.signals.append(Signal(nc, name))
            return self.signals[-1]
        self.products = signal("products")
        self.dve_evacuated = signal("dve_evacuated")
        self.act_evacuated = signal("act_evacuated")
        self.dve_step = signal("dve_step")
        self.act_step = signal("act_step")
        self.small_loaded = signal("small_loaded")
        self.scores_ready = signal("scores_ready")
        self.scores_read = signal("scores_read")
        self.shift_ready = signal("shift_ready")
        self.exps_ready = signal("exps_ready")
        self.probs_ready = signal("probs_ready")
        self.probs_turned = signal("probs_turned")
        self.turned_copied = signal("turned_copied")
        self.heads_ready = signal("heads_ready")
        self.heads_scaled = signal("heads_scaled")
        self.rows_stored = signal("rows_stored")
        self.onehots_ready = signal("onehots_ready")
        self.gates_placed = signal("gates_placed")
        self.act_ready = signal("act_ready")
        self.weights_gated = signal("weights_gated")
        self.hidden_ready = signal("hidden_ready")
        self.gate_products = signal("gate_products")
        self.up_products = signal("up_products")
        self.silu_ready = signal("silu_ready")
        self.gated_ready = signal("gated_ready")
        self.down_products = signal("down_products")
        self.ring = self.sb("weight_ring", [P, SLOTS, SLOT])
        self.ps = ctx.enter_context(nc.psum_tensor("banks", [P, 8, 512], F32))
        self.stream = WeightStream(self)
        self.const_at, _ = shape_constants()
        self.col_at, ncols = column_places()
        self.cols_sb = self.sb("columns", [P, ncols])
        self.ident = self.sb("identity", [P, P])[:, :]

    def sb(self, name, shape, dt=F32, ctx=None):
        self.allocated += 1
        return (ctx or self.ctx).enter_context(self.nc.sbuf_tensor(f"{name}_{self.allocated}", shape, dt))

    @contextmanager
    def stage(self):
        with self.nc.Block() as block:
            yield block
        for s in self.signals:
            s.start = s.count

    def const(self, name, rows=P):
        a, n = self.const_at[name]
        return self.dram["consts"][0:rows, a:a + n]

    def col(self, name, i, rows=P):
        a, _ = self.col_at[name]
        return self.cols_sb[0:rows, a + i:a + i + 1]

    def cols(self, name, rows=P):
        a, n = self.col_at[name]
        return self.cols_sb[0:rows, a:a + n]

    def v(self, ins):
        ins.then_inc(self.dve_step.up(), 1)
        self.nc.vector.wait_ge(self.dve_step.sem, self.dve_step.count)

    def a(self, ins):
        ins.then_inc(self.act_step.up(), 1)
        self.nc.scalar.wait_ge(self.act_step.sem, self.act_step.count)

def load_small(k, pairs):
    with k.stage() as block:
        @block.sync
        def _(sp):
            if not k.stream.issued:
                k.stream.prefetch(sp, 0, 0, {})

        @block.scalar
        def _(act):
            for dst, src in pairs:
                act.dma_start(dst, src).then_inc(k.small_loaded.up(16), 16)
            act.wait_ge(k.small_loaded.sem, k.small_loaded.at(16 * len(pairs)))

def run_products(k, units, tiles=(0, 0)):
    nc = k.nc
    served = {"v": 0, "a": 0}
    order = []
    for tile, _, who, copies in units:
        served[who] += len(copies)
        order.append(served[who])
    freed = {}
    for u, (tile, *_) in enumerate(units):
        if tile is not None:
            freed[tile] = u + 1
    emptied = {"v": k.dve_evacuated, "a": k.act_evacuated}

    with k.stage() as block:
        @block.sync
        def _(sp):
            k.stream.prefetch(sp, tiles[1] if tiles[1] else k.stream.issued - SLOTS, tiles[0], freed)

        @block.tensor
        def _(pe):
            seen = set()
            for u, (tile, products, _, _) in enumerate(units):
                if tile is not None and tile not in seen:
                    k.stream.wait_landed(pe, tile)
                    seen.add(tile)
                if u >= 8:
                    pe.wait_ge(emptied[units[u - 8][2]].sem, emptied[units[u - 8][2]].at(order[u - 8]))
                for product in products:
                    last = product(k.ps[:, u % 8, :])
                last.then_inc(k.products.up(), 1)

        @block.vector
        def _(dve):
            for u, (_, _, who, copies) in enumerate(units):
                if who == "v":
                    dve.wait_ge(k.products.sem, k.products.at(u + 1))
                    for copy in copies:
                        copy(nc.vector, k.ps[:, u % 8, :]).then_inc(k.dve_evacuated.up(), 1)

        @block.scalar
        def _(act):
            for u, (_, _, who, copies) in enumerate(units):
                if who == "a":
                    act.wait_ge(k.products.sem, k.products.at(u + 1))
                    for copy in copies:
                        copy(nc.scalar, k.ps[:, u % 8, :]).then_inc(k.act_evacuated.up(), 1)

def mm(k, out, lhsT, rhs, start=True, stop=True):
    return k.nc.tensor.matmul(out, lhsT, rhs, start=start, stop=stop)

def copy_out(k, out, rows, cols, scale=None, cols0=0, rows0=0):
    def go(eng, ps):
        src = ps[rows0:rows0 + rows, cols0:cols0 + cols]
        if len(out.shape) == 3:
            src = src.rearrange("p (a b) -> p a b", a=out.shape[1])
        if eng is k.nc.scalar:
            return eng.activation(out, src, ACT.Copy, scale=1.0 if scale is None else scale)
        if scale is None:
            return eng.tensor_copy(out, src)
        return eng.tensor_scalar(out, src, scale, None, ALU.mult)
    return go

def token_products(k, xT, kc, tile, cols, c0, width, out, who=None, copy=None):
    units = []
    w = k.stream.view(tile, kc, cols)
    for tt in range(NT):
        def prod(ps, kk, tt=tt):
            return mm(k, ps[:, 0:width], xT[:, kk, tt * P:(tt + 1) * P], w[:, kk, c0:c0 + width],
                      kk == 0, kk == kc - 1)
        cp = copy(tt) if copy else copy_out(k, out(tt), P, width)
        units.append((tile, [lambda ps, kk=kk, prod=prod: prod(ps, kk) for kk in range(kc)],
                      who or "va"[tt % 2], [cp]))
    return units

def feature_products(k, xT, kc, tile, cols, c0, m, outs, who):
    w = k.stream.view(tile, kc, cols)
    prods = [lambda ps, kk=kk: mm(k, ps[0:m, 0:S], w[:, kk, c0:c0 + m], xT[:, kk, 0:S],
                                  kk == 0, kk == kc - 1) for kk in range(kc)]
    return (tile, prods, who, [copy_out(k, o, r, S, rows0=r0) for o, r0, r in outs])

def turn(k, src, n, outT, gain=None, pt=P, tiles=NT):
    units = []
    for c in range(n):
        trs = [lambda ps, c=c, tt=tt: k.nc.tensor.transpose(ps[:, tt * pt:(tt + 1) * pt],
                                                            src[0:pt, tt, c * P:(c + 1) * P],
                                                            k.ident[0:pt, 0:pt]) for tt in range(tiles)]
        units.append((None, trs, "va"[c % 2],
                      [copy_out(k, outT[:, c, :], P, tiles * pt, gain(c) if gain else None)]))
    run_products(k, units)

def row_rsqrt(k, jobs, eps):
    nc = k.nc
    with ExitStack() as c:
        sq = k.sb("squares", [P, 2048], ctx=c)
        with k.stage() as block:
            @block.vector
            def _(dve):
                for src, out in jobs:
                    p, g, w = src.shape
                    view = sq[0:p, 0:g * w].rearrange("p (g w) -> p g w", g=g)
                    k.v(nc.vector.tensor_tensor(view, src, src, ALU.mult))
                    k.v(nc.vector.tensor_reduce(out, view, AX, ALU.add))
                    k.v(nc.vector.tensor_scalar(out, out, 1.0 / w, eps, ALU.mult, ALU.add))
                for n, (_, out) in enumerate(jobs):
                    dve.wait_ge(k.act_step.sem, k.act_step.at(n + 1))
                    nc.vector.reciprocal(out, out).then_inc(k.dve_step.up(), 1)

            @block.scalar
            def _(act):
                for n, (_, out) in enumerate(jobs):
                    act.wait_ge(k.dve_step.sem, k.dve_step.at(3 * (n + 1)))
                    nc.scalar.activation(out, out, ACT.Sqrt).then_inc(k.act_step.up(), 1)

def scale_groups(k, jobs):
    with k.stage() as block:
        @block.vector
        def _(dve):
            for rows, f in jobs:
                p, g, w = rows.shape
                k.nc.vector.tensor_tensor(rows, rows, f.unsqueeze(2).to_broadcast([p, g, w]),
                                          ALU.mult).then_inc(k.dve_step.up(), 1)

def layer_norm(k, x, g_row, b_row, eps=1e-5):
    nc = k.nc
    with ExitStack() as c:
        gb = k.sb("ln_gain_bias", [P, 2, D], ctx=c)
        st = k.sb("ln_stats", [P, NT, 2, 6], ctx=c)
        mv = k.sb("ln_mean_var", [P, NT, 2], ctx=c)
        rs = k.sb("ln_rstd", [P, NT, 1], ctx=c)
        with k.stage() as block:
            @block.scalar
            def _(act):
                act.dma_start(gb[:, 0, :], g_row.partition_broadcast(P)).then_inc(k.small_loaded.up(16), 16)
                act.dma_start(gb[:, 1, :], b_row.partition_broadcast(P)).then_inc(k.small_loaded.up(16), 16)
                for tt in range(NT):
                    act.wait_ge(k.dve_step.sem, k.dve_step.at(4 * (tt + 1)))
                    nc.scalar.activation(rs[:, tt, :], rs[:, tt, :], ACT.Sqrt).then_inc(k.act_step.up(), 1)

            @block.vector
            def _(dve):
                for tt in range(NT):
                    k.v(nc.vector.bn_stats(st[:, tt, 0, :], x[:, tt, 0:512]))
                    k.v(nc.vector.bn_stats(st[:, tt, 1, :], x[:, tt, 512:1024]))
                    k.v(nc.vector.bn_aggr(mv[:, tt, :], st[:, tt, :, :].rearrange("p a b -> p (a b)")))
                    k.v(nc.vector.tensor_scalar(rs[:, tt, :], mv[:, tt, 1:2], eps, None, ALU.add))
                dve.wait_ge(k.small_loaded.sem, k.small_loaded.at(32))
                for tt in range(NT):
                    dve.wait_ge(k.act_step.sem, k.act_step.at(tt + 1))
                    k.v(nc.vector.reciprocal(rs[:, tt, :], rs[:, tt, :]))
                    k.v(nc.vector.tensor_scalar(x[:, tt, :], x[:, tt, :], mv[:, tt, 0:1], rs[:, tt, :],
                                                ALU.subtract, ALU.mult))
                    k.v(nc.vector.tensor_tensor(x[:, tt, :], x[:, tt, :], gb[:, 0, :], ALU.mult))
                    k.v(nc.vector.tensor_tensor(x[:, tt, :], x[:, tt, :], gb[:, 1, :], ALU.add))

def attention(k, heads, dv):
    nc, H = k.nc, len(heads)
    with ExitStack() as c:
        sc = k.sb("scores", [P, 2, NT, S], ctx=c)
        pT = k.sb("probs_T", [P, 2, 2, S], ctx=c)
        top = k.sb("row_max", [P, H, NT], ctx=c)
        den = k.sb("row_sum", [P, H, NT], ctx=c)
        with k.stage() as block:
            @block.tensor
            def _(pe):
                for i in range(H + 2):
                    if i < H:
                        q, kt, _, _, _ = heads[i]
                        if i >= 2:
                            pe.wait_ge(k.scores_read.sem, k.scores_read.at(i - 1))
                        for tt in range(NT):
                            for n in range(len(q)):
                                last = mm(k, k.ps[:, i % 2, tt * S:(tt + 1) * S], q[n][:, tt * P:(tt + 1) * P],
                                          kt[n], n == 0, n == len(q) - 1)
                        last.then_inc(k.scores_ready.up(), 1)
                    h = i - 1
                    if 0 <= h < H:
                        pe.wait_ge(k.probs_ready.sem, k.probs_ready.at(h + 1))
                        if h >= 2:
                            pe.wait_ge(k.turned_copied.sem, k.turned_copied.at(h - 1))
                        for kt2 in range(2):
                            for tt in range(NT):
                                last = nc.tensor.transpose(k.ps[:, 2 + h % 2, kt2 * S + tt * P:kt2 * S + (tt + 1) * P],
                                                           sc[:, h % 2, tt, kt2 * P:(kt2 + 1) * P], k.ident)
                        last.then_inc(k.probs_turned.up(), 1)
                    h = i - 2
                    if 0 <= h < H:
                        pe.wait_ge(k.turned_copied.sem, k.turned_copied.at(h + 1))
                        if h >= 2:
                            pe.wait_ge(k.heads_scaled.sem, k.heads_scaled.at(NT * (h - 1)))
                        for tt in range(NT):
                            for kt2 in range(2):
                                last = mm(k, k.ps[:, 4 + h % 2, tt * 256:tt * 256 + dv],
                                          pT[:, h % 2, kt2, tt * P:(tt + 1) * P], heads[h][2](kt2),
                                          kt2 == 0, kt2 == 1)
                        last.then_inc(k.heads_ready.up(), 1)

            @block.vector
            def _(dve):
                for i in range(H + 2):
                    if i < H:
                        kind, arg = heads[i][3]
                        flat = sc[:, i % 2, :, :].rearrange("p a b -> p (a b)")
                        dve.wait_ge(k.scores_ready.sem, k.scores_ready.at(i + 1))
                        if i >= 2:
                            dve.wait_ge(k.probs_turned.sem, k.probs_turned.at(i - 1))
                        if kind == "alibi":
                            slope, dist, _ = arg
                            ins = nc.vector.scalar_tensor_tensor(out=flat, in0=dist, scalar=slope,
                                                                 in1=k.ps[:, i % 2, :], op0=ALU.mult, op1=ALU.add)
                        elif kind == "masked":
                            ins = nc.vector.tensor_tensor(flat, arg, k.ps[:, i % 2, :], ALU.add)
                        else:
                            ins = nc.vector.tensor_copy(flat, k.ps[:, i % 2, :])
                        ins.then_inc(k.scores_read.up(), 1)
                        dve.wait_ge(k.scores_read.sem, k.scores_read.at(i + 1))
                        k.v(nc.vector.tensor_reduce(top[:, i, :], sc[:, i % 2, :, :], AX, ALU.max))
                        nc.vector.tensor_scalar(top[:, i, :], top[:, i, :], -1.0, None,
                                                ALU.mult).then_inc(k.shift_ready.up(), 1)
                    h = i - 1
                    if 0 <= h < H:
                        kind, arg = heads[h][3]
                        dve.wait_ge(k.exps_ready.sem, k.exps_ready.at(NT * (h + 1)))
                        if kind == "alibi" and arg[2] is not None:
                            flat = sc[:, h % 2, :, :].rearrange("p a b -> p (a b)")
                            k.v(nc.vector.tensor_tensor(flat, flat, arg[2], ALU.mult))
                            k.v(nc.vector.tensor_reduce(den[:, h, :], sc[:, h % 2, :, :], AX, ALU.add))
                        nc.vector.reciprocal(den[:, h, :], den[:, h, :]).then_inc(k.probs_ready.up(), 1)
                    h = i - 2
                    if 0 <= h < H:
                        dve.wait_ge(k.probs_ready.sem, k.probs_ready.at(h + 1))
                        dve.wait_ge(k.heads_ready.sem, k.heads_ready.at(h + 1))
                        for tt in range(NT):
                            nc.vector.tensor_scalar(heads[h][4](tt), k.ps[:, 4 + h % 2, tt * 256:tt * 256 + dv],
                                                    den[:, h, tt:tt + 1], None,
                                                    ALU.mult).then_inc(k.heads_scaled.up(), 1)

            @block.scalar
            def _(act):
                for i in range(H + 1):
                    if i < H:
                        act.wait_ge(k.shift_ready.sem, k.shift_ready.at(i + 1))
                        for tt in range(NT):
                            nc.scalar.activation(sc[:, i % 2, tt, :], sc[:, i % 2, tt, :], ACT.Exp,
                                                 bias=top[:, i, tt:tt + 1],
                                                 accum_out=den[:, i, tt:tt + 1]).then_inc(k.exps_ready.up(), 1)
                    h = i - 1
                    if h >= 0:
                        act.wait_ge(k.probs_turned.sem, k.probs_turned.at(h + 1))
                        if h >= 2:
                            act.wait_ge(k.heads_ready.sem, k.heads_ready.at(h - 1))
                        nc.scalar.activation(pT[:, h % 2, :, :].rearrange("p a b -> p (a b)"),
                                             k.ps[:, 2 + h % 2, :], ACT.Copy).then_inc(k.turned_copied.up(), 1)

def residual(k, x, alpha, c0, width):
    def at(tt):
        def go(eng, ps):
            return k.nc.vector.scalar_tensor_tensor(out=x[:, tt, c0:c0 + width], in0=x[:, tt, c0:c0 + width],
                                                    scalar=alpha, in1=ps[:, 0:width], op0=ALU.mult, op1=ALU.add)
        return go
    return at

def project_residual(k, xT, kc, first, x, alpha):
    units = []
    for j in range(2):
        units += token_products(k, xT, kc, first + j, 512, 0, 512, None, "v", residual(k, x, alpha, 512 * j, 512))
    run_products(k, units, (first, first + 2))

def first_block_attention(k, x, tiles):
    nc, sb = k.nc, k.sb
    with ExitStack() as c:
        proj = sb("projections", [P, NT, IN_W], ctx=c)
        kv = sb("memory_kv", [P, NT, 2 * HD * H_MEM], ctx=c)
        with ExitStack() as c2:
            mem = sb("memory_rows", [P, NT, D], ctx=c2)
            xT = sb("x_T", [P, DC, S], ctx=c2)
            memT = sb("memory_T", [P, DC, S], ctx=c2)
            f = sb("row_factors", [P, 2 * NT], ctx=c2)
            y = sb("normed_rows", [P, NT, D], ctx=c2)
            load_small(k, [(x[:, :, :], k.dram["x"].rearrange("a (t p) d -> p (a t) d", p=P)),
                           (mem[:, :, :], k.dram["mem"].rearrange("a (t p) d -> p (a t) d", p=P)),
                           (k.cols_sb[:, :], k.dram["columns"]), (k.ident, k.const("ident"))])
            row_rsqrt(k, [(x[:, :, :], f[:, 0:NT]), (mem[:, :, :], f[:, NT:2 * NT])], 1e-6)
            for src, dst, at, gain in ((x, xT, 0, "g_mix"), (mem, memT, NT, "g_memtok")):
                with k.stage() as block:
                    @block.vector
                    def _(dve):
                        for tt in range(NT):
                            nc.vector.tensor_scalar(y[:, tt, :], src[:, tt, :], f[:, at + tt:at + tt + 1], None,
                                                    ALU.mult).then_inc(k.dve_step.up(), 1)
                turn(k, y, DC, dst, lambda ch, gain=gain: k.col(gain, ch))
            units = []
            for j in range(IN_W // 512):
                units += token_products(k, xT, DC, tiles["w_in"] + j, 512, 0, 512,
                                        lambda tt, j=j: proj[:, tt, 512 * j:512 * (j + 1)])
            units += token_products(k, memT, DC, tiles["w_mem_kv"], 512, 0, 512, lambda tt: kv[:, tt, :])
            run_products(k, units, (tiles["w_in"], tiles["w_mem_kv"] + 1))

        q_T = sb("queries_T", [HD, H_MIX, S], ctx=c)
        k_T = sb("keys_T", [HD, H_MIX, S], ctx=c)
        out = sb("mixed_heads", [P, NT, D], ctx=c)
        masks = sb("attention_constants", [P, 3, NT * S], ctx=c)
        gf = sb("group_factors", [P, NT, 40], ctx=c)
        load_small(k, [(masks[:, n, :], k.const(name)) for n, name in enumerate(("dist_dil", "dist_moba", "count"))])
        wd = HD * H_DIL
        jobs = []
        for tt in range(NT):
            for n, (src, c0, g) in enumerate(((proj, 0, 12), (proj, 3 * wd, 12), (proj, 6 * wd, 4), (kv, 0, 4))):
                g0 = (0, 12, 24, 28)[n]
                jobs.append((src[:, tt, c0:c0 + g * HD].rearrange("p (g w) -> p g w", g=g), gf[:, tt, g0:g0 + g]))
        row_rsqrt(k, jobs, 1e-6)
        scale_groups(k, jobs)
        units = []
        at = 0
        for dst, h0, n, src, c0, gain in ((q_T, 0, 6, proj, 0, "qg_dil"), (k_T, 0, 6, proj, wd, "kg_dil"),
                                          (q_T, 6, 6, proj, 3 * wd, "qg_moba"), (k_T, 6, 6, proj, 4 * wd, "kg_moba"),
                                          (q_T, 12, 4, proj, 6 * wd, "qg_mem"), (k_T, 12, 4, kv, 0, "kg_mem")):
            for h in range(0, n, 2):
                trs = [lambda ps, a=a, tt=tt, src=src, c0=c0, h=h:
                       nc.tensor.transpose(ps[0:HD, a * S + tt * P:a * S + (tt + 1) * P],
                                           src[:, tt, c0 + (h + a) * HD:c0 + (h + a + 1) * HD], k.ident)
                       for a in range(2) for tt in range(NT)]

                def gained(eng, ps, dst=dst, h=h0 + h, gain=gain):
                    o = dst[:, h:h + 2, :].rearrange("p a b -> p (a b)")
                    if eng is nc.scalar:
                        return eng.activation(o, ps[0:HD, :], ACT.Copy, scale=k.col(gain, 0, HD))
                    return eng.tensor_scalar(o, ps[0:HD, :], k.col(gain, 0, HD),
                                             HD ** -0.5 if dst is q_T else 1.0, ALU.mult, ALU.mult)
                units.append((None, trs, "v" if dst is q_T else "a", [gained]))
        run_products(k, units)

        heads = []
        for h in range(H_MIX):
            if h < H_DIL:
                v = lambda kt, h=h: proj[:, kt, 2 * wd + h * HD:2 * wd + (h + 1) * HD]
                kind = ("alibi", (SLOPES[2 * h], masks[:, 0, :], masks[:, 2, :]))
            elif h < H_DIL + H_MOBA:
                g = h - H_DIL
                v = lambda kt, g=g: proj[:, kt, 5 * wd + g * HD:5 * wd + (g + 1) * HD]
                kind = ("alibi", (SLOPES[2 * g + 1], masks[:, 1, :], None))
            else:
                g = h - H_DIL - H_MOBA
                v = lambda kt, g=g: kv[:, kt, (H_MEM + g) * HD:(H_MEM + g + 1) * HD]
                kind = ("plain", None)
            heads.append(([q_T[:, h, :]], [k_T[:, h, :]], v, kind,
                          lambda tt, h=h: out[:, tt, h * HD:(h + 1) * HD]))
        attention(k, heads, HD)

        jobs = [(out[:, tt, c0:c0 + n].unsqueeze(1), gf[:, tt, i:i + 1])
                for tt in range(NT) for i, (c0, n) in enumerate(((0, wd), (wd, wd), (2 * wd, D - 2 * wd)))]
        row_rsqrt(k, jobs, 1e-6)
        scale_groups(k, jobs)
        outT = sb("mixed_T", [P, DC, S], ctx=c)
        turn(k, out, DC, outT, lambda ch: k.col("og_dil", ch))
        project_residual(k, outT, DC, tiles["w_out"], x, 1.0)

def top16(k, lists):
    v = k.nc.vector
    steps = [lambda a, b, t, i: v.max(t[:, 0:8], a),
             lambda a, b, t, i: v.max_index(i[:, 0:8], t[:, 0:8], a),
             lambda a, b, t, i: v.match_replace(b, t[:, 0:8], a, -3e38),
             lambda a, b, t, i: v.max(t[:, 8:16], b),
             lambda a, b, t, i: v.max_index(i[:, 8:16], t[:, 8:16], b)]
    for step in steps:
        for item in lists:
            step(*item).then_inc(k.dve_step.up(), 1)
        v.wait_ge(k.dve_step.sem, k.dve_step.count)

def peer_routing(k, hT, tiles, slots_T):
    nc, sb = k.nc, k.sb
    with ExitStack() as c:
        qT = sb("peer_queries_T", [P, 2 * PH, S], ctx=c)
        units = []
        for j in range(4):
            for m in range(4):
                units.append(feature_products(k, hT, DC, tiles["w_peer_q"] + j, 512, m * P, P,
                                              [(qT[:, 4 * j + m, :], 0, P)], "va"[m % 2]))
        run_products(k, units, (tiles["w_peer_q"], tiles["w_peer_q"] + 4))
        sub = sb("sub_keys_T", [P, 2, PH, PK], ctx=c)
        load_small(k, [(sub[:, n, :, :], k.dram[f"subkeys_T_{n + 1}"]) for n in range(2)])
        sc = sb("sub_scores", [P, 2, NT, PH, PK], ctx=c)
        units = []
        for side in range(2):
            for tt in range(NT):
                for hh in range(0, PH, 4):
                    prods = [lambda ps, h=h, side=side, tt=tt, hh=hh:
                             mm(k, ps[:, (h - hh) * PK:(h - hh + 1) * PK], qT[:, 2 * h + side, tt * P:(tt + 1) * P],
                                sub[:, side, h, :]) for h in range(hh, hh + 4)]
                    units.append((None, prods, "va"[tt], [copy_out(
                        k, sc[:, side, tt, hh:hh + 4, :].rearrange("p a b -> p (a b)"), P, 512)]))
        run_products(k, units)

        best = sb("best_keys", [P, NT, 2, PH, TOPK], ctx=c)
        place = sb("best_places", [P, NT, 2, PH, TOPK], U32, ctx=c)
        placef = sb("best_places_float", [P, NT, 2, PH, TOPK], ctx=c)
        pair = sb("pair_sums", [P, PH, TOPK * TOPK], ctx=c)
        spare = sb("spare", [P, 2 * PH * TOPK * TOPK], ctx=c)
        ps_top = sb("pair_best", [P, NT, PH, TOPK], ctx=c)
        ps_at = sb("pair_places", [P, NT, PH, TOPK], U32, ctx=c)
        digit = sb("pair_digits", [P, 2, PH * TOPK], U32, ctx=c)
        digitf = sb("pair_digits_float", [P, 2, PH * TOPK], ctx=c)
        rows = sb("slot_rows", [P, NT, 3, PH * TOPK], ctx=c)
        iota = sb("iota_16", [P, TOPK], ctx=c)
        tot = sb("gate_sums", [P, NT * PH], ctx=c)
        load_small(k, [(iota[:, :], k.const("iota")[:, 0:TOPK])])
        G = [P, PH * TOPK, TOPK]
        with k.stage() as block:
            @block.vector
            def _(dve):
                v = nc.vector
                for tt in range(NT):
                    sp = spare[:, :].rearrange("p (s h n) -> p s h n", s=2, h=PH)
                    top16(k, [(sc[:, s, tt, h, :], sp[:, s, h, 0:PK], best[:, tt, s, h, :], place[:, tt, s, h, :])
                              for s in range(2) for h in range(PH)])
                    k.v(v.tensor_copy(placef[:, tt], place[:, tt]))
                    for h in range(PH):
                        v.tensor_tensor(pair[:, h, :].rearrange("p (a b) -> p a b", a=TOPK),
                                        best[:, tt, 0, h, :].unsqueeze(2).to_broadcast([P, TOPK, TOPK]),
                                        best[:, tt, 1, h, :].unsqueeze(1).to_broadcast([P, TOPK, TOPK]),
                                        ALU.add).then_inc(k.dve_step.up(), 1)
                    v.wait_ge(k.dve_step.sem, k.dve_step.count)
                    top16(k, [(pair[:, h, :], sp[:, 0, h, :], ps_top[:, tt, h, :], ps_at[:, tt, h, :])
                              for h in range(PH)])
                    at = ps_at[:, tt, :, :].rearrange("p h j -> p (h j)")
                    k.v(v.tensor_scalar(digit[:, 0, :], at, 4, None, ALU.logical_shift_right))
                    k.v(v.tensor_scalar(digit[:, 1, :], at, TOPK - 1, None, ALU.bitwise_and))
                    k.v(v.tensor_copy(digitf[:, :, :], digit[:, :, :]))
                    for s in range(2):
                        hot = spare[:, 0:PH * TOPK * TOPK].rearrange("p (j a) -> p j a", a=TOPK)
                        k.v(v.tensor_tensor(hot, digitf[:, s, :].unsqueeze(2).to_broadcast(G),
                                            iota[:, :].unsqueeze(1).to_broadcast(G), ALU.is_equal))
                        for h in range(PH):
                            hh = hot[:, h * TOPK:(h + 1) * TOPK, :]
                            v.tensor_tensor(hh, hh, placef[:, tt, s, h, :].unsqueeze(1).to_broadcast([P, TOPK, TOPK]),
                                            ALU.mult).then_inc(k.dve_step.up(), 1)
                        v.wait_ge(k.dve_step.sem, k.dve_step.count)
                        k.v(v.tensor_reduce(rows[:, tt, s, :], hot, AX, ALU.add))
                    v.tensor_tensor(rows[:, tt, 2, :].rearrange("p (h j) -> p h j", h=PH), ps_top[:, tt, :, :],
                                    ps_top[:, tt, :, 0:1].to_broadcast([P, PH, TOPK]),
                                    ALU.subtract).then_inc(k.shift_ready.up(), 1)
                for tt in range(NT):
                    dve.wait_ge(k.exps_ready.sem, k.exps_ready.at(tt + 1))
                    e = rows[:, tt, 2, :].rearrange("p (h j) -> p h j", h=PH)
                    t = tot[:, tt * PH:(tt + 1) * PH]
                    k.v(v.tensor_reduce(t, e, AX, ALU.add))
                    k.v(v.reciprocal(t, t))
                    k.v(v.tensor_tensor(e, e, t.unsqueeze(2).to_broadcast([P, PH, TOPK]), ALU.mult))

            @block.scalar
            def _(act):
                for tt in range(NT):
                    act.wait_ge(k.shift_ready.sem, k.shift_ready.at(tt + 1))
                    nc.scalar.activation(rows[:, tt, 2, :], rows[:, tt, 2, :],
                                         ACT.Exp).then_inc(k.exps_ready.up(), 1)
        units = []
        for n in range(3):
            trs = [lambda ps, n=n, tt=tt: nc.tensor.transpose(ps[:, tt * P:(tt + 1) * P], rows[:, tt, n, :], k.ident)
                   for tt in range(NT)]
            units.append((None, trs, "va"[n % 2], [copy_out(k, slots_T[:, n, :], P, S)]))
        run_products(k, units)

def peer_gates(k, slots_T, gates):
    nc = k.nc
    GRP = 4
    with ExitStack() as c:
        hot = k.sb("one_hots", [P, 2, 2, GRP, P], ctx=c)
        iota = k.sb("iota_keys", [P, PK], ctx=c)
        load_small(k, [(iota[:, :], k.const("iota"))])
        steps = S // GRP

        with k.stage() as block:
            def hots(dve, g, b, wait):
                if wait:
                    dve.wait_ge(k.products.sem, k.products.at(g - 1))
                for t in range(GRP):
                    tok = g * GRP + t
                    nc.vector.tensor_scalar(hot[:, b, 0, t, :], iota[:, :], slots_T[:, 0, bass.ds(tok, 1)], None,
                                            ALU.is_equal)
                    ins = nc.vector.tensor_scalar(hot[:, b, 1, t, :], iota[:, :], slots_T[:, 1, bass.ds(tok, 1)],
                                                  slots_T[:, 2, bass.ds(tok, 1)], ALU.is_equal, ALU.mult)
                ins.then_inc(k.onehots_ready.up(), 1)

            def outer(pe, g, b, wait):
                pe.wait_ge(k.onehots_ready.sem, k.onehots_ready.at(g + 1))
                if wait:
                    pe.wait_ge(k.gates_placed.sem, k.gates_placed.at(g - 1))
                for t in range(GRP):
                    last = mm(k, k.ps[:, b, t * P:(t + 1) * P], hot[:, b, 0, t, :], hot[:, b, 1, t, :])
                last.then_inc(k.products.up(), 1)

            def place(act, g, b):
                act.wait_ge(k.products.sem, k.products.at(g + 1))
                nc.scalar.activation(gates[:, :, bass.ds(g * GRP, GRP)],
                                     k.ps[:, b, :].rearrange("p (t n) -> p n t", t=GRP),
                                     ACT.Copy).then_inc(k.gates_placed.up(), 1)

            @block.vector
            def _(dve):
                for b in range(2):
                    hots(dve, b, b, False)
                with dve.Fori(1, steps // 2) as i:
                    for b in range(2):
                        hots(dve, 2 * i + b, b, True)
                k.onehots_ready.repeated(steps // 2 - 1, 2)

            @block.tensor
            def _(pe):
                for b in range(2):
                    outer(pe, b, b, False)
                with pe.Fori(1, steps // 2) as i:
                    for b in range(2):
                        outer(pe, 2 * i + b, b, True)
                k.products.repeated(steps // 2 - 1, 2)

            @block.scalar
            def _(act):
                with act.Fori(0, steps // 2) as i:
                    for b in range(2):
                        place(act, 2 * i + b, b)
                k.gates_placed.repeated(steps // 2, 2)

def peer_experts(k, hT, gates, first):
    nc = k.nc
    with ExitStack() as c:
        act_sb = k.sb("gelu_out", [P, 2, S], ctx=c)
        w_sb = k.sb("gated", [P, 2, S], ctx=c)
        loops = PK // 8

        def halves(j):
            tile = k.ring[:, (first + j // 2) % SLOTS, :]
            return (tile[:, (j % 2) * 1024:(j % 2 + 1) * 1024].rearrange("p (c e) -> p c e", c=DC),
                    tile[:, 2048 + (j % 2) * 1024:2048 + (j % 2 + 1) * 1024])

        with k.stage() as block:
            def pre(pe, i, j, start):
                n = 8 * i + j
                tile = first + j // 2
                if j % 2 == 0:
                    pe.wait_ge(k.stream.landed[tile % SLOTS].sem, 16 * (tile // SLOTS + 1) + 16 * i)
                if not start:
                    pe.wait_ge(k.act_ready.sem, k.act_ready.at(n - 3))
                u, _ = halves(j)
                for ch in range(DC):
                    last = mm(k, k.ps[:, 4 + j % 4, 0:S], u[:, ch, :], hT[:, ch, :], ch == 0, ch == DC - 1)
                last.then_inc(k.products.up(), 1)

            def post(pe, i, j, first_one, last_one):
                n = 8 * i + j
                pe.wait_ge(k.weights_gated.sem, k.weights_gated.at(n + 1))
                _, vv = halves(j)
                for tt in range(NT):
                    for half in range(2):
                        last = mm(k, k.ps[:, 2 * tt + half, :], w_sb[:, j % 2, tt * P:(tt + 1) * P],
                                  vv[:, half * 512:(half + 1) * 512], first_one, last_one)
                last.then_inc(k.down_products.up(), 1)

            def pe_turn(pe, i, first_turn, last_turn):
                for j in range(8):
                    if j < 7:
                        pre(pe, i, j + 1, first_turn and j + 1 < 4)
                    elif not last_turn:
                        pre(pe, i + 1, 0, False)
                    post(pe, i, j, first_turn and j == 0, last_turn and j == 7)

            def act_turn(act, i, first_turn):
                for j in range(8):
                    n = 8 * i + j
                    act.wait_ge(k.products.sem, k.products.at(n + 1))
                    if not (first_turn and j < 2):
                        act.wait_ge(k.weights_gated.sem, k.weights_gated.at(n - 1))
                    nc.scalar.activation(act_sb[:, j % 2, :], k.ps[:, 4 + j % 4, 0:S],
                                         ACT.Gelu).then_inc(k.act_ready.up(), 1)

            def dve_turn(dve, i, first_turn):
                for j in range(8):
                    n = 8 * i + j
                    dve.wait_ge(k.act_ready.sem, k.act_ready.at(n + 1))
                    if not (first_turn and j < 2):
                        dve.wait_ge(k.down_products.sem, k.down_products.at(n - 1))
                    g = gates[:, bass.ds(n, 1), :].rearrange("p a t -> p (a t)")
                    nc.vector.tensor_tensor(w_sb[:, j % 2, :], act_sb[:, j % 2, :], g,
                                            ALU.mult).then_inc(k.weights_gated.up(), 1)

            @block.sync
            def _(sp):
                def reload(i, j):
                    sp.wait_ge(k.down_products.sem, k.down_products.at(8 * i + 2 * j + 2))
                    slot = (first + j) % SLOTS
                    sp.dma_start(k.ring[:, slot, :].unsqueeze(1),
                                 k.dram["peer_uv"][bass.ds(4 * i + 4 + j, 1)].rearrange("a p n -> p a n")
                                 ).then_inc(k.stream.landed[slot].sem, 16)
                with sp.Fori(0, loops - 1) as i:
                    for j in range(4):
                        reload(i, j)
                k.stream.issued += 4 * (loops - 1)
                for j in range(4):
                    sp.wait_ge(k.down_products.sem, k.down_products.at(8 * (loops - 1) + 2 * j + 2))
                    k.stream.load(sp, k.stream.issued)
                    k.stream.issued += 1

            @block.tensor
            def _(pe):
                pre(pe, 0, 0, True)
                pe_turn(pe, 0, True, False)
                with pe.Fori(1, loops - 1) as i:
                    pe_turn(pe, i, False, False)
                k.products.repeated(loops - 2, 8)
                k.down_products.repeated(loops - 2, 8)
                pe_turn(pe, loops - 1, False, True)

            @block.scalar
            def _(act):
                act_turn(act, 0, True)
                with act.Fori(1, loops) as i:
                    act_turn(act, i, False)
                k.act_ready.repeated(loops - 1, 8)

            @block.vector
            def _(dve):
                dve_turn(dve, 0, True)
                with dve.Fori(1, loops) as i:
                    dve_turn(dve, i, False)
                k.weights_gated.repeated(loops - 1, 8)

def first_block(k, tiles):
    nc, sb = k.nc, k.sb
    keep, hT_keep = k.dram["x_rows"], k.dram["h_T"]
    with ExitStack() as c:
        x = sb("x", [P, NT, D], ctx=c)
        first_block_attention(k, x, tiles)
        hT = sb("peer_input_T", [P, DC, S], ctx=c)
        f = sb("x_factors", [P, NT], ctx=c)
        with ExitStack() as c2:
            y = sb("normed_x", [P, NT, D], ctx=c2)
            row_rsqrt(k, [(x[:, :, :], f[:, :])], 1e-6)
            with k.stage() as block:
                @block.vector
                def _(dve):
                    for tt in range(NT):
                        nc.vector.tensor_scalar(y[:, tt, :], x[:, tt, :], f[:, tt:tt + 1], None,
                                                ALU.mult).then_inc(k.dve_step.up(), 1)
            turn(k, y, DC, hT, lambda ch: k.col("g_ffn", ch))
        store(k, [(keep, x[:, :, :]), (hT_keep, hT[:, :, :])])
        slots_T = sb("slots_T", [P, 3, S], ctx=c)
        peer_routing(k, hT, tiles, slots_T)
        store(k, [(k.dram["slots"], slots_T[:, :, :])])
    with ExitStack() as c:
        gates = sb("gates", [P, PK, S], ctx=c)
        with ExitStack() as c2:
            slots_T = sb("slots_T_again", [P, 3, S], ctx=c2)
            load_small(k, [(slots_T[:, :, :], k.dram["slots"])])
            peer_gates(k, slots_T, gates)
        hT = sb("peer_input_T_again", [P, DC, S], ctx=c)
        load_small(k, [(hT[:, :, :], hT_keep)])
        peer_experts(k, hT, gates, tiles["peer"])

def store(k, pairs):
    with k.stage() as block:
        @block.scalar
        def _(act):
            for dst, src in pairs:
                act.dma_start(dst, src).then_inc(k.rows_stored.up(16), 16)
            act.wait_ge(k.rows_stored.sem, k.rows_stored.at(16 * len(pairs)))

def rwkv_and_gating(k, tiles, hT, cat_T):
    nc, sb = k.nc, k.sb
    W = RW_H * S
    with ExitStack() as c:
        AR = sb("rw_A_R", [64, RW_H, NCH, 2, CH], ctx=c)
        Bt = sb("rw_B_then_T", [64, W], ctx=c)
        Kt = sb("rw_K_then_T_T", [64, W], ctx=c)
        VN = sb("rw_V_rows", [64, NCH, RW_H, 64], ctx=c)
        sgl = sb("rw_gate_low", [P, S], ctx=c)
        decay_end = sb("rw_chunk_decay", [64, RW_H, NCH], ctx=c)
        bonus = sb("rw_bonus", [64, NCH * RW_H], ctx=c)
        pu = sb("sg_u", [P, NT, 512], ctx=c)
        pv = sb("sg_v", [P, NT, 512], ctx=c)
        hv = lambda t: t.rearrange("p (h t) -> p h t", h=RW_H)
        with ExitStack() as c2:
            r, kx, vx, ax, lw, cum, ex = (sb(n, [64, W], ctx=c2)[:, :] for n in
                                          ("rw_r", "rw_k", "rw_v", "rw_a", "rw_log_decay", "rw_cum", "rw_exp"))
            lora = sb("rw_lora", [64, 2, S], ctx=c2)
            low = sb("rw_lora_up", [64, 2, 512], ctx=c2)
            units = []
            t0 = tiles["ab_in"]
            for j, dst in enumerate((r, kx, vx)):
                for m in range(4):
                    d = hv(dst)
                    units.append(feature_products(k, hT, DC, t0 + j, 512, m * P, P,
                                                  [(d[:, 2 * m, :], 0, 64), (d[:, 2 * m + 1, :], 64, 64)],
                                                  "va"[m % 2]))
            units.append(feature_products(k, hT, DC, t0 + 3, 256, 0, P,
                                          [(lora[:, 0, :], 0, 64), (lora[:, 1, :], 64, 64)], "v"))
            units.append(feature_products(k, hT, DC, t0 + 3, 256, P, P, [(sgl[:, :], 0, P)], "a"))
            for j, dst in enumerate((pu, pv)):
                units += token_products(k, hT, DC, t0 + 4 + j, 512, 0, 512, lambda tt, dst=dst: dst[:, tt, :])
            run_products(k, units, (t0, t0 + 6))

            with k.stage() as block:
                @block.vector
                def _(dve):
                    v = nc.vector

                    def shift(dst, g, rows, mus):
                        d = dst.rearrange("p (g t) -> p g t", g=g)
                        e = (sg_tmp if rows == P else ex)[0:rows, 0:g * S].rearrange("p (g t) -> p g t", g=g)
                        k.v(v.tensor_tensor(e[:, :, 1:S], d[:, :, 0:S - 1], d[:, :, 1:S], ALU.subtract))
                        k.v(v.tensor_scalar(e[:, :, 0:1], d[:, :, 0:1], -1.0, None, ALU.mult))
                        for i in range(g):
                            v.scalar_tensor_tensor(out=d[:, i, :], in0=e[:, i, :], scalar=mus(i), in1=d[:, i, :],
                                                   op0=ALU.mult, op1=ALU.add).then_inc(k.dve_step.up(), 1)
                        v.wait_ge(k.dve_step.sem, k.dve_step.count)
                    sg_tmp = cat_T[:, 0, :]
                    for n, dst in enumerate((r, kx, vx)):
                        shift(dst, RW_H, 64, lambda i, n=n: k.col("mu_rkv", 8 * n + i, 64))
                    shift(lora[:, :, :].rearrange("p a t -> p (a t)"), 2, 64, lambda i: k.col("mu_rkv", 24 + i, 64))
                    shift(sgl[:, :], 1, P, lambda i: k.col("mu_g", 13))

                @block.scalar
                def _(act):
                    act.dma_start(low[:, 0, :], k.dram["rw_w2_2"].rearrange("a p n -> (a p) n")
                                  ).then_inc(k.small_loaded.up(16), 16)
                    act.dma_start(low[:, 1, :], k.dram["rw_a2_2"].rearrange("a p n -> (a p) n")
                                  ).then_inc(k.small_loaded.up(16), 16)
                    act.wait_ge(k.small_loaded.sem, k.small_loaded.at(32))
                    act.wait_ge(k.dve_step.sem, k.dve_step.count)
                    nc.scalar.activation(lora[:, 0, :], lora[:, 0, :], ACT.Tanh).then_inc(k.act_step.up(), 1)
                    nc.scalar.activation(sgl[:, :], sgl[:, :], ACT.Sigmoid).then_inc(k.act_step.up(), 1)

            def squashed(dst, h, name):
                def go(eng, ps):
                    return nc.scalar.activation(hv(dst)[:, h, :], ps[0:64, 0:S], ACT.Sigmoid,
                                                bias=k.col(name, h, 64))
                return go
            units = []
            for n, (dst, name) in enumerate(((lw, "w0"), (ax, "a0"))):
                for h in range(RW_H):
                    units.append((None, [lambda ps, n=n, h=h: mm(k, ps[0:64, 0:S], low[:, n, h * 64:(h + 1) * 64],
                                                                 lora[:, n, :])], "a", [squashed(dst, h, name)]))
            run_products(k, units)

            with ExitStack() as c3:
                reset = sb("rw_chunk_resets", [64, W], ctx=c3)
                load_small(k, [(reset[:, :], k.const("reset", 64))])
                with k.stage() as block:
                    @block.vector
                    def _(dve):
                        v = nc.vector
                        k.v(v.tensor_scalar(lw, lw, -math.exp(-0.5), None, ALU.mult))
                        k.v(v.tensor_tensor_scan(cum, reset[:, :], lw, 0.0, ALU.mult, ALU.add))
                        for h in range(RW_H):
                            v.tensor_scalar(hv(ex)[:, h, :], hv(kx)[:, h, :], k.col("k_k", h, 64), None,
                                            ALU.mult).then_inc(k.dve_step.up(), 1)
                        v.wait_ge(k.dve_step.sem, k.dve_step.count)
                        k.v(v.tensor_tensor(reset[:, :], ex, ex, ALU.mult))
                ones = sb("rw_ones", [64, 64], ctx=c3)
                load_small(k, [(ones[:, :], k.const("ones", 64))])
                run_products(k, [(None, [lambda ps, n=n: mm(k, ps[0:64, :], ones[:, :],
                                                            reset[:, n * 512:(n + 1) * 512])], "a",
                                  [lambda eng, ps, n=n: nc.scalar.activation(Bt[:, n * 512:(n + 1) * 512],
                                                                             ps[0:64, :], ACT.Sqrt)])
                                 for n in range(W // 512)])
                with k.stage() as block:
                    @block.vector
                    def _(dve):
                        v = nc.vector
                        k.v(v.tensor_scalar(Bt[:, :], Bt[:, :], 1e-12, None, ALU.max))
                        k.v(v.reciprocal(Bt[:, :], Bt[:, :]))
                        k.v(v.tensor_tensor(ex, ex, Bt[:, :], ALU.mult))
                        for h in range(RW_H):
                            v.tensor_scalar(hv(reset[:, :])[:, h, :], hv(ax)[:, h, :], 1.0, k.col("k_a", h, 64),
                                            ALU.subtract, ALU.mult).then_inc(k.dve_step.up(), 1)
                        v.wait_ge(k.dve_step.sem, k.dve_step.count)
                        k.v(v.scalar_tensor_tensor(out=kx, in0=reset[:, :], scalar=1.0, in1=kx,
                                                   op0=ALU.add, op1=ALU.mult))
                        k.v(v.tensor_tensor(reset[:, :], r, kx, ALU.mult))
                        v.tensor_tensor(lw, cum, lw, ALU.subtract).then_inc(k.shift_ready.up(), 1)
                        k.v(v.tensor_tensor(ax, ax, ex, ALU.mult))
                        dve.wait_ge(k.exps_ready.sem, k.exps_ready.at(1))
                        part = lambda i: AR[:, :, :, i, :].rearrange("p h c t -> p (h c) t")
                        ch = lambda t: t.rearrange("p (g t) -> p g t", t=CH)
                        k.v(v.scalar_tensor_tensor(out=part(0), in0=ch(ex), scalar=-1.0, in1=ch(lw),
                                                   op0=ALU.mult, op1=ALU.mult))
                        dve.wait_ge(k.exps_ready.sem, k.exps_ready.at(2))
                        k.v(v.tensor_tensor(Bt[:, :], ax, Kt[:, :], ALU.mult))
                        k.v(v.tensor_tensor(Kt[:, :], kx, Kt[:, :], ALU.mult))
                        dve.wait_ge(k.exps_ready.sem, k.exps_ready.at(3))
                        k.v(v.tensor_tensor(part(1), ch(r), ch(cum), ALU.mult))
                        k.v(v.tensor_copy(decay_end[:, :, :].rearrange("p h c -> p (h c)"),
                                          ch(cum)[:, :, CH - 1]))

                    @block.scalar
                    def _(act):
                        act.wait_ge(k.shift_ready.sem, k.shift_ready.at(1))
                        for out, src, s in ((lw, lw, 1.0), (Kt[:, :], cum, -1.0), (cum, cum, 1.0)):
                            nc.scalar.activation(out, src, ACT.Exp, scale=s).then_inc(k.exps_ready.up(), 1)
                units = []
                for n in range(2):
                    units.append((None, [lambda ps, i=i, n=n: mm(
                        k, ps[0:64, i:i + 1], hv(reset[:, :])[:, (16 * n + i) % RW_H,
                                                             (16 * n + i) // RW_H * CH:((16 * n + i) // RW_H + 1) * CH],
                        k.col("r_k", (16 * n + i) % RW_H, 64)) for i in range(16)], "v",
                        [copy_out(k, bonus[:, 16 * n:16 * n + 16], 64, 16)]))
                units += chunk_rows(k, vx, VN)
                run_products(k, units)

        with ExitStack() as c2:
            rows = sb("sg_norm_rows", [P, 2, 512], ctx=c2)
            wT = sb("sg_weights_T", [P, SG, P], ctx=c2)
            stt = sb("sg_sums", [P, NT * SG], ctx=c2)
            var = sb("sg_vars", [P, NT * SG], ctx=c2)
            sq = sb("sg_squares", [P, NT * SG, P], ctx=c2)
            z = pv[:, :, :].rearrange("p t (g n) -> p (t g) n", g=SG)
            bc = lambda t: t.unsqueeze(2).to_broadcast([P, NT * SG, P])
            with k.stage() as block:
                @block.scalar
                def _(act):
                    act.dma_start(rows[:, 0, :], k.dram["sg_ln_g_2"].rearrange("a g n -> (a g n)")
                                  .partition_broadcast(P)).then_inc(k.small_loaded.up(16), 16)
                    act.dma_start(rows[:, 1, :], k.dram["sg_ln_b_2"].rearrange("a g n -> (a g n)")
                                  .partition_broadcast(P)).then_inc(k.small_loaded.up(16), 16)
                    act.dma_start(wT[:, :, :], k.dram["sg_ws_T"]).then_inc(k.small_loaded.up(16), 16)
                    for t in (pv, pu):
                        nc.scalar.activation(t[:, :, :], t[:, :, :], ACT.Gelu_apprx_tanh
                                             ).then_inc(k.act_step.up(), 1)
                    act.wait_ge(k.shift_ready.sem, k.shift_ready.at(1))
                    nc.scalar.activation(var[:, :], var[:, :], ACT.Sqrt).then_inc(k.act_step.up(), 1)

                @block.gpsimd
                def _(pool):
                    pool.wait_ge(k.small_loaded.sem, k.small_loaded.at(48))
                    nc.gpsimd.affine_select(out=wT[:, :, :], in_=wT[:, :, :], pattern=[[0, SG], [1, P]],
                                            compare_op=ALU.is_ge, fill=0.0, base=0, channel_multiplier=-1
                                            ).then_inc(k.gated_ready.up(), 1)
                    pool.wait_ge(k.gated_ready.sem, k.gated_ready.at(1))

                @block.vector
                def _(dve):
                    v = nc.vector
                    dve.wait_ge(k.act_step.sem, k.act_step.at(2))
                    k.v(v.tensor_reduce(stt[:, :], z, AX, ALU.add))
                    k.v(v.tensor_scalar(stt[:, :], stt[:, :], 1.0 / P, None, ALU.mult))
                    k.v(v.tensor_tensor(z, z, bc(stt[:, :]), ALU.subtract))
                    k.v(v.tensor_tensor(sq[:, :, :], z, z, ALU.mult))
                    k.v(v.tensor_reduce(var[:, :], sq[:, :, :], AX, ALU.add))
                    v.tensor_scalar(var[:, :], var[:, :], 1.0 / P, 1e-5, ALU.mult,
                                    ALU.add).then_inc(k.shift_ready.up(), 1)
                    dve.wait_ge(k.small_loaded.sem, k.small_loaded.at(48))
                    dve.wait_ge(k.act_step.sem, k.act_step.at(3))
                    k.v(v.reciprocal(var[:, :], var[:, :]))
                    k.v(v.tensor_tensor(z, z, bc(var[:, :]), ALU.mult))
                    for tt in range(NT):
                        k.v(v.tensor_tensor(pv[:, tt, :], pv[:, tt, :], rows[:, 0, :], ALU.mult))
                        k.v(v.tensor_tensor(pv[:, tt, :], pv[:, tt, :], rows[:, 1, :], ALU.add))
            units = []
            for tt in range(NT):
                def gate(g, tt=tt):
                    def go(eng, ps):
                        col = slice(g * P, (g + 1) * P)
                        return nc.vector.scalar_tensor_tensor(out=pu[:, tt, col], in0=ps[:, col],
                                                              scalar=k.col("sg_b", g), in1=pu[:, tt, col],
                                                              op0=ALU.add, op1=ALU.mult)
                    return go
                units.append((None, [lambda ps, g=g, tt=tt: mm(k, ps[:, g * P:(g + 1) * P], wT[:, g, :],
                                                               pv[:, tt, g * P:(g + 1) * P]) for g in range(SG)],
                              "v", [gate(g) for g in range(SG)]))
            run_products(k, units)
        turn(k, pu, 4, cat_T[:, 4:8, :])

        BN = sb("rw_B_rows", [64, NCH, RW_H, 64], ctx=c)
        KN = sb("rw_K_rows", [64, NCH, RW_H, 64], ctx=c)
        LB = sb("rw_lower_B", [64, NCH * RW_H, 2 * CH], ctx=c)
        LK = sb("rw_lower_K", [64, NCH * RW_H, 2 * CH], ctx=c)
        X = sb("rw_level_product", [64, W], ctx=c)
        Lm = sb("rw_level_part", [64, W], ctx=c)
        lv = sb("rw_levels", [64, 6, CH], ctx=c)
        tri = sb("rw_triangles", [64, 2 * CH], ctx=c)
        load_small(k, [(lv[:, :, :].rearrange("p a b -> p (a b)"), k.const("levels", 64)), (tri[:, :], k.const("tri", 64))])
        units = chunk_rows(k, Bt[:, :], BN) + chunk_rows(k, Kt[:, :], KN)
        for src, dst in ((Bt, LB), (Kt, LK)):
            for g in range(8):
                def masked(eng, ps, dst=dst, g=g):
                    return nc.vector.tensor_tensor(dst[:, 4 * g:4 * g + 4, :],
                                                   ps[0:64, :].rearrange("p (a b) -> p a b", a=4),
                                                   tri[:, :].unsqueeze(1).to_broadcast([64, 4, 2 * CH]), ALU.mult)
                def prod(ps, a, src=src, g=g):
                    ci, h = divmod(4 * g + a, RW_H)
                    return mm(k, ps[0:64, a * P:(a + 1) * P], hv(src[:, :])[:, h, ci * CH:(ci + 1) * CH],
                              AR[:, h, ci, :, :].rearrange("p a t -> p (a t)"))
                units.append((None, [lambda ps, a=a, prod=prod: prod(ps, a) for a in range(4)], "v", [masked]))
        run_products(k, units)

        T, TT = Bt, Kt
        pairs = NCH * RW_H
        q = lambda t: t[:, :].rearrange("p (g n) -> p g n", g=pairs)
        with k.stage() as block:
            @block.vector
            def _(dve):
                v = nc.vector
                eye = k.ident[0:64, 0:64].unsqueeze(1).to_broadcast([64, pairs, 64])
                v.tensor_copy(q(T), eye).then_inc(k.dve_step.up(), 1)
                v.tensor_copy(q(TT), eye).then_inc(k.dve_step.up(), 1)
        for level in range(6):
            with k.stage() as block:
                @block.vector
                def _(dve):
                    nc.vector.tensor_tensor(q(Lm), LB[:, :, 0:CH],
                                            lv[:, level, :].unsqueeze(1).to_broadcast([64, pairs, CH]),
                                            ALU.mult).then_inc(k.dve_step.up(), 1)
            run_products(k, [(None, [lambda ps, i=i, g=g: mm(k, ps[0:64, i * 64:(i + 1) * 64], q(Lm)[:, 8 * g + i, :],
                                                             q(T)[:, 8 * g + i, :]) for i in range(8)], "va"[g % 2],
                              [copy_out(k, X[:, g * 512:(g + 1) * 512], 64, 512)]) for g in range(4)])

            def added(dst, g):
                def go(eng, ps):
                    d = dst[:, g * 512:(g + 1) * 512]
                    return nc.vector.tensor_tensor(d, d, ps[0:64, :], ALU.add)
                return go
            units = []
            for g in range(4):
                units.append((None, [lambda ps, i=i, g=g: mm(k, ps[0:64, i * 64:(i + 1) * 64], q(X)[:, 8 * g + i, :],
                                                             q(TT)[:, 8 * g + i, :]) for i in range(8)], "v", []))
                units.append((None, [lambda ps, i=i, g=g: mm(k, ps[0:64, i * 64:(i + 1) * 64], q(TT)[:, 8 * g + i, :],
                                                             q(X)[:, 8 * g + i, :]) for i in range(8)], "v",
                              [lambda eng, ps, g=g: added(T, g)(eng, ps),
                               lambda eng, ps, g=g: added(TT, g)(eng, k.ps[:, 2 * g, :])]))
            run_products(k, units)

        gn = sb("rw_gn_rows", [64, 2, 512], ctx=c)
        Y = sb("rw_y", [64, NCH, RW_H, 64], ctx=c)
        U = sb("rw_U", [64, 512], ctx=c)
        SA = sb("rw_SA", [64, 512], ctx=c)
        ST = sb("rw_state_T", [64, RW_H, 64], ctx=c)
        hs = lambda h: slice(h * 64, (h + 1) * 64)
        with k.stage() as block:
            @block.tensor
            def _(pe):
                for ci in range(NCH):
                    A = lambda h: AR[:, h, ci, 0, :]
                    R = lambda h: AR[:, h, ci, 1, :]
                    if ci:
                        pe.wait_ge(k.hidden_ready.sem, k.hidden_ready.at(2 * ci))
                    for h in range(RW_H):
                        if ci:
                            mm(k, k.ps[0:64, 0, hs(h)], A(h), ST[:, h, :], True, False)
                        last = mm(k, k.ps[0:64, 0, hs(h)], LK[:, ci * RW_H + h, 0:CH], VN[:, ci, h, :], not ci, True)
                    last.then_inc(k.products.up(), 1)
                    pe.wait_ge(k.act_ready.sem, k.act_ready.at(3 * ci + 1))
                    for h in range(RW_H):
                        last = mm(k, k.ps[0:64, 1, hs(h)], q(TT)[:, ci * RW_H + h, :], U[:, hs(h)])
                    last.then_inc(k.products.up(), 1)
                    pe.wait_ge(k.act_ready.sem, k.act_ready.at(3 * ci + 2))
                    for h in range(RW_H):
                        mm(k, k.ps[0:64, 2, hs(h)], BN[:, ci, h, :], SA[:, hs(h)], True, False)
                        last = mm(k, k.ps[0:64, 2, hs(h)], KN[:, ci, h, :], VN[:, ci, h, :], False, True)
                    last.then_inc(k.products.up(), 1)
                    for h in range(RW_H):
                        if ci:
                            mm(k, k.ps[0:64, 3, hs(h)], R(h), ST[:, h, :], True, False)
                        mm(k, k.ps[0:64, 3, hs(h)], LB[:, ci * RW_H + h, CH:2 * CH], SA[:, hs(h)], not ci, False)
                        last = mm(k, k.ps[0:64, 3, hs(h)], LK[:, ci * RW_H + h, CH:2 * CH], VN[:, ci, h, :], False, True)
                    last.then_inc(k.products.up(), 1)

            @block.scalar
            def _(act):
                act.dma_start(gn[:, 0, :], k.dram["rw_gn_g_2"].rearrange("a n -> (a n)").partition_broadcast(64)
                              ).then_inc(k.small_loaded.up(16), 16)
                act.dma_start(gn[:, 1, :], k.dram["rw_gn_b_2"].rearrange("a n -> (a n)").partition_broadcast(64)
                              ).then_inc(k.small_loaded.up(16), 16)
                act.wait_ge(k.small_loaded.sem, k.small_loaded.at(32))
                for ci in range(NCH):
                    for n, dst in enumerate((U[:, :], SA[:, :], Y[:, ci, :, :].rearrange("p h n -> p (h n)"))):
                        bank = (0, 1, 3)[n]
                        act.wait_ge(k.products.sem, k.products.at(4 * ci + (1, 2, 4)[n]))
                        nc.scalar.activation(dst, k.ps[0:64, bank, :], ACT.Copy).then_inc(k.act_ready.up(), 1)

            @block.vector
            def _(dve):
                v = nc.vector
                for ci in range(NCH):
                    flat = ST[:, :, :].rearrange("p h n -> p (h n)")
                    dve.wait_ge(k.products.sem, k.products.at(4 * ci + 4))
                    if ci:
                        v.tensor_tensor(flat, flat, k.ps[0:64, 2, :], ALU.add).then_inc(k.hidden_ready.up(), 1)
                    else:
                        v.tensor_copy(flat, k.ps[0:64, 2, :]).then_inc(k.hidden_ready.up(), 1)
                    v.wait_ge(k.hidden_ready.sem, k.hidden_ready.at(2 * ci + 1))
                    dve.wait_ge(k.act_ready.sem, k.act_ready.at(3 * ci + 3))
                    v.tensor_tensor(ST[:, :, :], ST[:, :, :], decay_end[:, :, ci:ci + 1].to_broadcast([64, RW_H, 64]),
                                    ALU.mult).then_inc(k.hidden_ready.up(), 1)

        with ExitStack() as c2:
            g2 = pu[:, 0, :]
            load_small(k, [(g2, k.dram["rw_g2_2"].rearrange("a p n -> (a p) n"))])
            mean = sb("rw_means", [64, pairs], ctx=c2)
            var = sb("rw_vars", [64, pairs], ctx=c2)
            y3 = Y[:, :, :, :].rearrange("p c h n -> p (c h) n")
            sq = q(X)
            bc = lambda t: t.unsqueeze(2).to_broadcast([64, pairs, 64])
            with k.stage() as block:
                @block.vector
                def _(dve):
                    v = nc.vector
                    k.v(v.tensor_reduce(mean[:, :], y3, AX, ALU.add))
                    k.v(v.tensor_scalar(mean[:, :], mean[:, :], 1.0 / RW_N, None, ALU.mult))
                    k.v(v.tensor_tensor(y3, y3, bc(mean[:, :]), ALU.subtract))
                    k.v(v.tensor_tensor(sq, y3, y3, ALU.mult))
                    k.v(v.tensor_reduce(var[:, :], sq, AX, ALU.add))
                    v.tensor_scalar(var[:, :], var[:, :], 1.0 / RW_N, 64e-5, ALU.mult,
                                    ALU.add).then_inc(k.shift_ready.up(), 1)
                    dve.wait_ge(k.act_step.sem, k.act_step.at(1))
                    k.v(v.reciprocal(var[:, :], var[:, :]))
                    k.v(v.tensor_tensor(y3, y3, bc(var[:, :]), ALU.mult))
                    yc = Y[:, :, :, :].rearrange("p c h n -> p c (h n)")
                    row = lambda n: gn[:, n, :].unsqueeze(1).to_broadcast([64, NCH, 512])
                    k.v(v.tensor_tensor(yc, yc, row(0), ALU.mult))
                    k.v(v.tensor_tensor(yc, yc, row(1), ALU.add))
                    k.v(v.tensor_tensor(sq, VN[:, :, :, :].rearrange("p c h n -> p (c h) n"), bc(bonus[:, :]),
                                        ALU.mult))
                    k.v(v.tensor_tensor(y3, y3, sq, ALU.add))

                @block.scalar
                def _(act):
                    act.wait_ge(k.shift_ready.sem, k.shift_ready.at(1))
                    nc.scalar.activation(var[:, :], var[:, :], ACT.Sqrt).then_inc(k.act_step.up(), 1)

            def gated(ci):
                def go(eng, ps):
                    y = Y[:, ci, :, :].rearrange("p h n -> p (h n)")
                    return nc.vector.tensor_tensor(y, y, ps[0:64, :], ALU.mult)
                return go
            run_products(k, [(None, [lambda ps, ci=ci: mm(k, ps[0:64, :], sgl[:, ci * CH:(ci + 1) * CH], g2)],
                              "v", [gated(ci)]) for ci in range(NCH)])
            turn(k, Y[:, :, :, :].rearrange("p c h n -> p c (h n)"), 4, cat_T, None, CH, NCH)

def chunk_rows(k, src, dst):
    units = []
    for ci in range(NCH):
        trs = [lambda ps, h=h, ci=ci: k.nc.tensor.transpose(
            ps[0:64, h * 64:(h + 1) * 64], src[:, h * S + ci * CH:h * S + (ci + 1) * CH],
            k.ident[0:64, 0:64]) for h in range(RW_H)]
        units.append((None, trs, "va"[ci % 2],
                      [copy_out(k, dst[:, ci, :, :].rearrange("p h n -> p (h n)"), 64, 512)]))
    return units

def mla(k, x, hT, tiles):
    nc, sb = k.nc, k.sb
    with ExitStack() as c:
        q_T = sb("mla_q_T", [MLA_QK, MLA_H, S], ctx=c)
        k_T = sb("mla_k_T", [MLA_QK, MLA_H, S], ctx=c)
        kv = sb("mla_kv", [P, NT, 2048], ctx=c)
        with ExitStack() as c2:
            p = sb("mla_p", [P, NT, 544], ctx=c2)
            low_T = sb("mla_low_T", [P, 4, S], ctx=c2)
            f = sb("mla_factors", [P, NT, 2], ctx=c2)
            t0 = tiles["mla_in"]
            units = token_products(k, hT, DC, t0, 512, 0, 512, lambda tt: p[:, tt, 0:512])
            units += token_products(k, hT, DC, t0 + 1, 32, 0, 32, lambda tt: p[:, tt, 512:544])
            run_products(k, units, (t0, t0 + 2))
            jobs = [(p[:, tt, 256 * i:256 * (i + 1)].unsqueeze(1), f[:, tt, i:i + 1])
                    for tt in range(NT) for i in range(2)]
            row_rsqrt(k, jobs, 1e-6)
            scale_groups(k, jobs)
            turn(k, p, 4, low_T, lambda ch: k.col("q_norm", ch))
            q = sb("mla_q", [P, NT, MLA_H * MLA_QK], ctx=c2)
            units = []
            for j in range(3):
                units += token_products(k, low_T[:, 0:2, :], 2, t0 + 2, 1536, 512 * j, 512,
                                        lambda tt, j=j: q[:, tt, 512 * j:512 * (j + 1)])
            for j in range(4):
                units += token_products(k, low_T[:, 2:4, :], 2, t0 + 3, 2048, 512 * j, 512,
                                        lambda tt, j=j: kv[:, tt, 512 * j:512 * (j + 1)])
            run_products(k, units, (t0 + 2, t0 + 4))
            half = MLA_ROPE // 2
            trig = sb("mla_cos_sin", [P, 2, NT, half], ctx=c2)
            tmp = sb("mla_rotated", [P, MLA_H + 1, 2 * half], ctx=c2)
            kf = sb("mla_k", [P, NT, MLA_H, MLA_QK], ctx=c2)
            load_small(k, [(trig[:, n, :, :].rearrange("p a b -> p (a b)"), k.const(s)) for n, s in enumerate(("cos", "sin"))])
            with k.stage() as block:
                @block.vector
                def _(dve):
                    v = nc.vector
                    for tt in range(NT):
                        qs = q[:, tt, :].rearrange("p (h w) -> p h w", h=MLA_H)[:, :, MLA_NOPE:]
                        ks = p[:, tt, 512:544].unsqueeze(1)
                        for a, n, t in ((qs, MLA_H, tmp[:, 0:MLA_H, :]), (ks, 1, tmp[:, MLA_H:, :])):
                            sh = [P, n, half]
                            cs = trig[:, 0, tt, :].unsqueeze(1).to_broadcast(sh)
                            sn = trig[:, 1, tt, :].unsqueeze(1).to_broadcast(sh)
                            a1, a2 = a[:, :, 0:half], a[:, :, half:]
                            k.v(v.tensor_tensor(t[:, :, 0:half], a2, sn, ALU.mult))
                            k.v(v.tensor_tensor(t[:, :, half:], a1, sn, ALU.mult))
                            k.v(v.tensor_tensor(a1, a1, cs, ALU.mult))
                            k.v(v.tensor_tensor(a2, a2, cs, ALU.mult))
                            k.v(v.tensor_tensor(a1, a1, t[:, :, 0:half], ALU.subtract))
                            k.v(v.tensor_tensor(a2, a2, t[:, :, half:], ALU.add))
                        v.tensor_copy(kf[:, tt, :, MLA_NOPE:], ks.to_broadcast([P, MLA_H, MLA_ROPE])
                                      ).then_inc(k.dve_step.up(), 1)
                        v.tensor_copy(kf[:, tt, :, 0:MLA_NOPE], kv[:, tt, :].rearrange(
                            "p (h w) -> p h w", h=MLA_H)[:, :, 0:MLA_NOPE]).then_inc(k.dve_step.up(), 1)
            units = []
            for src, dst, who, s in ((q, q_T, "v", MLA_QK ** -0.5), (kf, k_T, "a", None)):
                for h in range(0, MLA_H, 2):
                    def piece(tt, hh, src=src):
                        if src is q:
                            return q[:, tt, hh * MLA_QK:(hh + 1) * MLA_QK]
                        return kf[:, tt, hh, :]
                    trs = [lambda ps, a=a, tt=tt, h=h, piece=piece: nc.tensor.transpose(
                        ps[0:MLA_QK, a * S + tt * P:a * S + (tt + 1) * P], piece(tt, h + a), k.ident)
                        for a in range(2) for tt in range(NT)]
                    units.append((None, trs, who, [copy_out(k, dst[:, h:h + 2, :].rearrange("p a b -> p (a b)"),
                                                            MLA_QK, 512, s)]))
            run_products(k, units)
        out = sb("mla_out", [P, NT, D], ctx=c)
        mask = sb("mla_causal", [P, NT * S], ctx=c)
        load_small(k, [(mask[:, :], k.const("causal"))])
        attention(k, [([q_T[:, h, :]], [k_T[:, h, :]],
                       lambda kt, h=h: kv[:, kt, h * 128 + MLA_NOPE:(h + 1) * 128], ("masked", mask[:, :]),
                       lambda tt, h=h: out[:, tt, h * MLA_V:(h + 1) * MLA_V]) for h in range(MLA_H)], MLA_V)
        outT = sb("mla_out_T", [P, DC, S], ctx=c)
        turn(k, out, DC, outT)
        project_residual(k, outT, DC, t0 + 4, x, ALPHA)

def cross_attention(k, x, hT, layer, tiles):
    nc, sb = k.nc, k.sb
    t0 = tiles[f"xa{layer}"]
    with ExitStack() as c:
        q_T = sb("xa_q_T", [P, DC, S], ctx=c)
        k_T = sb("xa_k_T", [P, DC, S], ctx=c)
        v = sb("xa_v", [P, NT, D], ctx=c)
        out = sb("xa_out", [P, NT, D], ctx=c)
        memT = sb("memory_2_T", [P, DC, S], ctx=c)
        load_small(k, [(memT[:, :, :], k.dram["mem_2_T"])])
        units = []
        for src, dst, t, s in ((hT, q_T, t0, XA_D ** -0.5), (memT, k_T, t0 + 2, None)):
            for j in range(2):
                for m in range(4):
                    u = feature_products(k, src, DC, t + j, 512, m * P, P, [(dst[:, 4 * j + m, :], 0, P)], "va"[m % 2])
                    units.append(u[:3] + ([copy_out(k, dst[:, 4 * j + m, :], P, S, s)],))
        for j in range(2):
            units += token_products(k, memT, DC, t0 + 4 + j, 512, 0, 512, lambda tt, j=j: v[:, tt, 512 * j:512 * (j + 1)])
        run_products(k, units, (t0, t0 + 6))
        attention(k, [([q_T[:, 2 * h, :], q_T[:, 2 * h + 1, :]], [k_T[:, 2 * h, :], k_T[:, 2 * h + 1, :]],
                       lambda kt, h=h: v[:, kt, h * XA_D:(h + 1) * XA_D], ("plain", None),
                       lambda tt, h=h: out[:, tt, h * XA_D:(h + 1) * XA_D]) for h in range(XA_H)], XA_D)
        outT = sb("xa_out_T", [P, DC, S], ctx=c)
        turn(k, out, DC, outT)
        project_residual(k, outT, DC, t0 + 6, x, ALPHA)

def moe(k, x, hT, layer, tiles):
    nc, sb = k.nc, k.sb
    first = tiles[f"moe{layer}"]
    with ExitStack() as c:
        gate_rows = sb("expert_gates_all", [P, NE, S], ctx=c)
        with ExitStack() as c2:
            NL = NG + NE
            w = sb("router_weights", [P, DC, NL], ctx=c2)
            bias = sb("router_bias", [P, NL], ctx=c2)
            iota = sb("router_iota", [P, NE], ctx=c2)
            lg = sb("router_logits", [P, NT, NL], ctx=c2)
            g8 = sb("group_logits", [P, NT, 8], ctx=c2)
            top = sb("router_top", [P, NT, 8], ctx=c2)
            at = sb("router_at", [P, NT, 8], U32, ctx=c2)
            atf = sb("router_at_float", [P, NT, 8], ctx=c2)
            neg = sb("router_neg", [P, NT, 1], ctx=c2)
            gsum = sb("router_sum", [P, NT, 1], ctx=c2)
            hot = sb("group_hot", [P, NT, NG], ctx=c2)
            off = sb("group_off", [P, NT, NG], ctx=c2)
            gexp = sb("group_exps", [P, NT, NG], ctx=c2)
            le = sb("expert_logits", [P, NT, NE], ctx=c2)
            e2 = sb("second_exp", [P, NT, 1], ctx=c2)
            g1 = sb("gate_first", [P, NT, 2], ctx=c2)
            gt = sb("gate_table", [P, NT, NE], ctx=c2)
            g2t = sb("gate_table_second", [P, NT, NE], ctx=c2)
            gT = sb("gate_table_T", [NE, S], ctx=c2)
            load_small(k, [(w[:, :, 0:NG], k.dram["moe_w_group_2"][layer].rearrange("(c p) n -> p c n", p=P)),
                           (w[:, :, NG:NL], k.dram["moe_w_expert_2"][layer].rearrange("(c p) n -> p c n", p=P)),
                           (bias[:, 0:NG], k.dram["moe_b_group_2"][layer].partition_broadcast(P)),
                           (bias[:, NG:NL], k.dram["moe_b_expert_2"][layer].partition_broadcast(P)),
                           (iota[:, :], k.const("iota")[:, 0:NE])])
            run_products(k, [(None, [lambda ps, kk=kk, tt=tt: mm(k, ps[:, 0:NL], hT[:, kk, tt * P:(tt + 1) * P],
                                                                 w[:, kk, :], kk == 0, kk == DC - 1)
                                     for kk in range(DC)], "v",
                              [lambda eng, ps, tt=tt: nc.vector.tensor_tensor(lg[:, tt, :], ps[:, 0:NL], bias[:, :],
                                                                              ALU.add)]) for tt in range(NT)])
            with k.stage() as block:
                @block.vector
                def _(dve):
                    v = nc.vector
                    k.v(v.memset(g8[:, :, :], -3e38))
                    k.v(v.tensor_copy(g8[:, :, 0:NG], lg[:, :, 0:NG]))
                    for tt in range(NT):
                        k.v(v.max(top[:, tt, :], g8[:, tt, :]))
                        k.v(v.max_index(at[:, tt, :], top[:, tt, :], g8[:, tt, :]))
                    k.v(v.tensor_copy(atf[:, :, :], at[:, :, :]))
                    v.tensor_scalar(neg[:, :, :], top[:, :, 0:1], -1.0, None,
                                    ALU.mult).then_inc(k.shift_ready.up(), 1)
                    for tt in range(NT):
                        k.v(v.tensor_scalar(hot[:, tt, :], iota[:, 0:NG], atf[:, tt, 0:1], None, ALU.is_equal))
                    k.v(v.tensor_scalar(off[:, :, :], hot[:, :, :], 1.0, 1e30, ALU.subtract, ALU.mult))
                    for tt in range(NT):
                        e = le[:, tt, :].rearrange("p (g n) -> p g n", g=NG)
                        lt = lg[:, tt, NG:NL].rearrange("p (g n) -> p g n", g=NG)
                        bc = lambda t: t.unsqueeze(2).to_broadcast([P, NG, NPG])
                        k.v(v.tensor_tensor(e, lt, bc(hot[:, tt, :]), ALU.mult))
                        k.v(v.tensor_tensor(e, e, bc(off[:, tt, :]), ALU.add))
                        k.v(v.max(top[:, tt, :], le[:, tt, :]))
                        k.v(v.max_index(at[:, tt, :], top[:, tt, :], le[:, tt, :]))
                    k.v(v.tensor_copy(atf[:, :, :], at[:, :, :]))
                    v.tensor_tensor(e2[:, :, :], top[:, :, 1:2], top[:, :, 0:1],
                                    ALU.subtract).then_inc(k.shift_ready.up(), 1)
                    dve.wait_ge(k.exps_ready.sem, k.exps_ready.at(NT))
                    k.v(v.reciprocal(gsum[:, :, :], gsum[:, :, :]))
                    dve.wait_ge(k.exps_ready.sem, k.exps_ready.at(NT + 1))
                    k.v(v.tensor_scalar(g1[:, :, 0:1], e2[:, :, :], 1.0, None, ALU.add))
                    k.v(v.reciprocal(g1[:, :, 0:1], g1[:, :, 0:1]))
                    k.v(v.tensor_tensor(g1[:, :, 0:1], g1[:, :, 0:1], gsum[:, :, :], ALU.mult))
                    k.v(v.tensor_tensor(g1[:, :, 1:2], g1[:, :, 0:1], e2[:, :, :], ALU.mult))
                    for tt in range(NT):
                        k.v(v.tensor_scalar(gt[:, tt, :], iota[:, :], atf[:, tt, 0:1], g1[:, tt, 0:1],
                                            ALU.is_equal, ALU.mult))
                        k.v(v.tensor_scalar(g2t[:, tt, :], iota[:, :], atf[:, tt, 1:2], g1[:, tt, 1:2],
                                            ALU.is_equal, ALU.mult))
                    k.v(v.tensor_tensor(gt[:, :, :], gt[:, :, :], g2t[:, :, :], ALU.add))

                @block.scalar
                def _(act):
                    act.wait_ge(k.shift_ready.sem, k.shift_ready.at(1))
                    for tt in range(NT):
                        nc.scalar.activation(gexp[:, tt, :], lg[:, tt, 0:NG], ACT.Exp,
                                             bias=neg[:, tt, :], accum_out=gsum[:, tt, :]
                                             ).then_inc(k.exps_ready.up(), 1)
                    act.wait_ge(k.shift_ready.sem, k.shift_ready.at(2))
                    nc.scalar.activation(e2[:, :, :], e2[:, :, :], ACT.Exp).then_inc(k.exps_ready.up(), 1)
            run_products(k, [(None, [lambda ps, tt=tt: nc.tensor.transpose(ps[0:NE, tt * P:(tt + 1) * P],
                                                                           gt[:, tt, :], k.ident)
                                     for tt in range(NT)], "v", [copy_out(k, gT[:, :], NE, S)])])
            store(k, [(k.dram["expert_gates"], gT[:, :])])
            load_small(k, [(gate_rows[:, :, :], k.dram["expert_gates"].partition_broadcast(P))])

        silu = sb("silu_out", [P, 2, S], ctx=c)
        hid = sb("expert_hidden", [P, 2, 4, S], ctx=c)
        TURN = 4
        turns = NE // TURN
        with k.stage() as block:
            def tile_of(i, e, part, eng=None):
                tile = first + 3 * e + part
                if eng is not None:
                    eng.wait_ge(k.stream.landed[tile % SLOTS].sem, 16 * (tile // SLOTS + 1) + 48 * i)
                flat = k.ring[:, tile % SLOTS, :]
                return flat.rearrange("p (c n) -> p c n", c=4 if part == 2 else DC)

            def ups(pe, i, e, start):
                n = TURN * i + e
                for m in range(4):
                    for part in range(2):
                        w = tile_of(i, e, part, pe if m == 0 else None)
                        if not (start and m < 2):
                            s = (k.silu_ready, k.gated_ready)[part]
                            pe.wait_ge(s.sem, s.at(4 * n + m - 1))
                        for kk in range(DC):
                            last = mm(k, k.ps[:, 4 + 2 * (m % 2) + part, 0:S], w[:, kk, m * P:(m + 1) * P],
                                      hT[:, kk, :], kk == 0, kk == DC - 1)
                        last.then_inc((k.gate_products, k.up_products)[part].up(), 1)

            def downs(pe, i, e, first_one, last_one):
                n = TURN * i + e
                w = tile_of(i, e, 2, pe)
                pe.wait_ge(k.hidden_ready.sem, k.hidden_ready.at(4 * n + 4))
                for tt in range(NT):
                    for half in range(2):
                        for m in range(4):
                            last = mm(k, k.ps[:, 2 * tt + half, :], hid[:, e % 2, m, tt * P:(tt + 1) * P],
                                      w[:, m, half * 512:(half + 1) * 512], first_one and m == 0, last_one and m == 3)
                last.then_inc(k.down_products.up(), 1)

            def pe_turn(pe, i, first_turn, last_turn):
                for e in range(TURN):
                    if e < TURN - 1:
                        ups(pe, i, e + 1, False)
                    elif not last_turn:
                        ups(pe, i + 1, 0, False)
                    downs(pe, i, e, first_turn and e == 0, last_turn and e == TURN - 1)

            def act_turn(act, i, start):
                for e in range(TURN):
                    for m in range(4):
                        n = 4 * (TURN * i + e) + m
                        act.wait_ge(k.gate_products.sem, k.gate_products.at(n + 1))
                        if not (start and e == 0 and m < 2):
                            act.wait_ge(k.gated_ready.sem, k.gated_ready.at(n - 1))
                        nc.scalar.activation(silu[:, m % 2, :], k.ps[:, 4 + 2 * (m % 2), 0:S],
                                             ACT.Silu).then_inc(k.silu_ready.up(), 1)

            def dve_turn(dve, i, start):
                for e in range(TURN):
                    x_n = TURN * i + e
                    g = gate_rows[:, bass.ds(x_n, 1), :].rearrange("p a t -> p (a t)")
                    for m in range(4):
                        n = 4 * x_n + m
                        h = hid[:, e % 2, m, :]
                        if m == 0 and not (start and e < 2):
                            dve.wait_ge(k.down_products.sem, k.down_products.at(x_n - 1))
                        dve.wait_ge(k.silu_ready.sem, k.silu_ready.at(n + 1))
                        dve.wait_ge(k.up_products.sem, k.up_products.at(n + 1))
                        nc.vector.tensor_tensor(h, silu[:, m % 2, :], k.ps[:, 5 + 2 * (m % 2), 0:S],
                                                ALU.mult).then_inc(k.gated_ready.up(), 1)
                        dve.wait_ge(k.gated_ready.sem, k.gated_ready.at(n + 1))
                        nc.vector.tensor_tensor(h, h, g, ALU.mult).then_inc(k.hidden_ready.up(), 1)

            @block.sync
            def _(sp):
                end = first + 3 * NE

                def reload(i, t, dynamic):
                    e, part = divmod(t, 3)
                    n = TURN * i + e
                    if part < 2:
                        s = (k.gate_products, k.up_products)[part]
                        sp.wait_ge(s.sem, s.at(4 * n + 4))
                    else:
                        sp.wait_ge(k.down_products.sem, k.down_products.at(n + 1))
                    if dynamic:
                        slot = (first + t) % SLOTS
                        ahead = t + SLOTS
                        e2, part2 = divmod(ahead, 3)
                        src = k.dram["moe_parts"][part2][layer, bass.ds(TURN * i + e2, 1)].rearrange(
                            "a (c p) n -> p (a c) n", p=P)
                        dst = k.ring[:, slot, :].rearrange("p (c n) -> p c n", c=4 if part2 == 2 else DC)
                        sp.dma_start(dst, src).then_inc(k.stream.landed[slot].sem, 16)
                    elif k.stream.issued < len(k.stream.sources):
                        k.stream.load(sp, k.stream.issued)
                        k.stream.issued += 1
                with sp.Fori(0, turns - 1) as i:
                    for t in range(3 * TURN):
                        reload(i, t, True)
                k.stream.issued += 3 * TURN * (turns - 1)
                for t in range(3 * TURN):
                    reload(turns - 1, t, False)

            @block.tensor
            def _(pe):
                ups(pe, 0, 0, True)
                pe_turn(pe, 0, True, False)
                with pe.Fori(1, turns - 1) as i:
                    pe_turn(pe, i, False, False)
                for s, each in ((k.gate_products, 4), (k.up_products, 4), (k.down_products, 1)):
                    s.repeated(turns - 2, each * TURN)
                pe_turn(pe, turns - 1, False, True)

            @block.scalar
            def _(act):
                act_turn(act, 0, True)
                with act.Fori(1, turns) as i:
                    act_turn(act, i, False)
                k.silu_ready.repeated(turns - 1, 4 * TURN)

            @block.vector
            def _(dve):
                dve_turn(dve, 0, True)
                with dve.Fori(1, turns) as i:
                    dve_turn(dve, i, False)
                k.gated_ready.repeated(turns - 1, 4 * TURN)
                k.hidden_ready.repeated(turns - 1, 4 * TURN)
        add_banks(k, x, ALPHA)

def add_banks(k, x, alpha):
    with k.stage() as block:
        @block.vector
        def _(dve):
            for tt in range(NT):
                for half in range(2):
                    xs = x[:, tt, half * 512:(half + 1) * 512]
                    k.nc.vector.scalar_tensor_tensor(out=xs, in0=xs, scalar=alpha, in1=k.ps[:, 2 * tt + half, :],
                                                     op0=ALU.mult, op1=ALU.add).then_inc(k.dve_step.up(), 1)

def second_block(k, tiles, out):
    nc, sb = k.nc, k.sb
    keep = k.dram["x_rows"]
    layer_rows = lambda name, layer: k.dram[name][layer]
    with ExitStack() as c:
        cat_T = sb("mixed_2_T", [P, DC, S], ctx=c)
        with ExitStack() as c2:
            x = sb("x_first", [P, NT, D], ctx=c2)
            load_small(k, [(x[:, :, :], keep)])
            add_banks(k, x, 1.0)
            store(k, [(keep, x[:, :, :])])
            turn(k, x, DC, cat_T)
        rwkv_and_gating(k, tiles, cat_T, cat_T)
        x = sb("x_second", [P, NT, D], ctx=c)
        load_small(k, [(x[:, :, :], keep)])
        project_residual(k, cat_T, DC, tiles["ab_out"], x, ALPHA)
        hT = sb("h_T", [P, DC, S], ctx=c)
        for layer in range(2):
            if layer == 1:
                mla(k, x, hT, tiles)
            layer_norm(k, x, layer_rows("ln1_g_2", layer), layer_rows("ln1_b_2", layer))
            turn(k, x, DC, hT)
            cross_attention(k, x, hT, layer, tiles)
            layer_norm(k, x, layer_rows("ln2_g_2", layer), layer_rows("ln2_b_2", layer))
            turn(k, x, DC, hT)
            moe(k, x, hT, layer, tiles)
            layer_norm(k, x, layer_rows("ln3_g_2", layer), layer_rows("ln3_b_2", layer))
            if layer == 0:
                turn(k, x, DC, hT)
        store(k, [(out.rearrange("a (t p) d -> p (a t) d", p=P), x[:, :, :])])

def build(nc, dram, out):
    with ExitStack() as ctx:
        k = Kernel(nc, dram, ctx)

        def columns(w, width=512):
            n = w.shape[1]
            v = w.rearrange("(c p) n -> p c n", p=P)
            return [v[:, :, j:min(j + width, n)] for j in range(0, n, width)]

        def wt(name, layer=0):
            return dram[name][layer]
        st, tiles = k.stream, {}
        tiles["w_in"] = st.add(columns(wt("w_in")))
        tiles["w_mem_kv"] = st.add(columns(wt("w_mem_kv")))
        tiles["w_out"] = st.add(columns(wt("w_out")))
        tiles["w_peer_q"] = st.add(columns(wt("w_peer_q")))
        tiles["peer"] = st.add([dram["peer_uv"][i].unsqueeze(1) for i in range(PK // 2)])
        w = wt("ab_w_in_2")
        tiles["ab_in"] = st.add(columns(w[:, 0:1536]) + columns(w[:, 1536:1792]) + columns(w[:, 1792:2816]))
        tiles["ab_out"] = st.add(columns(wt("ab_w_out_2")))

        def tail(layer):
            tiles[f"xa{layer}"] = st.add(columns(wt("xa_wq_2", layer)) + columns(wt("xa_wkv_2", layer))
                                         + columns(wt("xa_wo_2", layer)))
            parts = []
            for e in range(NE):
                for m in k.dram["moe_parts"]:
                    parts += columns(m[layer, e], 1024)
            tiles[f"moe{layer}"] = st.add(parts)
        tail(0)
        tiles["mla_in"] = st.add(columns(wt("mla_w_in_2")) + columns(wt("mla_wq_b_2"), 2048)
                                 + columns(wt("mla_wkv_b_2"), 2048) + columns(wt("mla_w_out_2")))
        tail(1)
        first_block(k, tiles)
        second_block(k, tiles, out)

PLAIN = ["x", "mem", "w_in", "w_mem_kv", "w_out", "w_peer_q", "ab_w_in_2", "rw_w2_2", "rw_a2_2", "rw_g2_2",
         "rw_gn_g_2", "rw_gn_b_2", "sg_ln_g_2", "sg_ln_b_2", "ab_w_out_2", "mla_w_in_2", "mla_wq_b_2",
         "mla_wkv_b_2", "mla_w_out_2", "ln1_g_2", "ln1_b_2", "xa_wq_2", "xa_wkv_2", "xa_wo_2", "ln2_g_2",
         "ln2_b_2", "moe_w_group_2", "moe_b_group_2", "moe_w_expert_2", "moe_b_expert_2", "moe_w_gate_2",
         "moe_w_up_2", "moe_w_down_2", "ln3_g_2", "ln3_b_2"]

def laid_out(inputs):
    a = {n: np.ascontiguousarray(inputs[n]) for n in PLAIN}
    for n in (1, 2):
        a[f"subkeys_T_{n}"] = np.ascontiguousarray(np.asarray(inputs[f"peer_subkeys_{n}"])[0].transpose(2, 0, 1))
    u = np.asarray(inputs["peer_u"])[0].reshape(PK, PK // 2, 2, DC, P).transpose(1, 4, 2, 3, 0)
    v = np.asarray(inputs["peer_v"])[0].reshape(PK, PK // 2, 2, D).transpose(1, 0, 2, 3)
    a["peer_uv"] = np.concatenate([u.reshape(PK // 2, P, -1), v.reshape(PK // 2, P, -1)], 2)
    a["sg_ws_T"] = np.ascontiguousarray(np.asarray(inputs["sg_ws_2"])[0].transpose(2, 0, 1))
    a["mem_2_T"] = np.ascontiguousarray(np.asarray(inputs["mem_2"])[0].T.reshape(DC, P, S).transpose(1, 0, 2))
    cols = []
    for name, src, rows, n in vector_columns():
        m = np.asarray(inputs[src]).reshape(n, rows).T
        cols.append(np.concatenate([m, np.zeros((P - rows, n), m.dtype)], 0))
    a["columns"] = np.ascontiguousarray(np.concatenate(cols, 1))
    a["consts"] = shape_constants()[1]
    return a

def kernel(**inputs):
    import concourse.bacc as bacc
    from concourse.bass_utils import run_bass_kernel_spmd

    nc = bacc.Bacc("TRN2", target_bir_lowering=False, num_devices=1)
    arrays = laid_out(inputs)
    dram = {n: nc.dram_tensor(f"in_{n}", a.shape, F32, kind="ExternalInput").ap() for n, a in arrays.items()}
    for n, shape in (("x_rows", [P, NT, D]), ("h_T", [P, DC, S]), ("slots", [P, 3, S]), ("expert_gates", [NE, S])):
        dram[n] = nc.dram_tensor(n, shape, F32, kind="Internal").ap()
    dram["moe_parts"] = [dram["moe_w_gate_2"], dram["moe_w_up_2"], dram["moe_w_down_2"]]
    out = nc.dram_tensor("out_rows", [1, S, D], F32, kind="ExternalOutput").ap()
    build(nc, dram, out)
    r = run_bass_kernel_spmd(nc, [{f"in_{n}": a for n, a in arrays.items()}], core_ids=[0])
    return r.results[0]["out_rows"]
```

```python
from contextlib import ExitStack, contextmanager
import math

import numpy as np
import concourse.bass as bass
from concourse import mybir

ALU = mybir.AluOpType
ACT = mybir.ActivationFunctionType
F32 = mybir.dt.float32
U32 = mybir.dt.uint32
AX = mybir.AxisListType.X

P = 128
S = 256
NT = S // P
D = 1024
DC = D // P
MASKED = -1e32

HD = 64
H_DIL, H_MOBA, H_MEM = 6, 6, 4
H_MIX = H_DIL + H_MOBA + H_MEM
IN_W = 3 * HD * (H_DIL + H_MOBA) + HD * H_MEM
N_ALIBI = H_DIL + H_MOBA
SLOPES = [2.0 ** (-8.0 * (i + 1) / N_ALIBI) for i in range(N_ALIBI)]

PH, PK, TOPK = 8, 128, 16
RW_H, RW_N, CH = 8, 64, 64
NCH = S // CH
SG = 4
MLA_H, MLA_NOPE, MLA_ROPE, MLA_V = 16, 64, 32, 64
MLA_QK = MLA_NOPE + MLA_ROPE
XA_H, XA_D = 4, 256
NG, NPG = 4, 8
NE = NG * NPG
FF = 512
PAIRS = 2 * S
WINDOWS = NE + (PAIRS - 1) // (P + 1)
ALPHA = 4.0 ** 0.25
SLOT = 4096
SLOTS = 4

def shape_constants():
    t = np.arange(S)
    dist = (t[:, None] - t[None, :]).astype(np.float32)
    causal = dist >= 0
    idist = dist.astype(np.int64)
    count = ((causal & (idist <= 128)).astype(np.float32) + (causal & (idist % 4 == 0))
             + (causal & (idist % 16 == 0))).astype(np.float32)
    rows = lambda m: m.reshape(NT, P, S).transpose(1, 0, 2).reshape(P, NT * S)
    c = {}
    c["ident"] = np.eye(P, dtype=np.float32)
    c["iota"] = np.tile(np.arange(PAIRS + P, dtype=np.float32), (P, 1))
    c["ones"] = np.ones((P, P), np.float32)
    c["before"] = (np.arange(P)[:, None] < np.arange(P)[None, :]).astype(np.float32)
    c["dist_moba"] = rows(np.where(causal, -dist, MASKED))
    c["dist_dil"] = rows(np.where(count > 0, -dist, MASKED))
    c["count"] = rows(count)
    c["causal"] = rows(np.where(causal, 0.0, MASKED))
    half = MLA_ROPE // 2
    inv = 10000.0 ** (-np.arange(half, dtype=np.float32) / half)
    ang = (t[:, None].astype(np.float32) * inv[None, :]).astype(np.float32)
    pack = lambda m: m.reshape(NT, P, half).transpose(1, 0, 2).reshape(P, NT * half)
    c["cos"], c["sin"] = pack(np.cos(ang)), pack(np.sin(ang))
    s64, t64 = np.arange(CH)[:, None], np.arange(CH)[None, :]
    pad = lambda m: np.concatenate([m.reshape(CH, -1), np.zeros((P - CH, m.size // CH))], 0)
    c["tri"] = pad(np.concatenate([s64 < t64, s64 <= t64], 1))
    lev = [((s64 // (2 * b) == t64 // (2 * b)) & (s64 % (2 * b) < b) & (t64 % (2 * b) >= b))
           for b in (1, 2, 4, 8, 16, 32)]
    c["levels"] = pad(np.stack(lev, 1))
    c["reset"] = np.tile((np.arange(RW_H * S) % CH != 0).astype(np.float32), (P, 1))
    at, parts, n = {}, [], 0
    for k, v in c.items():
        v = np.ascontiguousarray(v, dtype=np.float32)
        at[k] = (n, v.shape[1])
        n += v.shape[1]
        parts.append(v)
    return at, np.concatenate(parts, 1)

def vector_columns():
    return [("g_mix", "g_mix", P, DC), ("g_memtok", "g_memtok", P, DC), ("g_ffn", "g_ffn", P, DC),
            ("qg_dil", "qg_dil", HD, 1), ("kg_dil", "kg_dil", HD, 1), ("qg_moba", "qg_moba", HD, 1),
            ("kg_moba", "kg_moba", HD, 1), ("qg_mem", "qg_mem", HD, 1), ("kg_mem", "kg_mem", HD, 1),
            ("og_dil", "og_dil", P, 3), ("og_moba", "og_moba", P, 3), ("og_mem", "og_mem", P, 2),
            ("mu_rkv", "ab_mu_2", 64, 28), ("w0", "rw_w0_2", 64, 8), ("a0", "rw_a0_2", 64, 8),
            ("k_k", "rw_k_k_2", 64, 8), ("k_a", "rw_k_a_2", 64, 8), ("r_k", "rw_r_k_2", 64, 8),
            ("mu_g", "ab_mu_2", P, 14), ("sg_b", "sg_b_2", P, SG),
            ("q_norm", "mla_q_norm_2", P, 2), ("kv_norm", "mla_kv_norm_2", P, 2)]

def column_places():
    at, n = {}, 0
    for name, _, _, cols in vector_columns():
        at[name] = (n, cols)
        n += cols
    return at, n

class Signal:

    def __init__(self, nc, name):
        self.sem = nc.alloc_semaphore(name=name)
        self.count = self.start = 0

    def up(self, n=1):
        self.count += n
        return self.sem

    def at(self, n):
        return self.start + n

    def repeated(self, times, each):
        self.count += (times - 1) * each

class WeightStream:

    def __init__(self, k):
        self.k = k
        self.sources = []
        self.issued = 0
        self.landed = [Signal(k.nc, f"weights_landed_{i}") for i in range(SLOTS)]

    def add(self, aps):
        first = len(self.sources)
        self.sources += aps
        return first

    def view(self, n, kc, cols):
        return self.k.ring[:, n % SLOTS, 0:kc * cols].rearrange("p (k n) -> p k n", k=kc)

    def load(self, sp, n):
        src = self.sources[n]
        kc, cols = src.shape[1], src.shape[2]
        sp.dma_start(self.view(n, kc, cols), src).then_inc(self.landed[n % SLOTS].up(16), 16)

    def wait_landed(self, pe, n):
        pe.wait_ge(self.landed[n % SLOTS].sem, 16 * (n // SLOTS + 1))

    def prefetch(self, sp, end, first, freed):
        while self.issued < min(end + SLOTS, len(self.sources)) and self.sources[self.issued] is not None:
            old = self.issued - SLOTS
            if old >= first:
                sp.wait_ge(self.k.products.sem, self.k.products.at(freed[old]))
            self.load(sp, self.issued)
            self.issued += 1

class Kernel:
    def __init__(self, nc, dram, ctx):
        self.nc, self.dram, self.ctx, self.allocated = nc, dram, ctx, 0
        self.signals = []

        def signal(name):
            self.signals.append(Signal(nc, name))
            return self.signals[-1]
        self.products = signal("products")
        self.dve_evacuated = signal("dve_evacuated")
        self.act_evacuated = signal("act_evacuated")
        self.dve_step = signal("dve_step")
        self.act_step = signal("act_step")
        self.small_loaded = signal("small_loaded")
        self.scores_ready = signal("scores_ready")
        self.scores_read = signal("scores_read")
        self.shift_ready = signal("shift_ready")
        self.exps_ready = signal("exps_ready")
        self.probs_ready = signal("probs_ready")
        self.probs_turned = signal("probs_turned")
        self.turned_copied = signal("turned_copied")
        self.heads_ready = signal("heads_ready")
        self.heads_scaled = signal("heads_scaled")
        self.rows_stored = signal("rows_stored")
        self.onehots_ready = signal("onehots_ready")
        self.gates_placed = signal("gates_placed")
        self.act_ready = signal("act_ready")
        self.weights_gated = signal("weights_gated")
        self.hidden_ready = signal("hidden_ready")
        self.gate_products = signal("gate_products")
        self.up_products = signal("up_products")
        self.silu_ready = signal("silu_ready")
        self.gated_ready = signal("gated_ready")
        self.window_ready = signal("window_ready")
        self.down_products = signal("down_products")
        self.ring = self.sb("weight_ring", [P, SLOTS, SLOT])
        self.ps = ctx.enter_context(nc.psum_tensor("banks", [P, 8, 512], F32))
        self.stream = WeightStream(self)
        self.const_at, _ = shape_constants()
        self.col_at, ncols = column_places()
        self.cols_sb = self.sb("columns", [P, ncols])
        self.ident = self.sb("identity", [P, P])[:, :]

    def sb(self, name, shape, dt=F32, ctx=None):
        self.allocated += 1
        return (ctx or self.ctx).enter_context(self.nc.sbuf_tensor(f"{name}_{self.allocated}", shape, dt))

    @contextmanager
    def stage(self):
        with self.nc.Block() as block:
            yield block
        for s in self.signals:
            s.start = s.count

    def const(self, name, rows=P):
        a, n = self.const_at[name]
        return self.dram["consts"][0:rows, a:a + n]

    def col(self, name, i, rows=P):
        a, _ = self.col_at[name]
        return self.cols_sb[0:rows, a + i:a + i + 1]

    def cols(self, name, rows=P):
        a, n = self.col_at[name]
        return self.cols_sb[0:rows, a:a + n]

    def v(self, ins):
        ins.then_inc(self.dve_step.up(), 1)
        self.nc.vector.wait_ge(self.dve_step.sem, self.dve_step.count)

    def a(self, ins):
        ins.then_inc(self.act_step.up(), 1)
        self.nc.scalar.wait_ge(self.act_step.sem, self.act_step.count)

def load_small(k, pairs):
    with k.stage() as block:
        @block.sync
        def _(sp):
            if not k.stream.issued:
                k.stream.prefetch(sp, 0, 0, {})

        @block.scalar
        def _(act):
            for dst, src in pairs:
                act.dma_start(dst, src).then_inc(k.small_loaded.up(16), 16)
            act.wait_ge(k.small_loaded.sem, k.small_loaded.at(16 * len(pairs)))

def run_products(k, units, tiles=(0, 0)):
    nc = k.nc
    served = {"v": 0, "a": 0}
    order = []
    for tile, _, who, copies in units:
        served[who] += len(copies)
        order.append(served[who])
    freed = {}
    for u, (tile, *_) in enumerate(units):
        if tile is not None:
            freed[tile] = u + 1
    emptied = {"v": k.dve_evacuated, "a": k.act_evacuated}

    with k.stage() as block:
        @block.sync
        def _(sp):
            k.stream.prefetch(sp, tiles[1] if tiles[1] else k.stream.issued - SLOTS, tiles[0], freed)

        @block.tensor
        def _(pe):
            seen = set()
            for u, (tile, products, _, _) in enumerate(units):
                if tile is not None and tile not in seen:
                    k.stream.wait_landed(pe, tile)
                    seen.add(tile)
                if u >= 8:
                    pe.wait_ge(emptied[units[u - 8][2]].sem, emptied[units[u - 8][2]].at(order[u - 8]))
                for product in products:
                    last = product(k.ps[:, u % 8, :])
                last.then_inc(k.products.up(), 1)

        @block.vector
        def _(dve):
            for u, (_, _, who, copies) in enumerate(units):
                if who == "v":
                    dve.wait_ge(k.products.sem, k.products.at(u + 1))
                    for copy in copies:
                        copy(nc.vector, k.ps[:, u % 8, :]).then_inc(k.dve_evacuated.up(), 1)

        @block.scalar
        def _(act):
            for u, (_, _, who, copies) in enumerate(units):
                if who == "a":
                    act.wait_ge(k.products.sem, k.products.at(u + 1))
                    for copy in copies:
                        copy(nc.scalar, k.ps[:, u % 8, :]).then_inc(k.act_evacuated.up(), 1)

def mm(k, out, lhsT, rhs, start=True, stop=True):
    return k.nc.tensor.matmul(out, lhsT, rhs, start=start, stop=stop)

def copy_out(k, out, rows, cols, scale=None, cols0=0, rows0=0):
    def go(eng, ps):
        src = ps[rows0:rows0 + rows, cols0:cols0 + cols]
        if len(out.shape) == 3:
            src = src.rearrange("p (a b) -> p a b", a=out.shape[1])
        if eng is k.nc.scalar:
            return eng.activation(out, src, ACT.Copy, scale=1.0 if scale is None else scale)
        if scale is None:
            return eng.tensor_copy(out, src)
        return eng.tensor_scalar(out, src, scale, None, ALU.mult)
    return go

def token_products(k, xT, kc, tile, cols, c0, width, out, who=None, copy=None):
    units = []
    w = k.stream.view(tile, kc, cols)
    for tt in range(NT):
        def prod(ps, kk, tt=tt):
            return mm(k, ps[:, 0:width], xT[:, kk, tt * P:(tt + 1) * P], w[:, kk, c0:c0 + width],
                      kk == 0, kk == kc - 1)
        cp = copy(tt) if copy else copy_out(k, out(tt), P, width)
        units.append((tile, [lambda ps, kk=kk, prod=prod: prod(ps, kk) for kk in range(kc)],
                      who or "va"[tt % 2], [cp]))
    return units

def feature_products(k, xT, kc, tile, cols, c0, m, outs, who):
    w = k.stream.view(tile, kc, cols)
    prods = [lambda ps, kk=kk: mm(k, ps[0:m, 0:S], w[:, kk, c0:c0 + m], xT[:, kk, 0:S],
                                  kk == 0, kk == kc - 1) for kk in range(kc)]
    return (tile, prods, who, [copy_out(k, o, r, S, rows0=r0) for o, r0, r in outs])

def turn(k, src, n, outT, gain=None, pt=P, tiles=NT):
    units = []
    for c in range(n):
        trs = [lambda ps, c=c, tt=tt: k.nc.tensor.transpose(ps[:, tt * pt:(tt + 1) * pt],
                                                            src[0:pt, tt, c * P:(c + 1) * P],
                                                            k.ident[0:pt, 0:pt]) for tt in range(tiles)]
        units.append((None, trs, "va"[c % 2],
                      [copy_out(k, outT[:, c, :], P, tiles * pt, gain(c) if gain else None)]))
    run_products(k, units)

def row_rsqrt(k, jobs, eps):
    nc = k.nc
    with ExitStack() as c:
        sq = k.sb("squares", [P, 2048], ctx=c)
        with k.stage() as block:
            @block.vector
            def _(dve):
                for src, out in jobs:
                    p, g, w = src.shape
                    view = sq[0:p, 0:g * w].rearrange("p (g w) -> p g w", g=g)
                    k.v(nc.vector.tensor_tensor(view, src, src, ALU.mult))
                    k.v(nc.vector.tensor_reduce(out, view, AX, ALU.add))
                    k.v(nc.vector.tensor_scalar(out, out, 1.0 / w, eps, ALU.mult, ALU.add))
                for n, (_, out) in enumerate(jobs):
                    dve.wait_ge(k.act_step.sem, k.act_step.at(n + 1))
                    nc.vector.reciprocal(out, out).then_inc(k.dve_step.up(), 1)

            @block.scalar
            def _(act):
                for n, (_, out) in enumerate(jobs):
                    act.wait_ge(k.dve_step.sem, k.dve_step.at(3 * (n + 1)))
                    nc.scalar.activation(out, out, ACT.Sqrt).then_inc(k.act_step.up(), 1)

def scale_groups(k, jobs):
    with k.stage() as block:
        @block.vector
        def _(dve):
            for rows, f in jobs:
                p, g, w = rows.shape
                k.nc.vector.tensor_tensor(rows, rows, f.unsqueeze(2).to_broadcast([p, g, w]),
                                          ALU.mult).then_inc(k.dve_step.up(), 1)

def layer_norm(k, x, g_row, b_row, eps=1e-5):
    nc = k.nc
    with ExitStack() as c:
        gb = k.sb("ln_gain_bias", [P, 2, D], ctx=c)
        st = k.sb("ln_stats", [P, NT, 2, 6], ctx=c)
        mv = k.sb("ln_mean_var", [P, NT, 2], ctx=c)
        rs = k.sb("ln_rstd", [P, NT, 1], ctx=c)
        with k.stage() as block:
            @block.scalar
            def _(act):
                act.dma_start(gb[:, 0, :], g_row.partition_broadcast(P)).then_inc(k.small_loaded.up(16), 16)
                act.dma_start(gb[:, 1, :], b_row.partition_broadcast(P)).then_inc(k.small_loaded.up(16), 16)
                for tt in range(NT):
                    act.wait_ge(k.dve_step.sem, k.dve_step.at(4 * (tt + 1)))
                    nc.scalar.activation(rs[:, tt, :], rs[:, tt, :], ACT.Sqrt).then_inc(k.act_step.up(), 1)

            @block.vector
            def _(dve):
                for tt in range(NT):
                    k.v(nc.vector.bn_stats(st[:, tt, 0, :], x[:, tt, 0:512]))
                    k.v(nc.vector.bn_stats(st[:, tt, 1, :], x[:, tt, 512:1024]))
                    k.v(nc.vector.bn_aggr(mv[:, tt, :], st[:, tt, :, :].rearrange("p a b -> p (a b)")))
                    k.v(nc.vector.tensor_scalar(rs[:, tt, :], mv[:, tt, 1:2], eps, None, ALU.add))
                dve.wait_ge(k.small_loaded.sem, k.small_loaded.at(32))
                for tt in range(NT):
                    dve.wait_ge(k.act_step.sem, k.act_step.at(tt + 1))
                    k.v(nc.vector.reciprocal(rs[:, tt, :], rs[:, tt, :]))
                    k.v(nc.vector.tensor_scalar(x[:, tt, :], x[:, tt, :], mv[:, tt, 0:1], rs[:, tt, :],
                                                ALU.subtract, ALU.mult))
                    k.v(nc.vector.tensor_tensor(x[:, tt, :], x[:, tt, :], gb[:, 0, :], ALU.mult))
                    k.v(nc.vector.tensor_tensor(x[:, tt, :], x[:, tt, :], gb[:, 1, :], ALU.add))

def attention(k, heads, dv):
    nc, H = k.nc, len(heads)
    with ExitStack() as c:
        sc = k.sb("scores", [P, 2, NT, S], ctx=c)
        pT = k.sb("probs_T", [P, 2, 2, S], ctx=c)
        top = k.sb("row_max", [P, H, NT], ctx=c)
        den = k.sb("row_sum", [P, H, NT], ctx=c)
        with k.stage() as block:
            @block.tensor
            def _(pe):
                for i in range(H + 2):
                    if i < H:
                        q, kt, _, _, _ = heads[i]
                        if i >= 2:
                            pe.wait_ge(k.scores_read.sem, k.scores_read.at(i - 1))
                        for tt in range(NT):
                            for n in range(len(q)):
                                last = mm(k, k.ps[:, i % 2, tt * S:(tt + 1) * S], q[n][:, tt * P:(tt + 1) * P],
                                          kt[n], n == 0, n == len(q) - 1)
                        last.then_inc(k.scores_ready.up(), 1)
                    h = i - 1
                    if 0 <= h < H:
                        pe.wait_ge(k.probs_ready.sem, k.probs_ready.at(h + 1))
                        if h >= 2:
                            pe.wait_ge(k.turned_copied.sem, k.turned_copied.at(h - 1))
                        for kt2 in range(2):
                            for tt in range(NT):
                                last = nc.tensor.transpose(k.ps[:, 2 + h % 2, kt2 * S + tt * P:kt2 * S + (tt + 1) * P],
                                                           sc[:, h % 2, tt, kt2 * P:(kt2 + 1) * P], k.ident)
                        last.then_inc(k.probs_turned.up(), 1)
                    h = i - 2
                    if 0 <= h < H:
                        pe.wait_ge(k.turned_copied.sem, k.turned_copied.at(h + 1))
                        if h >= 2:
                            pe.wait_ge(k.heads_scaled.sem, k.heads_scaled.at(NT * (h - 1)))
                        for tt in range(NT):
                            for kt2 in range(2):
                                last = mm(k, k.ps[:, 4 + h % 2, tt * 256:tt * 256 + dv],
                                          pT[:, h % 2, kt2, tt * P:(tt + 1) * P], heads[h][2](kt2),
                                          kt2 == 0, kt2 == 1)
                        last.then_inc(k.heads_ready.up(), 1)

            @block.vector
            def _(dve):
                for i in range(H + 2):
                    if i < H:
                        kind, arg = heads[i][3]
                        flat = sc[:, i % 2, :, :].rearrange("p a b -> p (a b)")
                        dve.wait_ge(k.scores_ready.sem, k.scores_ready.at(i + 1))
                        if i >= 2:
                            dve.wait_ge(k.probs_turned.sem, k.probs_turned.at(i - 1))
                        if kind == "alibi":
                            slope, dist, _ = arg
                            ins = nc.vector.scalar_tensor_tensor(out=flat, in0=dist, scalar=slope,
                                                                 in1=k.ps[:, i % 2, :], op0=ALU.mult, op1=ALU.add)
                        elif kind == "masked":
                            ins = nc.vector.tensor_tensor(flat, arg, k.ps[:, i % 2, :], ALU.add)
                        else:
                            ins = nc.vector.tensor_copy(flat, k.ps[:, i % 2, :])
                        ins.then_inc(k.scores_read.up(), 1)
                        dve.wait_ge(k.scores_read.sem, k.scores_read.at(i + 1))
                        k.v(nc.vector.tensor_reduce(top[:, i, :], sc[:, i % 2, :, :], AX, ALU.max))
                        nc.vector.tensor_scalar(top[:, i, :], top[:, i, :], -1.0, None,
                                                ALU.mult).then_inc(k.shift_ready.up(), 1)
                    h = i - 1
                    if 0 <= h < H:
                        kind, arg = heads[h][3]
                        dve.wait_ge(k.exps_ready.sem, k.exps_ready.at(NT * (h + 1)))
                        if kind == "alibi" and arg[2] is not None:
                            flat = sc[:, h % 2, :, :].rearrange("p a b -> p (a b)")
                            k.v(nc.vector.tensor_tensor(flat, flat, arg[2], ALU.mult))
                            k.v(nc.vector.tensor_reduce(den[:, h, :], sc[:, h % 2, :, :], AX, ALU.add))
                        nc.vector.reciprocal(den[:, h, :], den[:, h, :]).then_inc(k.probs_ready.up(), 1)
                    h = i - 2
                    if 0 <= h < H:
                        dve.wait_ge(k.probs_ready.sem, k.probs_ready.at(h + 1))
                        dve.wait_ge(k.heads_ready.sem, k.heads_ready.at(h + 1))
                        for tt in range(NT):
                            nc.vector.tensor_scalar(heads[h][4](tt), k.ps[:, 4 + h % 2, tt * 256:tt * 256 + dv],
                                                    den[:, h, tt:tt + 1], None,
                                                    ALU.mult).then_inc(k.heads_scaled.up(), 1)

            @block.scalar
            def _(act):
                for i in range(H + 1):
                    if i < H:
                        act.wait_ge(k.shift_ready.sem, k.shift_ready.at(i + 1))
                        for tt in range(NT):
                            nc.scalar.activation(sc[:, i % 2, tt, :], sc[:, i % 2, tt, :], ACT.Exp,
                                                 bias=top[:, i, tt:tt + 1],
                                                 accum_out=den[:, i, tt:tt + 1]).then_inc(k.exps_ready.up(), 1)
                    h = i - 1
                    if h >= 0:
                        act.wait_ge(k.probs_turned.sem, k.probs_turned.at(h + 1))
                        if h >= 2:
                            act.wait_ge(k.heads_ready.sem, k.heads_ready.at(h - 1))
                        nc.scalar.activation(pT[:, h % 2, :, :].rearrange("p a b -> p (a b)"),
                                             k.ps[:, 2 + h % 2, :], ACT.Copy).then_inc(k.turned_copied.up(), 1)

def residual(k, x, alpha, c0, width):
    def at(tt):
        def go(eng, ps):
            return k.nc.vector.scalar_tensor_tensor(out=x[:, tt, c0:c0 + width], in0=x[:, tt, c0:c0 + width],
                                                    scalar=alpha, in1=ps[:, 0:width], op0=ALU.mult, op1=ALU.add)
        return go
    return at

def project_residual(k, xT, kc, first, x, alpha):
    units = []
    for j in range(2):
        units += token_products(k, xT, kc, first + j, 512, 0, 512, None, "v", residual(k, x, alpha, 512 * j, 512))
    run_products(k, units, (first, first + 2))

def first_block_attention(k, x, tiles):
    nc, sb = k.nc, k.sb
    with ExitStack() as c:
        proj = sb("projections", [P, NT, IN_W], ctx=c)
        kv = sb("memory_kv", [P, NT, 2 * HD * H_MEM], ctx=c)
        with ExitStack() as c2:
            mem = sb("memory_rows", [P, NT, D], ctx=c2)
            xT = sb("x_T", [P, DC, S], ctx=c2)
            memT = sb("memory_T", [P, DC, S], ctx=c2)
            f = sb("row_factors", [P, 2 * NT], ctx=c2)
            y = sb("normed_rows", [P, NT, D], ctx=c2)
            load_small(k, [(x[:, :, :], k.dram["x"].rearrange("a (t p) d -> p (a t) d", p=P)),
                           (mem[:, :, :], k.dram["mem"].rearrange("a (t p) d -> p (a t) d", p=P)),
                           (k.cols_sb[:, :], k.dram["columns"]), (k.ident, k.const("ident"))])
            row_rsqrt(k, [(x[:, :, :], f[:, 0:NT]), (mem[:, :, :], f[:, NT:2 * NT])], 1e-6)
            for src, dst, at, gain in ((x, xT, 0, "g_mix"), (mem, memT, NT, "g_memtok")):
                with k.stage() as block:
                    @block.vector
                    def _(dve):
                        for tt in range(NT):
                            nc.vector.tensor_scalar(y[:, tt, :], src[:, tt, :], f[:, at + tt:at + tt + 1], None,
                                                    ALU.mult).then_inc(k.dve_step.up(), 1)
                turn(k, y, DC, dst, lambda ch, gain=gain: k.col(gain, ch))
            units = []
            for j in range(IN_W // 512):
                units += token_products(k, xT, DC, tiles["w_in"] + j, 512, 0, 512,
                                        lambda tt, j=j: proj[:, tt, 512 * j:512 * (j + 1)])
            units += token_products(k, memT, DC, tiles["w_mem_kv"], 512, 0, 512, lambda tt: kv[:, tt, :])
            run_products(k, units, (tiles["w_in"], tiles["w_mem_kv"] + 1))

        q_T = sb("queries_T", [HD, H_MIX, S], ctx=c)
        k_T = sb("keys_T", [HD, H_MIX, S], ctx=c)
        out = sb("mixed_heads", [P, NT, D], ctx=c)
        masks = sb("attention_constants", [P, 3, NT * S], ctx=c)
        gf = sb("group_factors", [P, NT, 40], ctx=c)
        load_small(k, [(masks[:, n, :], k.const(name)) for n, name in enumerate(("dist_dil", "dist_moba", "count"))])
        wd = HD * H_DIL
        jobs = []
        for tt in range(NT):
            for n, (src, c0, g) in enumerate(((proj, 0, 12), (proj, 3 * wd, 12), (proj, 6 * wd, 4), (kv, 0, 4))):
                g0 = (0, 12, 24, 28)[n]
                jobs.append((src[:, tt, c0:c0 + g * HD].rearrange("p (g w) -> p g w", g=g), gf[:, tt, g0:g0 + g]))
        row_rsqrt(k, jobs, 1e-6)
        scale_groups(k, jobs)
        units = []
        at = 0
        for dst, h0, n, src, c0, gain in ((q_T, 0, 6, proj, 0, "qg_dil"), (k_T, 0, 6, proj, wd, "kg_dil"),
                                          (q_T, 6, 6, proj, 3 * wd, "qg_moba"), (k_T, 6, 6, proj, 4 * wd, "kg_moba"),
                                          (q_T, 12, 4, proj, 6 * wd, "qg_mem"), (k_T, 12, 4, kv, 0, "kg_mem")):
            for h in range(0, n, 2):
                trs = [lambda ps, a=a, tt=tt, src=src, c0=c0, h=h:
                       nc.tensor.transpose(ps[0:HD, a * S + tt * P:a * S + (tt + 1) * P],
                                           src[:, tt, c0 + (h + a) * HD:c0 + (h + a + 1) * HD], k.ident)
                       for a in range(2) for tt in range(NT)]

                def gained(eng, ps, dst=dst, h=h0 + h, gain=gain):
                    o = dst[:, h:h + 2, :].rearrange("p a b -> p (a b)")
                    if eng is nc.scalar:
                        return eng.activation(o, ps[0:HD, :], ACT.Copy, scale=k.col(gain, 0, HD))
                    return eng.tensor_scalar(o, ps[0:HD, :], k.col(gain, 0, HD),
                                             HD ** -0.5 if dst is q_T else 1.0, ALU.mult, ALU.mult)
                units.append((None, trs, "v" if dst is q_T else "a", [gained]))
        run_products(k, units)

        heads = []
        for h in range(H_MIX):
            if h < H_DIL:
                v = lambda kt, h=h: proj[:, kt, 2 * wd + h * HD:2 * wd + (h + 1) * HD]
                kind = ("alibi", (SLOPES[2 * h], masks[:, 0, :], masks[:, 2, :]))
            elif h < H_DIL + H_MOBA:
                g = h - H_DIL
                v = lambda kt, g=g: proj[:, kt, 5 * wd + g * HD:5 * wd + (g + 1) * HD]
                kind = ("alibi", (SLOPES[2 * g + 1], masks[:, 1, :], None))
            else:
                g = h - H_DIL - H_MOBA
                v = lambda kt, g=g: kv[:, kt, (H_MEM + g) * HD:(H_MEM + g + 1) * HD]
                kind = ("plain", None)
            heads.append(([q_T[:, h, :]], [k_T[:, h, :]], v, kind,
                          lambda tt, h=h: out[:, tt, h * HD:(h + 1) * HD]))
        attention(k, heads, HD)

        jobs = [(out[:, tt, c0:c0 + n].unsqueeze(1), gf[:, tt, i:i + 1])
                for tt in range(NT) for i, (c0, n) in enumerate(((0, wd), (wd, wd), (2 * wd, D - 2 * wd)))]
        row_rsqrt(k, jobs, 1e-6)
        scale_groups(k, jobs)
        outT = sb("mixed_T", [P, DC, S], ctx=c)
        turn(k, out, DC, outT, lambda ch: k.col("og_dil", ch))
        project_residual(k, outT, DC, tiles["w_out"], x, 1.0)

def top16(k, lists):
    v = k.nc.vector
    steps = [lambda a, b, t, i: v.max(t[:, 0:8], a),
             lambda a, b, t, i: v.max_index(i[:, 0:8], t[:, 0:8], a),
             lambda a, b, t, i: v.match_replace(b, t[:, 0:8], a, -3e38),
             lambda a, b, t, i: v.max(t[:, 8:16], b),
             lambda a, b, t, i: v.max_index(i[:, 8:16], t[:, 8:16], b)]
    for step in steps:
        for item in lists:
            step(*item).then_inc(k.dve_step.up(), 1)
        v.wait_ge(k.dve_step.sem, k.dve_step.count)

def peer_routing(k, hT, tiles, slots_T):
    nc, sb = k.nc, k.sb
    with ExitStack() as c:
        qT = sb("peer_queries_T", [P, 2 * PH, S], ctx=c)
        units = []
        for j in range(4):
            for m in range(4):
                units.append(feature_products(k, hT, DC, tiles["w_peer_q"] + j, 512, m * P, P,
                                              [(qT[:, 4 * j + m, :], 0, P)], "va"[m % 2]))
        run_products(k, units, (tiles["w_peer_q"], tiles["w_peer_q"] + 4))
        sub = sb("sub_keys_T", [P, 2, PH, PK], ctx=c)
        load_small(k, [(sub[:, n, :, :], k.dram[f"subkeys_T_{n + 1}"]) for n in range(2)])
        sc = sb("sub_scores", [P, 2, NT, PH, PK], ctx=c)
        units = []
        for side in range(2):
            for tt in range(NT):
                for hh in range(0, PH, 4):
                    prods = [lambda ps, h=h, side=side, tt=tt, hh=hh:
                             mm(k, ps[:, (h - hh) * PK:(h - hh + 1) * PK], qT[:, 2 * h + side, tt * P:(tt + 1) * P],
                                sub[:, side, h, :]) for h in range(hh, hh + 4)]
                    units.append((None, prods, "va"[tt], [copy_out(
                        k, sc[:, side, tt, hh:hh + 4, :].rearrange("p a b -> p (a b)"), P, 512)]))
        run_products(k, units)

        best = sb("best_keys", [P, NT, 2, PH, TOPK], ctx=c)
        place = sb("best_places", [P, NT, 2, PH, TOPK], U32, ctx=c)
        placef = sb("best_places_float", [P, NT, 2, PH, TOPK], ctx=c)
        pair = sb("pair_sums", [P, PH, TOPK * TOPK], ctx=c)
        spare = sb("spare", [P, 2 * PH * TOPK * TOPK], ctx=c)
        ps_top = sb("pair_best", [P, NT, PH, TOPK], ctx=c)
        ps_at = sb("pair_places", [P, NT, PH, TOPK], U32, ctx=c)
        digit = sb("pair_digits", [P, 2, PH * TOPK], U32, ctx=c)
        digitf = sb("pair_digits_float", [P, 2, PH * TOPK], ctx=c)
        rows = sb("slot_rows", [P, NT, 3, PH * TOPK], ctx=c)
        iota = sb("iota_16", [P, TOPK], ctx=c)
        tot = sb("gate_sums", [P, NT * PH], ctx=c)
        load_small(k, [(iota[:, :], k.const("iota")[:, 0:TOPK])])
        G = [P, PH * TOPK, TOPK]
        with k.stage() as block:
            @block.vector
            def _(dve):
                v = nc.vector
                for tt in range(NT):
                    sp = spare[:, :].rearrange("p (s h n) -> p s h n", s=2, h=PH)
                    top16(k, [(sc[:, s, tt, h, :], sp[:, s, h, 0:PK], best[:, tt, s, h, :], place[:, tt, s, h, :])
                              for s in range(2) for h in range(PH)])
                    k.v(v.tensor_copy(placef[:, tt], place[:, tt]))
                    for h in range(PH):
                        v.tensor_tensor(pair[:, h, :].rearrange("p (a b) -> p a b", a=TOPK),
                                        best[:, tt, 0, h, :].unsqueeze(2).to_broadcast([P, TOPK, TOPK]),
                                        best[:, tt, 1, h, :].unsqueeze(1).to_broadcast([P, TOPK, TOPK]),
                                        ALU.add).then_inc(k.dve_step.up(), 1)
                    v.wait_ge(k.dve_step.sem, k.dve_step.count)
                    top16(k, [(pair[:, h, :], sp[:, 0, h, :], ps_top[:, tt, h, :], ps_at[:, tt, h, :])
                              for h in range(PH)])
                    at = ps_at[:, tt, :, :].rearrange("p h j -> p (h j)")
                    k.v(v.tensor_scalar(digit[:, 0, :], at, 4, None, ALU.logical_shift_right))
                    k.v(v.tensor_scalar(digit[:, 1, :], at, TOPK - 1, None, ALU.bitwise_and))
                    k.v(v.tensor_copy(digitf[:, :, :], digit[:, :, :]))
                    for s in range(2):
                        hot = spare[:, 0:PH * TOPK * TOPK].rearrange("p (j a) -> p j a", a=TOPK)
                        k.v(v.tensor_tensor(hot, digitf[:, s, :].unsqueeze(2).to_broadcast(G),
                                            iota[:, :].unsqueeze(1).to_broadcast(G), ALU.is_equal))
                        for h in range(PH):
                            hh = hot[:, h * TOPK:(h + 1) * TOPK, :]
                            v.tensor_tensor(hh, hh, placef[:, tt, s, h, :].unsqueeze(1).to_broadcast([P, TOPK, TOPK]),
                                            ALU.mult).then_inc(k.dve_step.up(), 1)
                        v.wait_ge(k.dve_step.sem, k.dve_step.count)
                        k.v(v.tensor_reduce(rows[:, tt, s, :], hot, AX, ALU.add))
                    v.tensor_tensor(rows[:, tt, 2, :].rearrange("p (h j) -> p h j", h=PH), ps_top[:, tt, :, :],
                                    ps_top[:, tt, :, 0:1].to_broadcast([P, PH, TOPK]),
                                    ALU.subtract).then_inc(k.shift_ready.up(), 1)
                for tt in range(NT):
                    dve.wait_ge(k.exps_ready.sem, k.exps_ready.at(tt + 1))
                    e = rows[:, tt, 2, :].rearrange("p (h j) -> p h j", h=PH)
                    t = tot[:, tt * PH:(tt + 1) * PH]
                    k.v(v.tensor_reduce(t, e, AX, ALU.add))
                    k.v(v.reciprocal(t, t))
                    k.v(v.tensor_tensor(e, e, t.unsqueeze(2).to_broadcast([P, PH, TOPK]), ALU.mult))

            @block.scalar
            def _(act):
                for tt in range(NT):
                    act.wait_ge(k.shift_ready.sem, k.shift_ready.at(tt + 1))
                    nc.scalar.activation(rows[:, tt, 2, :], rows[:, tt, 2, :],
                                         ACT.Exp).then_inc(k.exps_ready.up(), 1)
        units = []
        for n in range(3):
            trs = [lambda ps, n=n, tt=tt: nc.tensor.transpose(ps[:, tt * P:(tt + 1) * P], rows[:, tt, n, :], k.ident)
                   for tt in range(NT)]
            units.append((None, trs, "va"[n % 2], [copy_out(k, slots_T[:, n, :], P, S)]))
        run_products(k, units)

def peer_gates(k, slots_T, gates):
    nc = k.nc
    GRP = 4
    with ExitStack() as c:
        hot = k.sb("one_hots", [P, 2, 2, GRP, P], ctx=c)
        iota = k.sb("iota_keys", [P, PK], ctx=c)
        load_small(k, [(iota[:, :], k.const("iota")[:, 0:PK])])
        steps = S // GRP

        with k.stage() as block:
            def hots(dve, g, b, wait):
                if wait:
                    dve.wait_ge(k.products.sem, k.products.at(g - 1))
                for t in range(GRP):
                    tok = g * GRP + t
                    nc.vector.tensor_scalar(hot[:, b, 0, t, :], iota[:, :], slots_T[:, 0, bass.ds(tok, 1)], None,
                                            ALU.is_equal)
                    ins = nc.vector.tensor_scalar(hot[:, b, 1, t, :], iota[:, :], slots_T[:, 1, bass.ds(tok, 1)],
                                                  slots_T[:, 2, bass.ds(tok, 1)], ALU.is_equal, ALU.mult)
                ins.then_inc(k.onehots_ready.up(), 1)

            def outer(pe, g, b, wait):
                pe.wait_ge(k.onehots_ready.sem, k.onehots_ready.at(g + 1))
                if wait:
                    pe.wait_ge(k.gates_placed.sem, k.gates_placed.at(g - 1))
                for t in range(GRP):
                    last = mm(k, k.ps[:, b, t * P:(t + 1) * P], hot[:, b, 0, t, :], hot[:, b, 1, t, :])
                last.then_inc(k.products.up(), 1)

            def place(act, g, b):
                act.wait_ge(k.products.sem, k.products.at(g + 1))
                nc.scalar.activation(gates[:, :, bass.ds(g * GRP, GRP)],
                                     k.ps[:, b, :].rearrange("p (t n) -> p n t", t=GRP),
                                     ACT.Copy).then_inc(k.gates_placed.up(), 1)

            @block.vector
            def _(dve):
                for b in range(2):
                    hots(dve, b, b, False)
                with dve.Fori(1, steps // 2) as i:
                    for b in range(2):
                        hots(dve, 2 * i + b, b, True)
                k.onehots_ready.repeated(steps // 2 - 1, 2)

            @block.tensor
            def _(pe):
                for b in range(2):
                    outer(pe, b, b, False)
                with pe.Fori(1, steps // 2) as i:
                    for b in range(2):
                        outer(pe, 2 * i + b, b, True)
                k.products.repeated(steps // 2 - 1, 2)

            @block.scalar
            def _(act):
                with act.Fori(0, steps // 2) as i:
                    for b in range(2):
                        place(act, 2 * i + b, b)
                k.gates_placed.repeated(steps // 2, 2)

def peer_experts(k, hT, gates, first):
    nc = k.nc
    with ExitStack() as c:
        act_sb = k.sb("gelu_out", [P, 2, S], ctx=c)
        w_sb = k.sb("gated", [P, 2, S], ctx=c)
        loops = PK // 8

        def halves(j):
            tile = k.ring[:, (first + j // 2) % SLOTS, :]
            return (tile[:, (j % 2) * 1024:(j % 2 + 1) * 1024].rearrange("p (c e) -> p c e", c=DC),
                    tile[:, 2048 + (j % 2) * 1024:2048 + (j % 2 + 1) * 1024])

        with k.stage() as block:
            def pre(pe, i, j, start):
                n = 8 * i + j
                tile = first + j // 2
                if j % 2 == 0:
                    pe.wait_ge(k.stream.landed[tile % SLOTS].sem, 16 * (tile // SLOTS + 1) + 16 * i)
                if not start:
                    pe.wait_ge(k.act_ready.sem, k.act_ready.at(n - 3))
                u, _ = halves(j)
                for ch in range(DC):
                    last = mm(k, k.ps[:, 4 + j % 4, 0:S], u[:, ch, :], hT[:, ch, :], ch == 0, ch == DC - 1)
                last.then_inc(k.products.up(), 1)

            def post(pe, i, j, first_one, last_one):
                n = 8 * i + j
                pe.wait_ge(k.weights_gated.sem, k.weights_gated.at(n + 1))
                _, vv = halves(j)
                for tt in range(NT):
                    for half in range(2):
                        last = mm(k, k.ps[:, 2 * tt + half, :], w_sb[:, j % 2, tt * P:(tt + 1) * P],
                                  vv[:, half * 512:(half + 1) * 512], first_one, last_one)
                last.then_inc(k.down_products.up(), 1)

            def pe_turn(pe, i, first_turn, last_turn):
                for j in range(8):
                    if j < 7:
                        pre(pe, i, j + 1, first_turn and j + 1 < 4)
                    elif not last_turn:
                        pre(pe, i + 1, 0, False)
                    post(pe, i, j, first_turn and j == 0, last_turn and j == 7)

            def act_turn(act, i, first_turn):
                for j in range(8):
                    n = 8 * i + j
                    act.wait_ge(k.products.sem, k.products.at(n + 1))
                    if not (first_turn and j < 2):
                        act.wait_ge(k.weights_gated.sem, k.weights_gated.at(n - 1))
                    nc.scalar.activation(act_sb[:, j % 2, :], k.ps[:, 4 + j % 4, 0:S],
                                         ACT.Gelu).then_inc(k.act_ready.up(), 1)

            def dve_turn(dve, i, first_turn):
                for j in range(8):
                    n = 8 * i + j
                    dve.wait_ge(k.act_ready.sem, k.act_ready.at(n + 1))
                    if not (first_turn and j < 2):
                        dve.wait_ge(k.down_products.sem, k.down_products.at(n - 1))
                    g = gates[:, bass.ds(n, 1), :].rearrange("p a t -> p (a t)")
                    nc.vector.tensor_tensor(w_sb[:, j % 2, :], act_sb[:, j % 2, :], g,
                                            ALU.mult).then_inc(k.weights_gated.up(), 1)

            @block.sync
            def _(sp):
                def reload(i, j):
                    sp.wait_ge(k.down_products.sem, k.down_products.at(8 * i + 2 * j + 2))
                    slot = (first + j) % SLOTS
                    sp.dma_start(k.ring[:, slot, :].unsqueeze(1),
                                 k.dram["peer_uv"][bass.ds(4 * i + 4 + j, 1)].rearrange("a p n -> p a n")
                                 ).then_inc(k.stream.landed[slot].sem, 16)
                with sp.Fori(0, loops - 1) as i:
                    for j in range(4):
                        reload(i, j)
                k.stream.issued += 4 * (loops - 1)
                for j in range(4):
                    sp.wait_ge(k.down_products.sem, k.down_products.at(8 * (loops - 1) + 2 * j + 2))
                    k.stream.load(sp, k.stream.issued)
                    k.stream.issued += 1

            @block.tensor
            def _(pe):
                pre(pe, 0, 0, True)
                pe_turn(pe, 0, True, False)
                with pe.Fori(1, loops - 1) as i:
                    pe_turn(pe, i, False, False)
                k.products.repeated(loops - 2, 8)
                k.down_products.repeated(loops - 2, 8)
                pe_turn(pe, loops - 1, False, True)

            @block.scalar
            def _(act):
                act_turn(act, 0, True)
                with act.Fori(1, loops) as i:
                    act_turn(act, i, False)
                k.act_ready.repeated(loops - 1, 8)

            @block.vector
            def _(dve):
                dve_turn(dve, 0, True)
                with dve.Fori(1, loops) as i:
                    dve_turn(dve, i, False)
                k.weights_gated.repeated(loops - 1, 8)

def first_block(k, tiles):
    nc, sb = k.nc, k.sb
    keep, hT_keep = k.dram["x_rows"], k.dram["h_T"]
    with ExitStack() as c:
        x = sb("x", [P, NT, D], ctx=c)
        first_block_attention(k, x, tiles)
        hT = sb("peer_input_T", [P, DC, S], ctx=c)
        f = sb("x_factors", [P, NT], ctx=c)
        with ExitStack() as c2:
            y = sb("normed_x", [P, NT, D], ctx=c2)
            row_rsqrt(k, [(x[:, :, :], f[:, :])], 1e-6)
            with k.stage() as block:
                @block.vector
                def _(dve):
                    for tt in range(NT):
                        nc.vector.tensor_scalar(y[:, tt, :], x[:, tt, :], f[:, tt:tt + 1], None,
                                                ALU.mult).then_inc(k.dve_step.up(), 1)
            turn(k, y, DC, hT, lambda ch: k.col("g_ffn", ch))
        store(k, [(keep, x[:, :, :]), (hT_keep, hT[:, :, :])])
        slots_T = sb("slots_T", [P, 3, S], ctx=c)
        peer_routing(k, hT, tiles, slots_T)
        store(k, [(k.dram["slots"], slots_T[:, :, :])])
    with ExitStack() as c:
        gates = sb("gates", [P, PK, S], ctx=c)
        with ExitStack() as c2:
            slots_T = sb("slots_T_again", [P, 3, S], ctx=c2)
            load_small(k, [(slots_T[:, :, :], k.dram["slots"])])
            peer_gates(k, slots_T, gates)
        hT = sb("peer_input_T_again", [P, DC, S], ctx=c)
        load_small(k, [(hT[:, :, :], hT_keep)])
        peer_experts(k, hT, gates, tiles["peer"])

def store(k, pairs):
    with k.stage() as block:
        @block.scalar
        def _(act):
            for dst, src in pairs:
                act.dma_start(dst, src).then_inc(k.rows_stored.up(16), 16)
            act.wait_ge(k.rows_stored.sem, k.rows_stored.at(16 * len(pairs)))

def rwkv_and_gating(k, tiles, hT, cat_T):
    nc, sb = k.nc, k.sb
    W = RW_H * S
    with ExitStack() as c:
        AR = sb("rw_A_R", [64, RW_H, NCH, 2, CH], ctx=c)
        Bt = sb("rw_B_then_T", [64, W], ctx=c)
        Kt = sb("rw_K_then_T_T", [64, W], ctx=c)
        VN = sb("rw_V_rows", [64, NCH, RW_H, 64], ctx=c)
        sgl = sb("rw_gate_low", [P, S], ctx=c)
        decay_end = sb("rw_chunk_decay", [64, RW_H, NCH], ctx=c)
        bonus = sb("rw_bonus", [64, NCH * RW_H], ctx=c)
        pu = sb("sg_u", [P, NT, 512], ctx=c)
        pv = sb("sg_v", [P, NT, 512], ctx=c)
        hv = lambda t: t.rearrange("p (h t) -> p h t", h=RW_H)
        with ExitStack() as c2:
            r, kx, vx, ax, lw, cum, ex = (sb(n, [64, W], ctx=c2)[:, :] for n in
                                          ("rw_r", "rw_k", "rw_v", "rw_a", "rw_log_decay", "rw_cum", "rw_exp"))
            lora = sb("rw_lora", [64, 2, S], ctx=c2)
            low = sb("rw_lora_up", [64, 2, 512], ctx=c2)
            units = []
            t0 = tiles["ab_in"]
            for j, dst in enumerate((r, kx, vx)):
                for m in range(4):
                    d = hv(dst)
                    units.append(feature_products(k, hT, DC, t0 + j, 512, m * P, P,
                                                  [(d[:, 2 * m, :], 0, 64), (d[:, 2 * m + 1, :], 64, 64)],
                                                  "va"[m % 2]))
            units.append(feature_products(k, hT, DC, t0 + 3, 256, 0, P,
                                          [(lora[:, 0, :], 0, 64), (lora[:, 1, :], 64, 64)], "v"))
            units.append(feature_products(k, hT, DC, t0 + 3, 256, P, P, [(sgl[:, :], 0, P)], "a"))
            for j, dst in enumerate((pu, pv)):
                units += token_products(k, hT, DC, t0 + 4 + j, 512, 0, 512, lambda tt, dst=dst: dst[:, tt, :])
            run_products(k, units, (t0, t0 + 6))

            with k.stage() as block:
                @block.vector
                def _(dve):
                    v = nc.vector

                    def shift(dst, g, rows, mus):
                        d = dst.rearrange("p (g t) -> p g t", g=g)
                        e = (sg_tmp if rows == P else ex)[0:rows, 0:g * S].rearrange("p (g t) -> p g t", g=g)
                        k.v(v.tensor_tensor(e[:, :, 1:S], d[:, :, 0:S - 1], d[:, :, 1:S], ALU.subtract))
                        k.v(v.tensor_scalar(e[:, :, 0:1], d[:, :, 0:1], -1.0, None, ALU.mult))
                        for i in range(g):
                            v.scalar_tensor_tensor(out=d[:, i, :], in0=e[:, i, :], scalar=mus(i), in1=d[:, i, :],
                                                   op0=ALU.mult, op1=ALU.add).then_inc(k.dve_step.up(), 1)
                        v.wait_ge(k.dve_step.sem, k.dve_step.count)
                    sg_tmp = cat_T[:, 0, :]
                    for n, dst in enumerate((r, kx, vx)):
                        shift(dst, RW_H, 64, lambda i, n=n: k.col("mu_rkv", 8 * n + i, 64))
                    shift(lora[:, :, :].rearrange("p a t -> p (a t)"), 2, 64, lambda i: k.col("mu_rkv", 24 + i, 64))
                    shift(sgl[:, :], 1, P, lambda i: k.col("mu_g", 13))

                @block.scalar
                def _(act):
                    act.dma_start(low[:, 0, :], k.dram["rw_w2_2"].rearrange("a p n -> (a p) n")
                                  ).then_inc(k.small_loaded.up(16), 16)
                    act.dma_start(low[:, 1, :], k.dram["rw_a2_2"].rearrange("a p n -> (a p) n")
                                  ).then_inc(k.small_loaded.up(16), 16)
                    act.wait_ge(k.small_loaded.sem, k.small_loaded.at(32))
                    act.wait_ge(k.dve_step.sem, k.dve_step.count)
                    nc.scalar.activation(lora[:, 0, :], lora[:, 0, :], ACT.Tanh).then_inc(k.act_step.up(), 1)
                    nc.scalar.activation(sgl[:, :], sgl[:, :], ACT.Sigmoid).then_inc(k.act_step.up(), 1)

            def squashed(dst, h, name):
                def go(eng, ps):
                    return nc.scalar.activation(hv(dst)[:, h, :], ps[0:64, 0:S], ACT.Sigmoid,
                                                bias=k.col(name, h, 64))
                return go
            units = []
            for n, (dst, name) in enumerate(((lw, "w0"), (ax, "a0"))):
                for h in range(RW_H):
                    units.append((None, [lambda ps, n=n, h=h: mm(k, ps[0:64, 0:S], low[:, n, h * 64:(h + 1) * 64],
                                                                 lora[:, n, :])], "a", [squashed(dst, h, name)]))
            run_products(k, units)

            with ExitStack() as c3:
                reset = sb("rw_chunk_resets", [64, W], ctx=c3)
                load_small(k, [(reset[:, :], k.const("reset", 64))])
                with k.stage() as block:
                    @block.vector
                    def _(dve):
                        v = nc.vector
                        k.v(v.tensor_scalar(lw, lw, -math.exp(-0.5), None, ALU.mult))
                        k.v(v.tensor_tensor_scan(cum, reset[:, :], lw, 0.0, ALU.mult, ALU.add))
                        for h in range(RW_H):
                            v.tensor_scalar(hv(ex)[:, h, :], hv(kx)[:, h, :], k.col("k_k", h, 64), None,
                                            ALU.mult).then_inc(k.dve_step.up(), 1)
                        v.wait_ge(k.dve_step.sem, k.dve_step.count)
                        k.v(v.tensor_tensor(reset[:, :], ex, ex, ALU.mult))
                ones = sb("rw_ones", [64, 64], ctx=c3)
                load_small(k, [(ones[:, :], k.const("ones", 64)[:, 0:64])])
                run_products(k, [(None, [lambda ps, n=n: mm(k, ps[0:64, :], ones[:, :],
                                                            reset[:, n * 512:(n + 1) * 512])], "a",
                                  [lambda eng, ps, n=n: nc.scalar.activation(Bt[:, n * 512:(n + 1) * 512],
                                                                             ps[0:64, :], ACT.Sqrt)])
                                 for n in range(W // 512)])
                with k.stage() as block:
                    @block.vector
                    def _(dve):
                        v = nc.vector
                        k.v(v.tensor_scalar(Bt[:, :], Bt[:, :], 1e-12, None, ALU.max))
                        k.v(v.reciprocal(Bt[:, :], Bt[:, :]))
                        k.v(v.tensor_tensor(ex, ex, Bt[:, :], ALU.mult))
                        for h in range(RW_H):
                            v.tensor_scalar(hv(reset[:, :])[:, h, :], hv(ax)[:, h, :], 1.0, k.col("k_a", h, 64),
                                            ALU.subtract, ALU.mult).then_inc(k.dve_step.up(), 1)
                        v.wait_ge(k.dve_step.sem, k.dve_step.count)
                        k.v(v.scalar_tensor_tensor(out=kx, in0=reset[:, :], scalar=1.0, in1=kx,
                                                   op0=ALU.add, op1=ALU.mult))
                        k.v(v.tensor_tensor(reset[:, :], r, kx, ALU.mult))
                        v.tensor_tensor(lw, cum, lw, ALU.subtract).then_inc(k.shift_ready.up(), 1)
                        k.v(v.tensor_tensor(ax, ax, ex, ALU.mult))
                        dve.wait_ge(k.exps_ready.sem, k.exps_ready.at(1))
                        part = lambda i: AR[:, :, :, i, :].rearrange("p h c t -> p (h c) t")
                        ch = lambda t: t.rearrange("p (g t) -> p g t", t=CH)
                        k.v(v.scalar_tensor_tensor(out=part(0), in0=ch(ex), scalar=-1.0, in1=ch(lw),
                                                   op0=ALU.mult, op1=ALU.mult))
                        dve.wait_ge(k.exps_ready.sem, k.exps_ready.at(2))
                        k.v(v.tensor_tensor(Bt[:, :], ax, Kt[:, :], ALU.mult))
                        k.v(v.tensor_tensor(Kt[:, :], kx, Kt[:, :], ALU.mult))
                        dve.wait_ge(k.exps_ready.sem, k.exps_ready.at(3))
                        k.v(v.tensor_tensor(part(1), ch(r), ch(cum), ALU.mult))
                        k.v(v.tensor_copy(decay_end[:, :, :].rearrange("p h c -> p (h c)"),
                                          ch(cum)[:, :, CH - 1]))

                    @block.scalar
                    def _(act):
                        act.wait_ge(k.shift_ready.sem, k.shift_ready.at(1))
                        for out, src, s in ((lw, lw, 1.0), (Kt[:, :], cum, -1.0), (cum, cum, 1.0)):
                            nc.scalar.activation(out, src, ACT.Exp, scale=s).then_inc(k.exps_ready.up(), 1)
                units = []
                for n in range(2):
                    units.append((None, [lambda ps, i=i, n=n: mm(
                        k, ps[0:64, i:i + 1], hv(reset[:, :])[:, (16 * n + i) % RW_H,
                                                             (16 * n + i) // RW_H * CH:((16 * n + i) // RW_H + 1) * CH],
                        k.col("r_k", (16 * n + i) % RW_H, 64)) for i in range(16)], "v",
                        [copy_out(k, bonus[:, 16 * n:16 * n + 16], 64, 16)]))
                units += chunk_rows(k, vx, VN)
                run_products(k, units)

        with ExitStack() as c2:
            rows = sb("sg_norm_rows", [P, 2, 512], ctx=c2)
            wT = sb("sg_weights_T", [P, SG, P], ctx=c2)
            stt = sb("sg_sums", [P, NT * SG], ctx=c2)
            var = sb("sg_vars", [P, NT * SG], ctx=c2)
            sq = sb("sg_squares", [P, NT * SG, P], ctx=c2)
            z = pv[:, :, :].rearrange("p t (g n) -> p (t g) n", g=SG)
            bc = lambda t: t.unsqueeze(2).to_broadcast([P, NT * SG, P])
            with k.stage() as block:
                @block.scalar
                def _(act):
                    act.dma_start(rows[:, 0, :], k.dram["sg_ln_g_2"].rearrange("a g n -> (a g n)")
                                  .partition_broadcast(P)).then_inc(k.small_loaded.up(16), 16)
                    act.dma_start(rows[:, 1, :], k.dram["sg_ln_b_2"].rearrange("a g n -> (a g n)")
                                  .partition_broadcast(P)).then_inc(k.small_loaded.up(16), 16)
                    act.dma_start(wT[:, :, :], k.dram["sg_ws_T"]).then_inc(k.small_loaded.up(16), 16)
                    for t in (pv, pu):
                        nc.scalar.activation(t[:, :, :], t[:, :, :], ACT.Gelu_apprx_tanh
                                             ).then_inc(k.act_step.up(), 1)
                    act.wait_ge(k.shift_ready.sem, k.shift_ready.at(1))
                    nc.scalar.activation(var[:, :], var[:, :], ACT.Sqrt).then_inc(k.act_step.up(), 1)

                @block.gpsimd
                def _(pool):
                    pool.wait_ge(k.small_loaded.sem, k.small_loaded.at(48))
                    nc.gpsimd.affine_select(out=wT[:, :, :], in_=wT[:, :, :], pattern=[[0, SG], [1, P]],
                                            compare_op=ALU.is_ge, fill=0.0, base=0, channel_multiplier=-1
                                            ).then_inc(k.gated_ready.up(), 1)
                    pool.wait_ge(k.gated_ready.sem, k.gated_ready.at(1))

                @block.vector
                def _(dve):
                    v = nc.vector
                    dve.wait_ge(k.act_step.sem, k.act_step.at(2))
                    k.v(v.tensor_reduce(stt[:, :], z, AX, ALU.add))
                    k.v(v.tensor_scalar(stt[:, :], stt[:, :], 1.0 / P, None, ALU.mult))
                    k.v(v.tensor_tensor(z, z, bc(stt[:, :]), ALU.subtract))
                    k.v(v.tensor_tensor(sq[:, :, :], z, z, ALU.mult))
                    k.v(v.tensor_reduce(var[:, :], sq[:, :, :], AX, ALU.add))
                    v.tensor_scalar(var[:, :], var[:, :], 1.0 / P, 1e-5, ALU.mult,
                                    ALU.add).then_inc(k.shift_ready.up(), 1)
                    dve.wait_ge(k.small_loaded.sem, k.small_loaded.at(48))
                    dve.wait_ge(k.act_step.sem, k.act_step.at(3))
                    k.v(v.reciprocal(var[:, :], var[:, :]))
                    k.v(v.tensor_tensor(z, z, bc(var[:, :]), ALU.mult))
                    for tt in range(NT):
                        k.v(v.tensor_tensor(pv[:, tt, :], pv[:, tt, :], rows[:, 0, :], ALU.mult))
                        k.v(v.tensor_tensor(pv[:, tt, :], pv[:, tt, :], rows[:, 1, :], ALU.add))
            units = []
            for tt in range(NT):
                def gate(g, tt=tt):
                    def go(eng, ps):
                        col = slice(g * P, (g + 1) * P)
                        return nc.vector.scalar_tensor_tensor(out=pu[:, tt, col], in0=ps[:, col],
                                                              scalar=k.col("sg_b", g), in1=pu[:, tt, col],
                                                              op0=ALU.add, op1=ALU.mult)
                    return go
                units.append((None, [lambda ps, g=g, tt=tt: mm(k, ps[:, g * P:(g + 1) * P], wT[:, g, :],
                                                               pv[:, tt, g * P:(g + 1) * P]) for g in range(SG)],
                              "v", [gate(g) for g in range(SG)]))
            run_products(k, units)
        turn(k, pu, 4, cat_T[:, 4:8, :])

        BN = sb("rw_B_rows", [64, NCH, RW_H, 64], ctx=c)
        KN = sb("rw_K_rows", [64, NCH, RW_H, 64], ctx=c)
        LB = sb("rw_lower_B", [64, NCH * RW_H, 2 * CH], ctx=c)
        LK = sb("rw_lower_K", [64, NCH * RW_H, 2 * CH], ctx=c)
        X = sb("rw_level_product", [64, W], ctx=c)
        Lm = sb("rw_level_part", [64, W], ctx=c)
        lv = sb("rw_levels", [64, 6, CH], ctx=c)
        tri = sb("rw_triangles", [64, 2 * CH], ctx=c)
        load_small(k, [(lv[:, :, :].rearrange("p a b -> p (a b)"), k.const("levels", 64)), (tri[:, :], k.const("tri", 64))])
        units = chunk_rows(k, Bt[:, :], BN) + chunk_rows(k, Kt[:, :], KN)
        for src, dst in ((Bt, LB), (Kt, LK)):
            for g in range(8):
                def masked(eng, ps, dst=dst, g=g):
                    return nc.vector.tensor_tensor(dst[:, 4 * g:4 * g + 4, :],
                                                   ps[0:64, :].rearrange("p (a b) -> p a b", a=4),
                                                   tri[:, :].unsqueeze(1).to_broadcast([64, 4, 2 * CH]), ALU.mult)
                def prod(ps, a, src=src, g=g):
                    ci, h = divmod(4 * g + a, RW_H)
                    return mm(k, ps[0:64, a * P:(a + 1) * P], hv(src[:, :])[:, h, ci * CH:(ci + 1) * CH],
                              AR[:, h, ci, :, :].rearrange("p a t -> p (a t)"))
                units.append((None, [lambda ps, a=a, prod=prod: prod(ps, a) for a in range(4)], "v", [masked]))
        run_products(k, units)

        T, TT = Bt, Kt
        pairs = NCH * RW_H
        q = lambda t: t[:, :].rearrange("p (g n) -> p g n", g=pairs)
        with k.stage() as block:
            @block.vector
            def _(dve):
                v = nc.vector
                eye = k.ident[0:64, 0:64].unsqueeze(1).to_broadcast([64, pairs, 64])
                v.tensor_copy(q(T), eye).then_inc(k.dve_step.up(), 1)
                v.tensor_copy(q(TT), eye).then_inc(k.dve_step.up(), 1)
        for level in range(6):
            with k.stage() as block:
                @block.vector
                def _(dve):
                    nc.vector.tensor_tensor(q(Lm), LB[:, :, 0:CH],
                                            lv[:, level, :].unsqueeze(1).to_broadcast([64, pairs, CH]),
                                            ALU.mult).then_inc(k.dve_step.up(), 1)
            run_products(k, [(None, [lambda ps, i=i, g=g: mm(k, ps[0:64, i * 64:(i + 1) * 64], q(Lm)[:, 8 * g + i, :],
                                                             q(T)[:, 8 * g + i, :]) for i in range(8)], "va"[g % 2],
                              [copy_out(k, X[:, g * 512:(g + 1) * 512], 64, 512)]) for g in range(4)])

            def added(dst, g):
                def go(eng, ps):
                    d = dst[:, g * 512:(g + 1) * 512]
                    return nc.vector.tensor_tensor(d, d, ps[0:64, :], ALU.add)
                return go
            units = []
            for g in range(4):
                units.append((None, [lambda ps, i=i, g=g: mm(k, ps[0:64, i * 64:(i + 1) * 64], q(X)[:, 8 * g + i, :],
                                                             q(TT)[:, 8 * g + i, :]) for i in range(8)], "v", []))
                units.append((None, [lambda ps, i=i, g=g: mm(k, ps[0:64, i * 64:(i + 1) * 64], q(TT)[:, 8 * g + i, :],
                                                             q(X)[:, 8 * g + i, :]) for i in range(8)], "v",
                              [lambda eng, ps, g=g: added(T, g)(eng, ps),
                               lambda eng, ps, g=g: added(TT, g)(eng, k.ps[:, 2 * g, :])]))
            run_products(k, units)

        gn = sb("rw_gn_rows", [64, 2, 512], ctx=c)
        Y = sb("rw_y", [64, NCH, RW_H, 64], ctx=c)
        U = sb("rw_U", [64, 512], ctx=c)
        SA = sb("rw_SA", [64, 512], ctx=c)
        ST = sb("rw_state_T", [64, RW_H, 64], ctx=c)
        hs = lambda h: slice(h * 64, (h + 1) * 64)
        with k.stage() as block:
            @block.tensor
            def _(pe):
                for ci in range(NCH):
                    A = lambda h: AR[:, h, ci, 0, :]
                    R = lambda h: AR[:, h, ci, 1, :]
                    if ci:
                        pe.wait_ge(k.hidden_ready.sem, k.hidden_ready.at(2 * ci))
                    for h in range(RW_H):
                        if ci:
                            mm(k, k.ps[0:64, 0, hs(h)], A(h), ST[:, h, :], True, False)
                        last = mm(k, k.ps[0:64, 0, hs(h)], LK[:, ci * RW_H + h, 0:CH], VN[:, ci, h, :], not ci, True)
                    last.then_inc(k.products.up(), 1)
                    pe.wait_ge(k.act_ready.sem, k.act_ready.at(3 * ci + 1))
                    for h in range(RW_H):
                        last = mm(k, k.ps[0:64, 1, hs(h)], q(TT)[:, ci * RW_H + h, :], U[:, hs(h)])
                    last.then_inc(k.products.up(), 1)
                    pe.wait_ge(k.act_ready.sem, k.act_ready.at(3 * ci + 2))
                    for h in range(RW_H):
                        mm(k, k.ps[0:64, 2, hs(h)], BN[:, ci, h, :], SA[:, hs(h)], True, False)
                        last = mm(k, k.ps[0:64, 2, hs(h)], KN[:, ci, h, :], VN[:, ci, h, :], False, True)
                    last.then_inc(k.products.up(), 1)
                    for h in range(RW_H):
                        if ci:
                            mm(k, k.ps[0:64, 3, hs(h)], R(h), ST[:, h, :], True, False)
                        mm(k, k.ps[0:64, 3, hs(h)], LB[:, ci * RW_H + h, CH:2 * CH], SA[:, hs(h)], not ci, False)
                        last = mm(k, k.ps[0:64, 3, hs(h)], LK[:, ci * RW_H + h, CH:2 * CH], VN[:, ci, h, :], False, True)
                    last.then_inc(k.products.up(), 1)

            @block.scalar
            def _(act):
                act.dma_start(gn[:, 0, :], k.dram["rw_gn_g_2"].rearrange("a n -> (a n)").partition_broadcast(64)
                              ).then_inc(k.small_loaded.up(16), 16)
                act.dma_start(gn[:, 1, :], k.dram["rw_gn_b_2"].rearrange("a n -> (a n)").partition_broadcast(64)
                              ).then_inc(k.small_loaded.up(16), 16)
                act.wait_ge(k.small_loaded.sem, k.small_loaded.at(32))
                for ci in range(NCH):
                    for n, dst in enumerate((U[:, :], SA[:, :], Y[:, ci, :, :].rearrange("p h n -> p (h n)"))):
                        bank = (0, 1, 3)[n]
                        act.wait_ge(k.products.sem, k.products.at(4 * ci + (1, 2, 4)[n]))
                        nc.scalar.activation(dst, k.ps[0:64, bank, :], ACT.Copy).then_inc(k.act_ready.up(), 1)

            @block.vector
            def _(dve):
                v = nc.vector
                for ci in range(NCH):
                    flat = ST[:, :, :].rearrange("p h n -> p (h n)")
                    dve.wait_ge(k.products.sem, k.products.at(4 * ci + 4))
                    if ci:
                        v.tensor_tensor(flat, flat, k.ps[0:64, 2, :], ALU.add).then_inc(k.hidden_ready.up(), 1)
                    else:
                        v.tensor_copy(flat, k.ps[0:64, 2, :]).then_inc(k.hidden_ready.up(), 1)
                    v.wait_ge(k.hidden_ready.sem, k.hidden_ready.at(2 * ci + 1))
                    dve.wait_ge(k.act_ready.sem, k.act_ready.at(3 * ci + 3))
                    v.tensor_tensor(ST[:, :, :], ST[:, :, :], decay_end[:, :, ci:ci + 1].to_broadcast([64, RW_H, 64]),
                                    ALU.mult).then_inc(k.hidden_ready.up(), 1)

        with ExitStack() as c2:
            g2 = pu[:, 0, :]
            load_small(k, [(g2, k.dram["rw_g2_2"].rearrange("a p n -> (a p) n"))])
            mean = sb("rw_means", [64, pairs], ctx=c2)
            var = sb("rw_vars", [64, pairs], ctx=c2)
            y3 = Y[:, :, :, :].rearrange("p c h n -> p (c h) n")
            sq = q(X)
            bc = lambda t: t.unsqueeze(2).to_broadcast([64, pairs, 64])
            with k.stage() as block:
                @block.vector
                def _(dve):
                    v = nc.vector
                    k.v(v.tensor_reduce(mean[:, :], y3, AX, ALU.add))
                    k.v(v.tensor_scalar(mean[:, :], mean[:, :], 1.0 / RW_N, None, ALU.mult))
                    k.v(v.tensor_tensor(y3, y3, bc(mean[:, :]), ALU.subtract))
                    k.v(v.tensor_tensor(sq, y3, y3, ALU.mult))
                    k.v(v.tensor_reduce(var[:, :], sq, AX, ALU.add))
                    v.tensor_scalar(var[:, :], var[:, :], 1.0 / RW_N, 64e-5, ALU.mult,
                                    ALU.add).then_inc(k.shift_ready.up(), 1)
                    dve.wait_ge(k.act_step.sem, k.act_step.at(1))
                    k.v(v.reciprocal(var[:, :], var[:, :]))
                    k.v(v.tensor_tensor(y3, y3, bc(var[:, :]), ALU.mult))
                    yc = Y[:, :, :, :].rearrange("p c h n -> p c (h n)")
                    row = lambda n: gn[:, n, :].unsqueeze(1).to_broadcast([64, NCH, 512])
                    k.v(v.tensor_tensor(yc, yc, row(0), ALU.mult))
                    k.v(v.tensor_tensor(yc, yc, row(1), ALU.add))
                    k.v(v.tensor_tensor(sq, VN[:, :, :, :].rearrange("p c h n -> p (c h) n"), bc(bonus[:, :]),
                                        ALU.mult))
                    k.v(v.tensor_tensor(y3, y3, sq, ALU.add))

                @block.scalar
                def _(act):
                    act.wait_ge(k.shift_ready.sem, k.shift_ready.at(1))
                    nc.scalar.activation(var[:, :], var[:, :], ACT.Sqrt).then_inc(k.act_step.up(), 1)

            def gated(ci):
                def go(eng, ps):
                    y = Y[:, ci, :, :].rearrange("p h n -> p (h n)")
                    return nc.vector.tensor_tensor(y, y, ps[0:64, :], ALU.mult)
                return go
            run_products(k, [(None, [lambda ps, ci=ci: mm(k, ps[0:64, :], sgl[:, ci * CH:(ci + 1) * CH], g2)],
                              "v", [gated(ci)]) for ci in range(NCH)])
            turn(k, Y[:, :, :, :].rearrange("p c h n -> p c (h n)"), 4, cat_T, None, CH, NCH)

def chunk_rows(k, src, dst):
    units = []
    for ci in range(NCH):
        trs = [lambda ps, h=h, ci=ci: k.nc.tensor.transpose(
            ps[0:64, h * 64:(h + 1) * 64], src[:, h * S + ci * CH:h * S + (ci + 1) * CH],
            k.ident[0:64, 0:64]) for h in range(RW_H)]
        units.append((None, trs, "va"[ci % 2],
                      [copy_out(k, dst[:, ci, :, :].rearrange("p h n -> p (h n)"), 64, 512)]))
    return units

def mla(k, x, hT, tiles):
    nc, sb = k.nc, k.sb
    with ExitStack() as c:
        q_T = sb("mla_q_T", [MLA_QK, MLA_H, S], ctx=c)
        k_T = sb("mla_k_T", [MLA_QK, MLA_H, S], ctx=c)
        kv = sb("mla_kv", [P, NT, 2048], ctx=c)
        with ExitStack() as c2:
            p = sb("mla_p", [P, NT, 544], ctx=c2)
            low_T = sb("mla_low_T", [P, 4, S], ctx=c2)
            f = sb("mla_factors", [P, NT, 2], ctx=c2)
            t0 = tiles["mla_in"]
            units = token_products(k, hT, DC, t0, 512, 0, 512, lambda tt: p[:, tt, 0:512])
            units += token_products(k, hT, DC, t0 + 1, 32, 0, 32, lambda tt: p[:, tt, 512:544])
            run_products(k, units, (t0, t0 + 2))
            jobs = [(p[:, tt, 256 * i:256 * (i + 1)].unsqueeze(1), f[:, tt, i:i + 1])
                    for tt in range(NT) for i in range(2)]
            row_rsqrt(k, jobs, 1e-6)
            scale_groups(k, jobs)
            turn(k, p, 4, low_T, lambda ch: k.col("q_norm", ch))
            q = sb("mla_q", [P, NT, MLA_H * MLA_QK], ctx=c2)
            units = []
            for j in range(3):
                units += token_products(k, low_T[:, 0:2, :], 2, t0 + 2, 1536, 512 * j, 512,
                                        lambda tt, j=j: q[:, tt, 512 * j:512 * (j + 1)])
            for j in range(4):
                units += token_products(k, low_T[:, 2:4, :], 2, t0 + 3, 2048, 512 * j, 512,
                                        lambda tt, j=j: kv[:, tt, 512 * j:512 * (j + 1)])
            run_products(k, units, (t0 + 2, t0 + 4))
            half = MLA_ROPE // 2
            trig = sb("mla_cos_sin", [P, 2, NT, half], ctx=c2)
            tmp = sb("mla_rotated", [P, MLA_H + 1, 2 * half], ctx=c2)
            kf = sb("mla_k", [P, NT, MLA_H, MLA_QK], ctx=c2)
            load_small(k, [(trig[:, n, :, :].rearrange("p a b -> p (a b)"), k.const(s)) for n, s in enumerate(("cos", "sin"))])
            with k.stage() as block:
                @block.vector
                def _(dve):
                    v = nc.vector
                    for tt in range(NT):
                        qs = q[:, tt, :].rearrange("p (h w) -> p h w", h=MLA_H)[:, :, MLA_NOPE:]
                        ks = p[:, tt, 512:544].unsqueeze(1)
                        for a, n, t in ((qs, MLA_H, tmp[:, 0:MLA_H, :]), (ks, 1, tmp[:, MLA_H:, :])):
                            sh = [P, n, half]
                            cs = trig[:, 0, tt, :].unsqueeze(1).to_broadcast(sh)
                            sn = trig[:, 1, tt, :].unsqueeze(1).to_broadcast(sh)
                            a1, a2 = a[:, :, 0:half], a[:, :, half:]
                            k.v(v.tensor_tensor(t[:, :, 0:half], a2, sn, ALU.mult))
                            k.v(v.tensor_tensor(t[:, :, half:], a1, sn, ALU.mult))
                            k.v(v.tensor_tensor(a1, a1, cs, ALU.mult))
                            k.v(v.tensor_tensor(a2, a2, cs, ALU.mult))
                            k.v(v.tensor_tensor(a1, a1, t[:, :, 0:half], ALU.subtract))
                            k.v(v.tensor_tensor(a2, a2, t[:, :, half:], ALU.add))
                        v.tensor_copy(kf[:, tt, :, MLA_NOPE:], ks.to_broadcast([P, MLA_H, MLA_ROPE])
                                      ).then_inc(k.dve_step.up(), 1)
                        v.tensor_copy(kf[:, tt, :, 0:MLA_NOPE], kv[:, tt, :].rearrange(
                            "p (h w) -> p h w", h=MLA_H)[:, :, 0:MLA_NOPE]).then_inc(k.dve_step.up(), 1)
            units = []
            for src, dst, who, s in ((q, q_T, "v", MLA_QK ** -0.5), (kf, k_T, "a", None)):
                for h in range(0, MLA_H, 2):
                    def piece(tt, hh, src=src):
                        if src is q:
                            return q[:, tt, hh * MLA_QK:(hh + 1) * MLA_QK]
                        return kf[:, tt, hh, :]
                    trs = [lambda ps, a=a, tt=tt, h=h, piece=piece: nc.tensor.transpose(
                        ps[0:MLA_QK, a * S + tt * P:a * S + (tt + 1) * P], piece(tt, h + a), k.ident)
                        for a in range(2) for tt in range(NT)]
                    units.append((None, trs, who, [copy_out(k, dst[:, h:h + 2, :].rearrange("p a b -> p (a b)"),
                                                            MLA_QK, 512, s)]))
            run_products(k, units)
        out = sb("mla_out", [P, NT, D], ctx=c)
        mask = sb("mla_causal", [P, NT * S], ctx=c)
        load_small(k, [(mask[:, :], k.const("causal"))])
        attention(k, [([q_T[:, h, :]], [k_T[:, h, :]],
                       lambda kt, h=h: kv[:, kt, h * 128 + MLA_NOPE:(h + 1) * 128], ("masked", mask[:, :]),
                       lambda tt, h=h: out[:, tt, h * MLA_V:(h + 1) * MLA_V]) for h in range(MLA_H)], MLA_V)
        outT = sb("mla_out_T", [P, DC, S], ctx=c)
        turn(k, out, DC, outT)
        project_residual(k, outT, DC, t0 + 4, x, ALPHA)

def cross_attention(k, x, hT, layer, tiles):
    nc, sb = k.nc, k.sb
    t0 = tiles[f"xa{layer}"]
    with ExitStack() as c:
        q_T = sb("xa_q_T", [P, DC, S], ctx=c)
        k_T = sb("xa_k_T", [P, DC, S], ctx=c)
        v = sb("xa_v", [P, NT, D], ctx=c)
        out = sb("xa_out", [P, NT, D], ctx=c)
        memT = sb("memory_2_T", [P, DC, S], ctx=c)
        load_small(k, [(memT[:, :, :], k.dram["mem_2_T"])])
        units = []
        for src, dst, t, s in ((hT, q_T, t0, XA_D ** -0.5), (memT, k_T, t0 + 2, None)):
            for j in range(2):
                for m in range(4):
                    u = feature_products(k, src, DC, t + j, 512, m * P, P, [(dst[:, 4 * j + m, :], 0, P)], "va"[m % 2])
                    units.append(u[:3] + ([copy_out(k, dst[:, 4 * j + m, :], P, S, s)],))
        for j in range(2):
            units += token_products(k, memT, DC, t0 + 4 + j, 512, 0, 512, lambda tt, j=j: v[:, tt, 512 * j:512 * (j + 1)])
        run_products(k, units, (t0, t0 + 6))
        attention(k, [([q_T[:, 2 * h, :], q_T[:, 2 * h + 1, :]], [k_T[:, 2 * h, :], k_T[:, 2 * h + 1, :]],
                       lambda kt, h=h: v[:, kt, h * XA_D:(h + 1) * XA_D], ("plain", None),
                       lambda tt, h=h: out[:, tt, h * XA_D:(h + 1) * XA_D]) for h in range(XA_H)], XA_D)
        outT = sb("xa_out_T", [P, DC, S], ctx=c)
        turn(k, out, DC, outT)
        project_residual(k, outT, DC, t0 + 6, x, ALPHA)

def moe(k, x, hT, layer, tiles):
    nc, sb = k.nc, k.sb
    first = tiles[f"moe{layer}"]
    with ExitStack() as c:
        rows_T = sb("sorted_rows_T", [P, DC, PAIRS + P], ctx=c)
        outs_T = sb("sorted_outputs_T", [P, DC, PAIRS + P], ctx=c)
        spread = sb("gate_of_place", [P, NT, PAIRS], ctx=c)
        table = sb("window_table", [1, 2, WINDOWS + 1], U32, ctx=c)
        with ExitStack() as c2:
            NL = NG + NE
            w = sb("router_weights", [P, DC, NL], ctx=c2)
            bias = sb("router_bias", [P, NL], ctx=c2)
            iota = sb("router_iota", [P, PAIRS], ctx=c2)
            lg = sb("router_logits", [P, NT, NL], ctx=c2)
            g8 = sb("group_logits", [P, NT, 8], ctx=c2)
            top = sb("router_top", [P, NT, 8], ctx=c2)
            at = sb("router_at", [P, NT, 8], U32, ctx=c2)
            atf = sb("router_at_float", [P, NT, 8], ctx=c2)
            neg = sb("router_neg", [P, NT, 1], ctx=c2)
            gsum = sb("router_sum", [P, NT, 1], ctx=c2)
            hot = sb("group_hot", [P, NT, NG], ctx=c2)
            off = sb("group_off", [P, NT, NG], ctx=c2)
            gexp = sb("group_exps", [P, NT, NG], ctx=c2)
            le = sb("expert_logits", [P, NT, NE], ctx=c2)
            e2 = sb("second_exp", [P, NT, 1], ctx=c2)
            g1 = sb("gate_first", [P, NT, 2], ctx=c2)
            one = sb("chosen", [P, 2, NT, NE], ctx=c2)
            both = sb("chosen_both", [P, NT, NE], ctx=c2)
            ones = sb("router_ones", [P, 2, P], ctx=c2)
            num = sb("expert_counts", [P, NE], ctx=c2)
            cum = sb("pairs_before", [P, NT, NE], ctx=c2)
            start = sb("expert_starts", [P, NE], ctx=c2)
            win = sb("expert_windows", [P, 4, NE], ctx=c2)
            hit = sb("window_hits", [1, 2, WINDOWS, NE], ctx=c2)
            tf = sb("window_table_float", [1, 2, WINDOWS + 1], ctx=c2)
            place = sb("pair_places_of_token", [P, 2, NT], ctx=c2)
            sel = sb("token_of_place", [P, NT, PAIRS], ctx=c2)
            half2 = sb("second_gate_of_place", [P, PAIRS], ctx=c2)
            load_small(k, [(w[:, :, 0:NG], k.dram["moe_w_group_2"][layer].rearrange("(c p) n -> p c n", p=P)),
                           (w[:, :, NG:NL], k.dram["moe_w_expert_2"][layer].rearrange("(c p) n -> p c n", p=P)),
                           (bias[:, 0:NG], k.dram["moe_b_group_2"][layer].partition_broadcast(P)),
                           (bias[:, NG:NL], k.dram["moe_b_expert_2"][layer].partition_broadcast(P)),
                           (iota[:, :], k.const("iota")[:, 0:PAIRS]),
                           (ones[:, 0, :], k.const("ones")), (ones[:, 1, :], k.const("before"))])
            run_products(k, [(None, [lambda ps, kk=kk, tt=tt: mm(k, ps[:, 0:NL], hT[:, kk, tt * P:(tt + 1) * P],
                                                                 w[:, kk, :], kk == 0, kk == DC - 1)
                                     for kk in range(DC)], "v",
                              [lambda eng, ps, tt=tt: nc.vector.tensor_tensor(lg[:, tt, :], ps[:, 0:NL], bias[:, :],
                                                                              ALU.add)]) for tt in range(NT)])
            with k.stage() as block:
                @block.vector
                def _(dve):
                    v = nc.vector
                    k.v(v.memset(g8[:, :, :], -3e38))
                    k.v(v.tensor_copy(g8[:, :, 0:NG], lg[:, :, 0:NG]))
                    for tt in range(NT):
                        k.v(v.max(top[:, tt, :], g8[:, tt, :]))
                        k.v(v.max_index(at[:, tt, :], top[:, tt, :], g8[:, tt, :]))
                    k.v(v.tensor_copy(atf[:, :, :], at[:, :, :]))
                    v.tensor_scalar(neg[:, :, :], top[:, :, 0:1], -1.0, None,
                                    ALU.mult).then_inc(k.shift_ready.up(), 1)
                    for tt in range(NT):
                        k.v(v.tensor_scalar(hot[:, tt, :], iota[:, 0:NG], atf[:, tt, 0:1], None, ALU.is_equal))
                    k.v(v.tensor_scalar(off[:, :, :], hot[:, :, :], 1.0, 1e30, ALU.subtract, ALU.mult))
                    for tt in range(NT):
                        e = le[:, tt, :].rearrange("p (g n) -> p g n", g=NG)
                        lt = lg[:, tt, NG:NL].rearrange("p (g n) -> p g n", g=NG)
                        bc = lambda t: t.unsqueeze(2).to_broadcast([P, NG, NPG])
                        k.v(v.tensor_tensor(e, lt, bc(hot[:, tt, :]), ALU.mult))
                        k.v(v.tensor_tensor(e, e, bc(off[:, tt, :]), ALU.add))
                        k.v(v.max(top[:, tt, :], le[:, tt, :]))
                        k.v(v.max_index(at[:, tt, :], top[:, tt, :], le[:, tt, :]))
                    k.v(v.tensor_copy(atf[:, :, :], at[:, :, :]))
                    v.tensor_tensor(e2[:, :, :], top[:, :, 1:2], top[:, :, 0:1],
                                    ALU.subtract).then_inc(k.shift_ready.up(), 1)
                    dve.wait_ge(k.exps_ready.sem, k.exps_ready.at(NT))
                    k.v(v.reciprocal(gsum[:, :, :], gsum[:, :, :]))
                    dve.wait_ge(k.exps_ready.sem, k.exps_ready.at(NT + 1))
                    k.v(v.tensor_scalar(g1[:, :, 0:1], e2[:, :, :], 1.0, None, ALU.add))
                    k.v(v.reciprocal(g1[:, :, 0:1], g1[:, :, 0:1]))
                    k.v(v.tensor_tensor(g1[:, :, 0:1], g1[:, :, 0:1], gsum[:, :, :], ALU.mult))
                    k.v(v.tensor_tensor(g1[:, :, 1:2], g1[:, :, 0:1], e2[:, :, :], ALU.mult))
                    for tt in range(NT):
                        for j in range(2):
                            k.v(v.tensor_scalar(one[:, j, tt, :], iota[:, 0:NE], atf[:, tt, j:j + 1], None,
                                                ALU.is_equal))
                    k.v(v.tensor_tensor(both[:, :, :], one[:, 0, :, :], one[:, 1, :, :], ALU.add))

                @block.scalar
                def _(act):
                    act.wait_ge(k.shift_ready.sem, k.shift_ready.at(1))
                    for tt in range(NT):
                        nc.scalar.activation(gexp[:, tt, :], lg[:, tt, 0:NG], ACT.Exp,
                                             bias=neg[:, tt, :], accum_out=gsum[:, tt, :]
                                             ).then_inc(k.exps_ready.up(), 1)
                    act.wait_ge(k.shift_ready.sem, k.shift_ready.at(2))
                    nc.scalar.activation(e2[:, :, :], e2[:, :, :], ACT.Exp).then_inc(k.exps_ready.up(), 1)
            run_products(k, [
                (None, [lambda ps, tt=tt: mm(k, ps[:, 0:NE], ones[:, 0, :], both[:, tt, :], tt == 0, tt == 1)
                        for tt in range(NT)], "v", [copy_out(k, num[:, :], P, NE)]),
                (None, [lambda ps: mm(k, ps[:, 0:NE], ones[:, 1, :], both[:, 0, :])], "v",
                 [copy_out(k, cum[:, 0, :], P, NE)]),
                (None, [lambda ps: mm(k, ps[:, 0:NE], ones[:, 0, :], both[:, 0, :], True, False),
                        lambda ps: mm(k, ps[:, 0:NE], ones[:, 1, :], both[:, 1, :], False, True)], "v",
                 [copy_out(k, cum[:, 1, :], P, NE)])])
            with k.stage() as block:
                @block.vector
                def _(dve):
                    v = nc.vector
                    k.v(v.tensor_tensor_scan(start[:, :], ones[:, 0, 0:NE], num[:, :], 0.0, ALU.mult, ALU.add))
                    k.v(v.tensor_tensor(start[:, :], start[:, :], num[:, :], ALU.subtract))
                    for tt in range(NT):
                        k.v(v.tensor_tensor(cum[:, tt, :], cum[:, tt, :], start[:, :], ALU.add))
                        for j in range(2):
                            k.v(v.tensor_tensor(both[:, j, :], one[:, j, tt, :], cum[:, tt, :], ALU.mult))
                            k.v(v.tensor_reduce(place[:, j, tt:tt + 1], both[:, j, :], AX, ALU.add))
                    k.v(v.tensor_scalar(win[:, 0, :], num[:, :], float(P), 1.0, ALU.is_gt, ALU.add))
                    k.v(v.tensor_tensor_scan(win[:, 2, :], ones[:, 0, 0:NE], win[:, 0, :], 0.0, ALU.mult, ALU.add))
                    k.v(v.tensor_tensor(win[:, 1, :], win[:, 2, :], win[:, 0, :], ALU.subtract))
                    k.v(v.scalar_tensor_tensor(out=win[:, 3, :], in0=win[:, 1, :], scalar=-float(P),
                                               in1=start[:, :], op0=ALU.mult, op1=ALU.add))
                    sh = [1, WINDOWS, NE]
                    w_ids = iota[0:1, 0:WINDOWS].unsqueeze(2).to_broadcast(sh)
                    per_e = lambda t: t.unsqueeze(1).to_broadcast(sh)
                    h0, h1 = hit[:, 0, :, :], hit[:, 1, :, :]
                    k.v(v.tensor_tensor(h0, w_ids, per_e(win[0:1, 1, :]), ALU.is_ge))
                    k.v(v.tensor_tensor(h1, w_ids, per_e(win[0:1, 2, :]), ALU.is_lt))
                    k.v(v.tensor_tensor(h0, h0, h1, ALU.mult))
                    k.v(v.tensor_tensor(h1, h0, per_e(iota[0:1, 0:NE]), ALU.mult))
                    k.v(v.tensor_reduce(tf[:, 0, 0:WINDOWS], h1, AX, ALU.add))
                    k.v(v.tensor_tensor(h1, h0, per_e(win[0:1, 3, :]), ALU.mult))
                    k.v(v.tensor_reduce(tf[:, 1, 0:WINDOWS], h1, AX, ALU.add))
                    k.v(v.scalar_tensor_tensor(out=tf[:, 1, 0:WINDOWS], in0=iota[0:1, 0:WINDOWS], scalar=float(P),
                                               in1=tf[:, 1, 0:WINDOWS], op0=ALU.mult, op1=ALU.add))
                    for j in range(2):
                        k.v(v.tensor_copy(tf[:, j, WINDOWS:WINDOWS + 1], win[0:1, 2, NE - 1:NE]))
                    k.v(v.tensor_copy(table[:, :, :], tf[:, :, :]))
                    for tt in range(NT):
                        k.v(v.tensor_scalar(half2[:, :], iota[:, :], place[:, 0, tt:tt + 1], None, ALU.is_equal))
                        k.v(v.scalar_tensor_tensor(out=sel[:, tt, :], in0=iota[:, :], scalar=place[:, 1, tt:tt + 1],
                                                   in1=half2[:, :], op0=ALU.is_equal, op1=ALU.add))
                        k.v(v.tensor_scalar(spread[:, tt, :], iota[:, :], place[:, 0, tt:tt + 1], g1[:, tt, 0:1],
                                            ALU.is_equal, ALU.mult))
                        k.v(v.tensor_scalar(half2[:, :], iota[:, :], place[:, 1, tt:tt + 1], g1[:, tt, 1:2],
                                            ALU.is_equal, ALU.mult))
                        k.v(v.tensor_tensor(spread[:, tt, :], spread[:, tt, :], half2[:, :], ALU.add))

                @block.gpsimd
                def _(pool):
                    nc.gpsimd.memset(rows_T[:, :, PAIRS:], 0.0).then_inc(k.act_step.up(), 1)
                    pool.wait_ge(k.act_step.sem, k.act_step.at(1))
            run_products(k, [(None, [lambda ps, tt=tt, ch=ch: mm(k, ps, x[:, tt, ch * P:(ch + 1) * P], sel[:, tt, :],
                                                                 tt == 0, tt == 1) for tt in range(NT)],
                              "va"[ch % 2], [copy_out(k, rows_T[:, ch, 0:PAIRS], P, PAIRS)]) for ch in range(DC)])
        with ExitStack() as c2:
            main_windows(k, first, layer, rows_T, outs_T, table, c2)
        with ExitStack() as c2:
            late_windows(k, layer, rows_T, outs_T, table, c2)
        outs = sb("sorted_outputs", [P, PAIRS // P, D], ctx=c)
        back = sb("gate_of_place_T", [P, PAIRS // P, S], ctx=c)
        units = []
        for pc in range(PAIRS // P):
            units.append((None, [lambda ps, pc=pc, tt=tt: nc.tensor.transpose(
                ps[:, tt * P:(tt + 1) * P], spread[:, tt, pc * P:(pc + 1) * P], k.ident) for tt in range(NT)],
                "v", [copy_out(k, back[:, pc, :], P, S)]))
            for hf in range(2):
                units.append((None, [lambda ps, pc=pc, hf=hf, n=n: nc.tensor.transpose(
                    ps[:, n * P:(n + 1) * P], outs_T[:, 4 * hf + n, pc * P:(pc + 1) * P], k.ident)
                    for n in range(4)], "va"[hf], [copy_out(k, outs[:, pc, 512 * hf:512 * (hf + 1)], P, 512)]))
        run_products(k, units)
        run_products(k, [(None, [lambda ps, pc=pc, tt=tt, hf=hf: mm(
            k, ps, back[:, pc, tt * P:(tt + 1) * P], outs[:, pc, 512 * hf:512 * (hf + 1)], pc == 0,
            pc == PAIRS // P - 1) for pc in range(PAIRS // P)], "v",
            [residual(k, x, ALPHA, 512 * hf, 512)(tt)]) for tt in range(NT) for hf in range(2)])

def expert_part(k, flat, part):
    return flat.rearrange("p (c n) -> p c n", c=FF // P if part == 2 else DC)

def expert_source(k, layer, part, expert):
    return k.dram["moe_parts"][part][layer, bass.ds(expert, 1)].rearrange("a (c p) n -> p (a c) n", p=P)

def into_features(k, ps, w, rows):
    for m in range(FF // P):
        for ch in range(DC):
            last = mm(k, ps[:, m * P:(m + 1) * P], w[:, ch, m * P:(m + 1) * P], rows[:, ch, :], ch == 0, ch == DC - 1)
    return last

def out_of_features(k, ps2, w, hidden):
    for d in range(DC):
        for m in range(FF // P):
            last = mm(k, ps2[:, d // 4, (d % 4) * P:(d % 4 + 1) * P], w[:, m, d * P:(d + 1) * P],
                      hidden[:, m * P:(m + 1) * P], m == 0, m == FF // P - 1)
    return last

def main_windows(k, first, layer, rows_T, outs_T, table, c):
    nc, sb = k.nc, k.sb
    window = sb("window_rows_T", [P, 2, DC, P], ctx=c)
    silu = sb("silu_out", [P, 2, FF], ctx=c)
    hid = sb("expert_hidden", [P, 2, FF], ctx=c)
    TURN = 4
    turns = NE // TURN
    start_of = lambda eng, w: eng.value_load(table[0:1, 1, bass.ds(w, 1)], min_val=0, max_val=PAIRS)

    with k.stage() as block:
        LEFT = 3 * TURN - 3
        FIRST, LAST = 0, turns - 1

        def weights(pe, i, q):
            if q < 0 or (i is LAST and q > LEFT):
                tile, later = first + (q + 2 if q < 0 else 3 * NE - 1), 0
            else:
                tile, later = first + 2 + q, 3 * TURN // SLOTS * 16 * i
            pe.wait_ge(k.stream.landed[tile % SLOTS].sem, 16 * (tile // SLOTS + 1) + later)
            return expert_part(k, k.ring[:, tile % SLOTS, :], 2 if q >= 0 and q % 3 == 2 else (q + 2 if q < 0 else q % 3))

        def ups(pe, i, e, start, q):
            n = TURN * i + e
            pe.wait_ge(k.window_ready.sem, k.window_ready.at(n + 1))
            for part, ready, read in ((0, k.gate_products, k.silu_ready), (1, k.up_products, k.gated_ready)):
                w = weights(pe, i, q + part)
                if not start:
                    pe.wait_ge(read.sem, read.at(n - 1))
                into_features(k, k.ps[:, 2 * (e % 2) + part, :], w,
                              window[:, e % 2, :, :]).then_inc(ready.up(), 1)

        def downs(pe, i, e, start):
            n = TURN * i + e
            w = weights(pe, i, 3 * e + 2)
            pe.wait_ge(k.gated_ready.sem, k.gated_ready.at(n + 1))
            if not start:
                pe.wait_ge(k.dve_evacuated.sem, k.dve_evacuated.at(n - 1))
                pe.wait_ge(k.act_evacuated.sem, k.act_evacuated.at(n - 1))
            b = 4 + 2 * (e % 2)
            out_of_features(k, k.ps[:, b:b + 2, :], w, hid[:, e % 2, :]).then_inc(k.down_products.up(), 1)

        def pe_turn(pe, i, first_turn, last_turn):
            for e in range(TURN):
                if e < TURN - 1 or not last_turn:
                    ups(pe, i, e + 1, first_turn and e + 1 < 2, 3 * e)
                downs(pe, i, e, first_turn and e < 2)

        def place(eng, n, b, half, done, ordered=True):
            at = start_of(eng, n)
            eng.wait_ge(k.down_products.sem, k.down_products.at(n + 1))
            if ordered:
                eng.wait_ge(done.sem, done.at(n))
            dst = outs_T[:, 4 * half:4 * half + 4, bass.ds(at, P)]
            src = k.ps[:, 4 + 2 * b + half, :].rearrange("p (d n) -> p d n", d=4)
            ins = eng.tensor_copy(dst, src) if half == 0 else eng.activation(dst, src, ACT.Copy)
            ins.then_inc(done.up(), 1)

        def act_turn(act, i, start):
            for e in range(TURN):
                n = TURN * i + e
                act.wait_ge(k.gate_products.sem, k.gate_products.at(n + 1))
                if not (start and e < 2):
                    act.wait_ge(k.gated_ready.sem, k.gated_ready.at(n - 1))
                nc.scalar.activation(silu[:, e % 2, :], k.ps[:, 2 * (e % 2), :],
                                     ACT.Silu).then_inc(k.silu_ready.up(), 1)
                if not (start and e == 0):
                    place(act, n - 1, (e + 1) % 2, 1, k.act_evacuated, not (start and e == 1))

        def dve_turn(dve, i, start):
            for e in range(TURN):
                n = TURN * i + e
                dve.wait_ge(k.silu_ready.sem, k.silu_ready.at(n + 1))
                dve.wait_ge(k.up_products.sem, k.up_products.at(n + 1))
                if not (start and e < 2):
                    dve.wait_ge(k.down_products.sem, k.down_products.at(n - 1))
                nc.vector.tensor_tensor(hid[:, e % 2, :], silu[:, e % 2, :], k.ps[:, 2 * (e % 2) + 1, :],
                                        ALU.mult).then_inc(k.gated_ready.up(), 1)
                if not (start and e == 0):
                    place(dve, n - 1, (e + 1) % 2, 0, k.dve_evacuated, not (start and e == 1))

        def pool_turn(pool, i, start):
            for e in range(TURN):
                n = TURN * i + e
                at = start_of(pool, n)
                if not (start and e < 2):
                    pool.wait_ge(k.up_products.sem, k.up_products.at(n - 1))
                nc.gpsimd.tensor_copy(window[:, e % 2, :, :],
                                      rows_T[:, :, bass.ds(at, P)]).then_inc(k.window_ready.up(), 1)

        @block.sync
        def _(sp):
            def expert_of(w):
                return sp.value_load(table[0:1, 0, bass.ds(w, 1)], min_val=0, max_val=NE - 1)

            def load(t, expert, part):
                slot = (first + t) % SLOTS
                sp.dma_start(expert_part(k, k.ring[:, slot, :], part),
                             expert_source(k, layer, part, expert)).then_inc(k.stream.landed[slot].sem, 16)

            def used(i, q):
                e, part = divmod(q, 3)
                done = (k.gate_products, k.up_products, k.down_products)[part]
                sp.wait_ge(done.sem, done.at(TURN * i + e + (1 if part == 2 else 2)))

            def fill(i, q, tile):
                e, part = divmod(q, 3)
                expert = expert_of(TURN * i + e + (0 if part == 2 else 1))
                before = q - SLOTS
                if i is LAST and q > LEFT:
                    used(i, LEFT - SLOTS)
                elif before >= 0:
                    used(i, before)
                elif i is not FIRST:
                    used(i - 1, before + 3 * TURN)
                elif before >= -2:
                    done = (k.gate_products, k.up_products)[before + 2]
                    sp.wait_ge(done.sem, done.at(1))
                load(tile, expert, part)

            for q in range(3 * TURN):
                fill(FIRST, q, 2 + q)
            with sp.Fori(1, turns - 1) as i:
                for q in range(3 * TURN):
                    fill(i, q, 2 + q)
            for q in range(LEFT):
                fill(LAST, q, 2 + q)
            fill(LAST, 3 * TURN - 1, 3 * NE - 1)
            k.stream.issued = first + 3 * NE
            for q in (LEFT - 3, LEFT - 2, LEFT - 1, 3 * TURN - 1):
                used(LAST, q)
                if k.stream.issued < len(k.stream.sources):
                    k.stream.load(sp, k.stream.issued)
                    k.stream.issued += 1

        @block.gpsimd
        def _(pool):
            pool_turn(pool, 0, True)
            with pool.Fori(1, turns) as i:
                pool_turn(pool, i, False)
            k.window_ready.repeated(turns - 1, TURN)

        @block.tensor
        def _(pe):
            ups(pe, 0, 0, True, -2)
            pe_turn(pe, 0, True, False)
            with pe.Fori(1, turns - 1) as i:
                pe_turn(pe, i, False, False)
            for sig in (k.gate_products, k.up_products, k.down_products):
                sig.repeated(turns - 2, TURN)
            pe_turn(pe, LAST, False, True)

        @block.scalar
        def _(act):
            act_turn(act, 0, True)
            with act.Fori(1, turns) as i:
                act_turn(act, i, False)
            for sig in (k.silu_ready, k.act_evacuated):
                sig.repeated(turns - 1, TURN)
            place(act, NE - 1, 1, 1, k.act_evacuated)

        @block.vector
        def _(dve):
            dve_turn(dve, 0, True)
            with dve.Fori(1, turns) as i:
                dve_turn(dve, i, False)
            for sig in (k.gated_ready, k.dve_evacuated):
                sig.repeated(turns - 1, TURN)
            place(dve, NE - 1, 1, 0, k.dve_evacuated)

def late_windows(k, layer, rows_T, outs_T, table, c):
    nc, sb = k.nc, k.sb
    w_sb = sb("late_weights", [P, 3, SLOT], ctx=c)
    window = sb("late_rows_T", [P, DC, P], ctx=c)
    silu = sb("late_silu", [P, FF], ctx=c)
    hid = sb("late_hidden", [P, FF], ctx=c)
    landed, rows_in, up, silu_in, gated, down, placed_v, placed_a = (
        nc.alloc_semaphore(name=f"late_{n}_{layer}") for n in
        ("landed", "rows_in", "up", "silu_in", "gated", "down", "placed_v", "placed_a"))
    late = range(WINDOWS - NE)

    def exists(eng, n):
        count = eng.value_load(table[0:1, 0, WINDOWS:WINDOWS + 1], min_val=NE, max_val=WINDOWS)
        return eng.If(count > NE + n)

    start_of = lambda eng, n: eng.value_load(table[0:1, 1, NE + n:NE + n + 1], min_val=0, max_val=PAIRS)

    with k.stage() as block:
        @block.sync
        def _(sp):
            for n in late:
                with exists(sp, n):
                    if n:
                        sp.wait_ge(down, n)
                    expert = sp.value_load(table[0:1, 0, NE + n:NE + n + 1], min_val=0, max_val=NE - 1)
                    for part in range(3):
                        sp.dma_start(expert_part(k, w_sb[:, part, :], part),
                                     expert_source(k, layer, part, expert)).then_inc(landed, 16)
                    sp.wait_ge(landed, 48 * (n + 1))

        @block.gpsimd
        def _(pool):
            for n in late:
                with exists(pool, n):
                    if n:
                        pool.wait_ge(down, n)
                    nc.gpsimd.tensor_copy(window[:, :, :], rows_T[:, :, bass.ds(start_of(pool, n), P)]
                                          ).then_inc(rows_in, 1)
                    pool.wait_ge(rows_in, n + 1)

        @block.tensor
        def _(pe):
            for n in late:
                with exists(pe, n):
                    pe.wait_ge(landed, 48 * (n + 1))
                    pe.wait_ge(rows_in, n + 1)
                    into_features(k, k.ps[:, 0, :], expert_part(k, w_sb[:, 0, :], 0), window)
                    into_features(k, k.ps[:, 1, :], expert_part(k, w_sb[:, 1, :], 1), window).then_inc(up, 1)
                    pe.wait_ge(gated, n + 1)
                    if n:
                        pe.wait_ge(placed_v, n)
                        pe.wait_ge(placed_a, n)
                    out_of_features(k, k.ps[:, 2:4, :], expert_part(k, w_sb[:, 2, :], 2), hid).then_inc(down, 1)

        @block.scalar
        def _(act):
            for n in late:
                with exists(act, n):
                    act.wait_ge(up, n + 1)
                    nc.scalar.activation(silu[:, :], k.ps[:, 0, :], ACT.Silu).then_inc(silu_in, 1)
                    act.wait_ge(down, n + 1)
                    nc.scalar.activation(outs_T[:, 4:8, bass.ds(start_of(act, n), P)],
                                         k.ps[:, 3, :].rearrange("p (d n) -> p d n", d=4),
                                         ACT.Copy).then_inc(placed_a, 1)
                    act.wait_ge(placed_a, n + 1)

        @block.vector
        def _(dve):
            for n in late:
                with exists(dve, n):
                    dve.wait_ge(silu_in, n + 1)
                    nc.vector.tensor_tensor(hid[:, :], silu[:, :], k.ps[:, 1, :], ALU.mult).then_inc(gated, 1)
                    dve.wait_ge(down, n + 1)
                    nc.vector.tensor_copy(outs_T[:, 0:4, bass.ds(start_of(dve, n), P)],
                                          k.ps[:, 2, :].rearrange("p (d n) -> p d n", d=4)).then_inc(placed_v, 1)
                    dve.wait_ge(placed_v, n + 1)

def add_banks(k, x, alpha):
    with k.stage() as block:
        @block.vector
        def _(dve):
            for tt in range(NT):
                for half in range(2):
                    xs = x[:, tt, half * 512:(half + 1) * 512]
                    k.nc.vector.scalar_tensor_tensor(out=xs, in0=xs, scalar=alpha, in1=k.ps[:, 2 * tt + half, :],
                                                     op0=ALU.mult, op1=ALU.add).then_inc(k.dve_step.up(), 1)

def second_block(k, tiles, out):
    nc, sb = k.nc, k.sb
    keep = k.dram["x_rows"]
    layer_rows = lambda name, layer: k.dram[name][layer]
    with ExitStack() as c:
        cat_T = sb("mixed_2_T", [P, DC, S], ctx=c)
        with ExitStack() as c2:
            x = sb("x_first", [P, NT, D], ctx=c2)
            load_small(k, [(x[:, :, :], keep)])
            add_banks(k, x, 1.0)
            store(k, [(keep, x[:, :, :])])
            turn(k, x, DC, cat_T)
        rwkv_and_gating(k, tiles, cat_T, cat_T)
        x = sb("x_second", [P, NT, D], ctx=c)
        load_small(k, [(x[:, :, :], keep)])
        project_residual(k, cat_T, DC, tiles["ab_out"], x, ALPHA)
        hT = sb("h_T", [P, DC, S], ctx=c)
        for layer in range(2):
            if layer == 1:
                mla(k, x, hT, tiles)
            layer_norm(k, x, layer_rows("ln1_g_2", layer), layer_rows("ln1_b_2", layer))
            turn(k, x, DC, hT)
            cross_attention(k, x, hT, layer, tiles)
            layer_norm(k, x, layer_rows("ln2_g_2", layer), layer_rows("ln2_b_2", layer))
            turn(k, x, DC, hT)
            moe(k, x, hT, layer, tiles)
            layer_norm(k, x, layer_rows("ln3_g_2", layer), layer_rows("ln3_b_2", layer))
            if layer == 0:
                turn(k, x, DC, hT)
        store(k, [(out.rearrange("a (t p) d -> p (a t) d", p=P), x[:, :, :])])

def build(nc, dram, out):
    with ExitStack() as ctx:
        k = Kernel(nc, dram, ctx)

        def columns(w, width=512):
            n = w.shape[1]
            v = w.rearrange("(c p) n -> p c n", p=P)
            return [v[:, :, j:min(j + width, n)] for j in range(0, n, width)]

        def wt(name, layer=0):
            return dram[name][layer]
        st, tiles = k.stream, {}
        tiles["w_in"] = st.add(columns(wt("w_in")))
        tiles["w_mem_kv"] = st.add(columns(wt("w_mem_kv")))
        tiles["w_out"] = st.add(columns(wt("w_out")))
        tiles["w_peer_q"] = st.add(columns(wt("w_peer_q")))
        tiles["peer"] = st.add([dram["peer_uv"][i].unsqueeze(1) for i in range(PK // 2)])
        w = wt("ab_w_in_2")
        tiles["ab_in"] = st.add(columns(w[:, 0:1536]) + columns(w[:, 1536:1792]) + columns(w[:, 1792:2816]))
        tiles["ab_out"] = st.add(columns(wt("ab_w_out_2")))

        def tail(layer):
            tiles[f"xa{layer}"] = st.add(columns(wt("xa_wq_2", layer)) + columns(wt("xa_wkv_2", layer))
                                         + columns(wt("xa_wo_2", layer)))
            parts = []
            for e in range(NE):
                for m in k.dram["moe_parts"]:
                    parts += columns(m[layer, e], 1024)
            tiles[f"moe{layer}"] = st.add(parts[0:2] + [None] * (len(parts) - 2))
        tail(0)
        tiles["mla_in"] = st.add(columns(wt("mla_w_in_2")) + columns(wt("mla_wq_b_2"), 2048)
                                 + columns(wt("mla_wkv_b_2"), 2048) + columns(wt("mla_w_out_2")))
        tail(1)
        first_block(k, tiles)
        second_block(k, tiles, out)

PLAIN = ["x", "mem", "w_in", "w_mem_kv", "w_out", "w_peer_q", "ab_w_in_2", "rw_w2_2", "rw_a2_2", "rw_g2_2",
         "rw_gn_g_2", "rw_gn_b_2", "sg_ln_g_2", "sg_ln_b_2", "ab_w_out_2", "mla_w_in_2", "mla_wq_b_2",
         "mla_wkv_b_2", "mla_w_out_2", "ln1_g_2", "ln1_b_2", "xa_wq_2", "xa_wkv_2", "xa_wo_2", "ln2_g_2",
         "ln2_b_2", "moe_w_group_2", "moe_b_group_2", "moe_w_expert_2", "moe_b_expert_2", "moe_w_gate_2",
         "moe_w_up_2", "moe_w_down_2", "ln3_g_2", "ln3_b_2"]

def laid_out(inputs):
    a = {n: np.ascontiguousarray(inputs[n]) for n in PLAIN}
    for n in (1, 2):
        a[f"subkeys_T_{n}"] = np.ascontiguousarray(np.asarray(inputs[f"peer_subkeys_{n}"])[0].transpose(2, 0, 1))
    u = np.asarray(inputs["peer_u"])[0].reshape(PK, PK // 2, 2, DC, P).transpose(1, 4, 2, 3, 0)
    v = np.asarray(inputs["peer_v"])[0].reshape(PK, PK // 2, 2, D).transpose(1, 0, 2, 3)
    a["peer_uv"] = np.concatenate([u.reshape(PK // 2, P, -1), v.reshape(PK // 2, P, -1)], 2)
    a["sg_ws_T"] = np.ascontiguousarray(np.asarray(inputs["sg_ws_2"])[0].transpose(2, 0, 1))
    a["mem_2_T"] = np.ascontiguousarray(np.asarray(inputs["mem_2"])[0].T.reshape(DC, P, S).transpose(1, 0, 2))
    cols = []
    for name, src, rows, n in vector_columns():
        m = np.asarray(inputs[src]).reshape(n, rows).T
        cols.append(np.concatenate([m, np.zeros((P - rows, n), m.dtype)], 0))
    a["columns"] = np.ascontiguousarray(np.concatenate(cols, 1))
    a["consts"] = shape_constants()[1]
    return a

def kernel(**inputs):
    import concourse.bacc as bacc
    from concourse.bass_utils import run_bass_kernel_spmd

    nc = bacc.Bacc("TRN2", target_bir_lowering=False, num_devices=1)
    arrays = laid_out(inputs)
    dram = {n: nc.dram_tensor(f"in_{n}", a.shape, F32, kind="ExternalInput").ap() for n, a in arrays.items()}
    for n, shape in (("x_rows", [P, NT, D]), ("h_T", [P, DC, S]), ("slots", [P, 3, S])):
        dram[n] = nc.dram_tensor(n, shape, F32, kind="Internal").ap()
    dram["moe_parts"] = [dram["moe_w_gate_2"], dram["moe_w_up_2"], dram["moe_w_down_2"]]
    out = nc.dram_tensor("out_rows", [1, S, D], F32, kind="ExternalOutput").ap()
    build(nc, dram, out)
    r = run_bass_kernel_spmd(nc, [{f"in_{n}": a for n, a in arrays.items()}], core_ids=[0])
    return r.results[0]["out_rows"]
```

```python
from contextlib import ExitStack, contextmanager
import math

import numpy as np
import concourse.bass as bass
from concourse import mybir

ALU = mybir.AluOpType
ACT = mybir.ActivationFunctionType
F32 = mybir.dt.float32
F32R = mybir.dt.float32r
U32 = mybir.dt.uint32
AX = mybir.AxisListType.X

P = 128
S = 256
NT = S // P
D = 1024
DC = D // P
MASKED = -1e32

HD = 64
H_DIL, H_MOBA, H_MEM = 6, 6, 4
H_MIX = H_DIL + H_MOBA + H_MEM
IN_W = 3 * HD * (H_DIL + H_MOBA) + HD * H_MEM
N_ALIBI = H_DIL + H_MOBA
SLOPES = [2.0 ** (-8.0 * (i + 1) / N_ALIBI) for i in range(N_ALIBI)]

PH, PK, TOPK = 8, 128, 16
RW_H, RW_N, CH = 8, 64, 64
NCH = S // CH
SG = 4
MLA_H, MLA_NOPE, MLA_ROPE, MLA_V = 16, 64, 32, 64
MLA_QK = MLA_NOPE + MLA_ROPE
XA_H, XA_D = 4, 256
NG, NPG = 4, 8
NE = NG * NPG
FF = 512
PAIRS = 2 * S
WINDOWS = NE + (PAIRS - 1) // (P + 1)
ALPHA = 4.0 ** 0.25
SLOT = 4096
SLOTS = 4

def shape_constants():
    t = np.arange(S)
    dist = (t[:, None] - t[None, :]).astype(np.float32)
    causal = dist >= 0
    idist = dist.astype(np.int64)
    count = ((causal & (idist <= 128)).astype(np.float32) + (causal & (idist % 4 == 0))
             + (causal & (idist % 16 == 0))).astype(np.float32)
    rows = lambda m: m.reshape(NT, P, S).transpose(1, 0, 2).reshape(P, NT * S)
    c = {}
    c["ident"] = np.eye(P, dtype=np.float32)
    c["iota"] = np.tile(np.arange(PAIRS + P, dtype=np.float32), (P, 1))
    c["ones"] = np.ones((P, P), np.float32)
    c["before"] = (np.arange(P)[:, None] < np.arange(P)[None, :]).astype(np.float32)
    c["dist_moba"] = rows(np.where(causal, -dist, MASKED))
    c["dist_dil"] = rows(np.where(count > 0, -dist, MASKED))
    c["count"] = rows(count)
    c["causal"] = rows(np.where(causal, 0.0, MASKED))
    half = MLA_ROPE // 2
    inv = 10000.0 ** (-np.arange(half, dtype=np.float32) / half)
    ang = (t[:, None].astype(np.float32) * inv[None, :]).astype(np.float32)
    pack = lambda m: m.reshape(NT, P, half).transpose(1, 0, 2).reshape(P, NT * half)
    c["cos"], c["sin"] = pack(np.cos(ang)), pack(np.sin(ang))
    s64, t64 = np.arange(CH)[:, None], np.arange(CH)[None, :]
    pad = lambda m: np.concatenate([m.reshape(CH, -1), np.zeros((P - CH, m.size // CH))], 0)
    c["tri"] = pad(np.concatenate([s64 < t64, s64 <= t64], 1))
    lev = [((s64 // (2 * b) == t64 // (2 * b)) & (s64 % (2 * b) < b) & (t64 % (2 * b) >= b))
           for b in (1, 2, 4, 8, 16, 32)]
    c["levels"] = pad(np.stack(lev, 1))
    c["reset"] = np.tile((np.arange(RW_H * S) % CH != 0).astype(np.float32), (P, 1))
    at, parts, n = {}, [], 0
    for k, v in c.items():
        v = np.ascontiguousarray(v, dtype=np.float32)
        at[k] = (n, v.shape[1])
        n += v.shape[1]
        parts.append(v)
    return at, np.concatenate(parts, 1)

def vector_columns():
    return [("g_mix", "g_mix", P, DC), ("g_memtok", "g_memtok", P, DC), ("g_ffn", "g_ffn", P, DC),
            ("qg_dil", "qg_dil", HD, 1), ("kg_dil", "kg_dil", HD, 1), ("qg_moba", "qg_moba", HD, 1),
            ("kg_moba", "kg_moba", HD, 1), ("qg_mem", "qg_mem", HD, 1), ("kg_mem", "kg_mem", HD, 1),
            ("og_dil", "og_dil", P, 3), ("og_moba", "og_moba", P, 3), ("og_mem", "og_mem", P, 2),
            ("mu_rkv", "ab_mu_2", 64, 28), ("w0", "rw_w0_2", 64, 8), ("a0", "rw_a0_2", 64, 8),
            ("k_k", "rw_k_k_2", 64, 8), ("k_a", "rw_k_a_2", 64, 8), ("r_k", "rw_r_k_2", 64, 8),
            ("mu_g", "ab_mu_2", P, 14), ("sg_b", "sg_b_2", P, SG),
            ("q_norm", "mla_q_norm_2", P, 2), ("kv_norm", "mla_kv_norm_2", P, 2)]

def column_places():
    at, n = {}, 0
    for name, _, _, cols in vector_columns():
        at[name] = (n, cols)
        n += cols
    return at, n

class Signal:

    def __init__(self, nc, name):
        self.sem = nc.alloc_semaphore(name=name)
        self.count = self.start = 0

    def up(self, n=1):
        self.count += n
        return self.sem

    def at(self, n):
        return self.start + n

    def repeated(self, times, each):
        self.count += (times - 1) * each

class WeightStream:

    def __init__(self, k):
        self.k = k
        self.sources = []
        self.issued = 0
        self.restart = 0
        self.hold = None
        self.landed = [Signal(k.nc, f"weights_landed_{i}") for i in range(SLOTS)]

    def add(self, aps):
        first = len(self.sources)
        self.sources += aps
        return first

    def view(self, n, kc, cols):
        return self.k.ring[:, n % SLOTS, 0:kc * cols].rearrange("p (k n) -> p k n", k=kc)

    def load(self, sp, n):
        src = self.sources[n]
        kc, cols = src.shape[1], src.shape[2]
        sp.dma_start(self.view(n, kc, cols), src).then_inc(self.landed[n % SLOTS].up(16), 16)

    def wait_landed(self, pe, n):
        pe.wait_ge(self.landed[n % SLOTS].sem, 16 * (n // SLOTS + 1))

    def prefetch(self, sp, end, first, freed):
        while (self.issued < min(end + SLOTS, len(self.sources)) and self.sources[self.issued] is not None
               and self.issued != self.hold):
            old = self.issued - SLOTS
            if old >= first:
                sp.wait_ge(self.k.products.sem, self.k.products.at(freed[old]))
            self.load(sp, self.issued)
            self.issued += 1

class Kernel:
    def __init__(self, nc, dram, ctx):
        self.nc, self.dram, self.ctx, self.allocated = nc, dram, ctx, 0
        self.signals = []

        def signal(name):
            self.signals.append(Signal(nc, name))
            return self.signals[-1]
        self.products = signal("products")
        self.dve_evacuated = signal("dve_evacuated")
        self.act_evacuated = signal("act_evacuated")
        self.dve_step = signal("dve_step")
        self.act_step = signal("act_step")
        self.small_loaded = signal("small_loaded")
        self.scores_ready = signal("scores_ready")
        self.scores_read = signal("scores_read")
        self.shift_ready = signal("shift_ready")
        self.exps_ready = signal("exps_ready")
        self.probs_ready = signal("probs_ready")
        self.probs_turned = signal("probs_turned")
        self.turned_copied = signal("turned_copied")
        self.heads_ready = signal("heads_ready")
        self.heads_scaled = signal("heads_scaled")
        self.rows_stored = signal("rows_stored")
        self.onehots_ready = signal("onehots_ready")
        self.more_onehots = signal("more_onehots")
        self.onehots_gated = signal("onehots_gated")
        self.gates_placed = signal("gates_placed")
        self.act_ready = signal("act_ready")
        self.weights_gated = signal("weights_gated")
        self.hidden_ready = signal("hidden_ready")
        self.gate_products = signal("gate_products")
        self.up_products = signal("up_products")
        self.u_high_ready = signal("u_high_ready")
        self.u_low_ready = signal("u_low_ready")
        self.v_high_ready = signal("v_high_ready")
        self.v_low_ready = signal("v_low_ready")
        self.key_landed = [[nc.alloc_semaphore(name=f"{n}_landed_{b}") for b in range(2)] for n in "uv"]
        self.silu_ready = signal("silu_ready")
        self.gated_ready = signal("gated_ready")
        self.window_ready = signal("window_ready")
        self.down_products = signal("down_products")
        self.ps = ctx.enter_context(nc.psum_tensor("banks", [P, 8, 512], F32))
        self.stream = WeightStream(self)
        self.const_at, _ = shape_constants()
        self.col_at, ncols = column_places()
        self.cols_sb = self.sb("columns", [P, ncols])
        self.ident = self.sb("identity", [P, P])[:, :]
        self.place_ring()

    def place_ring(self):
        self.ring_place = self.ctx.enter_context(ExitStack())
        self.ring = self.sb("weight_ring", [P, SLOTS, SLOT], ctx=self.ring_place)

    def sb(self, name, shape, dt=F32, ctx=None):
        self.allocated += 1
        return (ctx or self.ctx).enter_context(self.nc.sbuf_tensor(f"{name}_{self.allocated}", shape, dt))

    @contextmanager
    def stage(self):
        with self.nc.Block() as block:
            yield block
        for s in self.signals:
            s.start = s.count

    def const(self, name, rows=P):
        a, n = self.const_at[name]
        return self.dram["consts"][0:rows, a:a + n]

    def col(self, name, i, rows=P):
        a, _ = self.col_at[name]
        return self.cols_sb[0:rows, a + i:a + i + 1]

    def cols(self, name, rows=P):
        a, n = self.col_at[name]
        return self.cols_sb[0:rows, a:a + n]

    def v(self, ins):
        ins.then_inc(self.dve_step.up(), 1)
        self.nc.vector.wait_ge(self.dve_step.sem, self.dve_step.count)

    def a(self, ins):
        ins.then_inc(self.act_step.up(), 1)
        self.nc.scalar.wait_ge(self.act_step.sem, self.act_step.count)

def load_small(k, pairs, wait=True):
    with k.stage() as block:
        @block.sync
        def _(sp):
            if k.stream.issued == k.stream.restart:
                if pairs and not k.stream.issued:
                    sp.wait_ge(k.small_loaded.sem, k.small_loaded.at(16 * len(pairs)))
                k.stream.prefetch(sp, k.stream.restart, k.stream.restart, {})

        @block.scalar
        def _(act):
            for dst, src in pairs:
                act.dma_start(dst, src).then_inc(k.small_loaded.up(16), 16)
            if wait:
                act.wait_ge(k.small_loaded.sem, k.small_loaded.at(16 * len(pairs)))

def run_products(k, units, tiles=(0, 0), beside=None):
    nc = k.nc
    served = {"v": 0, "a": 0}
    order = []
    for tile, _, who, copies in units:
        served[who] += len(copies)
        order.append(served[who])
    freed = {}
    for u, (tile, *_) in enumerate(units):
        if tile is not None:
            freed[tile] = u + 1
    emptied = {"v": k.dve_evacuated, "a": k.act_evacuated}

    with k.stage() as block:
        @block.sync
        def _(sp):
            k.stream.prefetch(sp, tiles[1] if tiles[1] else k.stream.issued - SLOTS, tiles[0], freed)
            if beside:
                beside[2](sp)

        @block.tensor
        def _(pe):
            seen = set()
            for u, (tile, products, _, _) in enumerate(units):
                if tile is not None and tile not in seen:
                    k.stream.wait_landed(pe, tile)
                    seen.add(tile)
                if u >= 8:
                    pe.wait_ge(emptied[units[u - 8][2]].sem, emptied[units[u - 8][2]].at(order[u - 8]))
                for product in products:
                    last = product(k.ps[:, u % 8, :])
                last.then_inc(k.products.up(), 1)

        @block.vector
        def _(dve):
            if beside:
                beside[0](dve)
            for u, (_, _, who, copies) in enumerate(units):
                if who == "v":
                    dve.wait_ge(k.products.sem, k.products.at(u + 1))
                    for copy in copies:
                        copy(nc.vector, k.ps[:, u % 8, :]).then_inc(k.dve_evacuated.up(), 1)

        @block.scalar
        def _(act):
            for u, (_, _, who, copies) in enumerate(units):
                if who == "a":
                    act.wait_ge(k.products.sem, k.products.at(u + 1))
                    for copy in copies:
                        copy(nc.scalar, k.ps[:, u % 8, :]).then_inc(k.act_evacuated.up(), 1)
            if beside:
                beside[1](act)

def mm(k, out, lhsT, rhs, start=True, stop=True):
    return k.nc.tensor.matmul(out, lhsT, rhs, start=start, stop=stop)

def copy_out(k, out, rows, cols, scale=None, cols0=0, rows0=0):
    def go(eng, ps):
        src = ps[rows0:rows0 + rows, cols0:cols0 + cols]
        if len(out.shape) == 3:
            src = src.rearrange("p (a b) -> p a b", a=out.shape[1])
        if eng is k.nc.scalar:
            return eng.activation(out, src, ACT.Copy, scale=1.0 if scale is None else scale)
        if scale is None:
            return eng.tensor_copy(out, src)
        return eng.tensor_scalar(out, src, scale, None, ALU.mult)
    return go

def token_products(k, xT, kc, tile, cols, c0, width, out, who=None, copy=None):
    units = []
    w = k.stream.view(tile, kc, cols)
    for tt in range(NT):
        def prod(ps, kk, tt=tt):
            return mm(k, ps[:, 0:width], xT[:, kk, tt * P:(tt + 1) * P], w[:, kk, c0:c0 + width],
                      kk == 0, kk == kc - 1)
        cp = copy(tt) if copy else copy_out(k, out(tt), P, width)
        units.append((tile, [lambda ps, kk=kk, prod=prod: prod(ps, kk) for kk in range(kc)],
                      who or "va"[tt % 2], [cp]))
    return units

def feature_products(k, xT, kc, tile, cols, c0, m, outs, who):
    w = k.stream.view(tile, kc, cols)
    prods = [lambda ps, kk=kk: mm(k, ps[0:m, 0:S], w[:, kk, c0:c0 + m], xT[:, kk, 0:S],
                                  kk == 0, kk == kc - 1) for kk in range(kc)]
    return (tile, prods, who, [copy_out(k, o, r, S, rows0=r0) for o, r0, r in outs])

def turn(k, src, n, outT, gain=None, pt=P, tiles=NT):
    units = []
    for c in range(n):
        trs = [lambda ps, c=c, tt=tt: k.nc.tensor.transpose(ps[:, tt * pt:(tt + 1) * pt],
                                                            src[0:pt, tt, c * P:(c + 1) * P],
                                                            k.ident[0:pt, 0:pt]) for tt in range(tiles)]
        units.append((None, trs, "va"[c % 2],
                      [copy_out(k, outT[:, c, :], P, tiles * pt, gain(c) if gain else None)]))
    run_products(k, units)

def row_rsqrt(k, jobs, eps):
    nc = k.nc
    with ExitStack() as c:
        sq = k.sb("squares", [P, 2048], ctx=c)
        with k.stage() as block:
            @block.vector
            def _(dve):
                for src, out in jobs:
                    p, g, w = src.shape
                    view = sq[0:p, 0:g * w].rearrange("p (g w) -> p g w", g=g)
                    k.v(nc.vector.tensor_tensor(view, src, src, ALU.mult))
                    k.v(nc.vector.tensor_reduce(out, view, AX, ALU.add))
                    k.v(nc.vector.tensor_scalar(out, out, 1.0 / w, eps, ALU.mult, ALU.add))
                for n, (_, out) in enumerate(jobs):
                    dve.wait_ge(k.act_step.sem, k.act_step.at(n + 1))
                    nc.vector.reciprocal(out, out).then_inc(k.dve_step.up(), 1)

            @block.scalar
            def _(act):
                for n, (_, out) in enumerate(jobs):
                    act.wait_ge(k.dve_step.sem, k.dve_step.at(3 * (n + 1)))
                    nc.scalar.activation(out, out, ACT.Sqrt).then_inc(k.act_step.up(), 1)

def scale_groups(k, jobs):
    with k.stage() as block:
        @block.vector
        def _(dve):
            for rows, f in jobs:
                p, g, w = rows.shape
                k.nc.vector.tensor_tensor(rows, rows, f.unsqueeze(2).to_broadcast([p, g, w]),
                                          ALU.mult).then_inc(k.dve_step.up(), 1)

def layer_norm(k, x, gb, eps=1e-5):
    nc = k.nc
    with ExitStack() as c:
        st = k.sb("ln_stats", [P, NT, 2, 6], ctx=c)
        mv = k.sb("ln_mean_var", [P, NT, 2], ctx=c)
        rs = k.sb("ln_rstd", [P, NT, 1], ctx=c)
        with k.stage() as block:
            @block.scalar
            def _(act):
                for tt in range(NT):
                    act.wait_ge(k.dve_step.sem, k.dve_step.at(4 * (tt + 1)))
                    nc.scalar.activation(rs[:, tt, :], rs[:, tt, :], ACT.Sqrt).then_inc(k.act_step.up(), 1)

            @block.vector
            def _(dve):
                for tt in range(NT):
                    k.v(nc.vector.bn_stats(st[:, tt, 0, :], x[:, tt, 0:512]))
                    k.v(nc.vector.bn_stats(st[:, tt, 1, :], x[:, tt, 512:1024]))
                    k.v(nc.vector.bn_aggr(mv[:, tt, :], st[:, tt, :, :].rearrange("p a b -> p (a b)")))
                    k.v(nc.vector.tensor_scalar(rs[:, tt, :], mv[:, tt, 1:2], eps, None, ALU.add))
                dve.wait_ge(k.small_loaded.sem, k.small_loaded.at(0))
                for tt in range(NT):
                    k.v(nc.vector.scalar_tensor_tensor(out=x[:, tt, :], in0=x[:, tt, :], scalar=mv[:, tt, 0:1],
                                                       in1=gb[:, 0, :], op0=ALU.subtract, op1=ALU.mult))
                for tt in range(NT):
                    dve.wait_ge(k.act_step.sem, k.act_step.at(tt + 1))
                    k.v(nc.vector.reciprocal(rs[:, tt, :], rs[:, tt, :]))
                    k.v(nc.vector.scalar_tensor_tensor(out=x[:, tt, :], in0=x[:, tt, :], scalar=rs[:, tt, :],
                                                       in1=gb[:, 1, :], op0=ALU.mult, op1=ALU.add))

def attention(k, heads, dv):
    nc, H = k.nc, len(heads)
    with ExitStack() as c:
        sc = k.sb("scores", [P, 3, NT, S], ctx=c)
        pT = k.sb("probs_T", [P, 2, 2, S], ctx=c)
        top = k.sb("row_max", [P, H, NT], ctx=c)
        den = k.sb("row_sum", [P, H, NT], ctx=c)
        with k.stage() as block:
            @block.tensor
            def _(pe):
                for i in range(H + 3):
                    if i < H:
                        q, kt, _, _, _ = heads[i]
                        if i >= 2:
                            pe.wait_ge(k.scores_read.sem, k.scores_read.at(i - 1))
                        for tt in range(NT):
                            for n in range(len(q)):
                                last = mm(k, k.ps[:, i % 2, tt * S:(tt + 1) * S], q[n][:, tt * P:(tt + 1) * P],
                                          kt[n], n == 0, n == len(q) - 1)
                        last.then_inc(k.scores_ready.up(), 1)
                    h = i - 2
                    if 0 <= h < H:
                        pe.wait_ge(k.probs_ready.sem, k.probs_ready.at(h + 1))
                        if h >= 2:
                            pe.wait_ge(k.turned_copied.sem, k.turned_copied.at(h - 1))
                        for kt2 in range(2):
                            for tt in range(NT):
                                last = nc.tensor.transpose(k.ps[:, 2 + h % 2, kt2 * S + tt * P:kt2 * S + (tt + 1) * P],
                                                           sc[:, h % 3, tt, kt2 * P:(kt2 + 1) * P], k.ident)
                        last.then_inc(k.probs_turned.up(), 1)
                    h = i - 3
                    if 0 <= h < H:
                        pe.wait_ge(k.turned_copied.sem, k.turned_copied.at(h + 1))
                        if h >= 2:
                            pe.wait_ge(k.heads_scaled.sem, k.heads_scaled.at(NT * (h - 1)))
                        for tt in range(NT):
                            for kt2 in range(2):
                                last = mm(k, k.ps[:, 4 + h % 2, tt * 256:tt * 256 + dv],
                                          pT[:, h % 2, kt2, tt * P:(tt + 1) * P], heads[h][2](kt2),
                                          kt2 == 0, kt2 == 1)
                        last.then_inc(k.heads_ready.up(), 1)

            @block.vector
            def _(dve):
                for i in range(H + 3):
                    if i < H:
                        kind, arg = heads[i][3]
                        flat = sc[:, i % 3, :, :].rearrange("p a b -> p (a b)")
                        dve.wait_ge(k.scores_ready.sem, k.scores_ready.at(i + 1))
                        if i >= 3:
                            dve.wait_ge(k.probs_turned.sem, k.probs_turned.at(i - 2))
                        if kind == "alibi":
                            slope, dist, _ = arg
                            ins = nc.vector.scalar_tensor_tensor(out=flat, in0=dist, scalar=slope,
                                                                 in1=k.ps[:, i % 2, :], op0=ALU.mult, op1=ALU.add)
                        elif kind == "masked":
                            ins = nc.vector.tensor_tensor(flat, arg, k.ps[:, i % 2, :], ALU.add)
                        else:
                            ins = nc.vector.tensor_copy(flat, k.ps[:, i % 2, :])
                        ins.then_inc(k.scores_read.up(), 1)
                        dve.wait_ge(k.scores_read.sem, k.scores_read.at(i + 1))
                        k.v(nc.vector.tensor_reduce(top[:, i, :], sc[:, i % 3, :, :], AX, ALU.max))
                        nc.vector.tensor_scalar(top[:, i, :], top[:, i, :], -1.0, None,
                                                ALU.mult).then_inc(k.shift_ready.up(), 1)
                    h = i - 1
                    if 0 <= h < H:
                        kind, arg = heads[h][3]
                        dve.wait_ge(k.exps_ready.sem, k.exps_ready.at(NT * (h + 1)))
                        if kind == "alibi" and arg[2] is not None:
                            flat = sc[:, h % 3, :, :].rearrange("p a b -> p (a b)")
                            k.v(nc.vector.tensor_tensor(flat, flat, arg[2], ALU.mult))
                            k.v(nc.vector.tensor_reduce(den[:, h, :], sc[:, h % 3, :, :], AX, ALU.add))
                        nc.vector.reciprocal(den[:, h, :], den[:, h, :]).then_inc(k.probs_ready.up(), 1)
                    h = i - 3
                    if 0 <= h < H:
                        dve.wait_ge(k.probs_ready.sem, k.probs_ready.at(h + 1))
                        dve.wait_ge(k.heads_ready.sem, k.heads_ready.at(h + 1))
                        for tt in range(NT):
                            nc.vector.tensor_scalar(heads[h][4](tt), k.ps[:, 4 + h % 2, tt * 256:tt * 256 + dv],
                                                    den[:, h, tt:tt + 1], None,
                                                    ALU.mult).then_inc(k.heads_scaled.up(), 1)

            @block.scalar
            def _(act):
                for i in range(H + 2):
                    if i < H:
                        act.wait_ge(k.shift_ready.sem, k.shift_ready.at(i + 1))
                        for tt in range(NT):
                            nc.scalar.activation(sc[:, i % 3, tt, :], sc[:, i % 3, tt, :], ACT.Exp,
                                                 bias=top[:, i, tt:tt + 1],
                                                 accum_out=den[:, i, tt:tt + 1]).then_inc(k.exps_ready.up(), 1)
                    h = i - 2
                    if h >= 0:
                        act.wait_ge(k.probs_turned.sem, k.probs_turned.at(h + 1))
                        if h >= 2:
                            act.wait_ge(k.heads_ready.sem, k.heads_ready.at(h - 1))
                        nc.scalar.activation(pT[:, h % 2, :, :].rearrange("p a b -> p (a b)"),
                                             k.ps[:, 2 + h % 2, :], ACT.Copy).then_inc(k.turned_copied.up(), 1)

def residual(k, x, alpha, c0, width):
    def at(tt):
        def go(eng, ps):
            return k.nc.vector.scalar_tensor_tensor(out=x[:, tt, c0:c0 + width], in0=x[:, tt, c0:c0 + width],
                                                    scalar=alpha, in1=ps[:, 0:width], op0=ALU.mult, op1=ALU.add)
        return go
    return at

def project_residual(k, xT, kc, first, x, alpha):
    units = []
    for j in range(2):
        units += token_products(k, xT, kc, first + j, 512, 0, 512, None, "v", residual(k, x, alpha, 512 * j, 512))
    run_products(k, units, (first, first + 2))

def first_block_attention(k, x, tiles):
    nc, sb = k.nc, k.sb
    with ExitStack() as c:
        proj = sb("projections", [P, NT, IN_W], ctx=c)
        kv = sb("memory_kv", [P, NT, 2 * HD * H_MEM], ctx=c)
        with ExitStack() as c2:
            mem = sb("memory_rows", [P, NT, D], ctx=c2)
            xT = sb("x_T", [P, DC, S], ctx=c2)
            memT = sb("memory_T", [P, DC, S], ctx=c2)
            f = sb("row_factors", [P, 2 * NT], ctx=c2)
            y = sb("normed_rows", [P, NT, D], ctx=c2)
            load_small(k, [(x[:, :, :], k.dram["x"].rearrange("a (t p) d -> p (a t) d", p=P)),
                           (mem[:, :, :], k.dram["mem"].rearrange("a (t p) d -> p (a t) d", p=P)),
                           (k.cols_sb[:, :], k.dram["columns"]), (k.ident, k.const("ident"))])
            row_rsqrt(k, [(x[:, :, :], f[:, 0:NT]), (mem[:, :, :], f[:, NT:2 * NT])], 1e-6)
            for src, dst, at, gain in ((x, xT, 0, "g_mix"), (mem, memT, NT, "g_memtok")):
                with k.stage() as block:
                    @block.vector
                    def _(dve):
                        for tt in range(NT):
                            nc.vector.tensor_scalar(y[:, tt, :], src[:, tt, :], f[:, at + tt:at + tt + 1], None,
                                                    ALU.mult).then_inc(k.dve_step.up(), 1)
                turn(k, y, DC, dst, lambda ch, gain=gain: k.col(gain, ch))
            units = []
            for j in range(IN_W // 512):
                units += token_products(k, xT, DC, tiles["w_in"] + j, 512, 0, 512,
                                        lambda tt, j=j: proj[:, tt, 512 * j:512 * (j + 1)])
            units += token_products(k, memT, DC, tiles["w_mem_kv"], 512, 0, 512, lambda tt: kv[:, tt, :])
            run_products(k, units, (tiles["w_in"], tiles["w_mem_kv"] + 1))

        q_T = sb("queries_T", [HD, H_MIX, S], ctx=c)
        k_T = sb("keys_T", [HD, H_MIX, S], ctx=c)
        out = sb("mixed_heads", [P, NT, D], ctx=c)
        masks = sb("attention_constants", [P, 3, NT * S], ctx=c)
        gf = sb("group_factors", [P, NT, 40], ctx=c)
        load_small(k, [(masks[:, n, :], k.const(name)) for n, name in enumerate(("dist_dil", "dist_moba", "count"))])
        wd = HD * H_DIL
        jobs = []
        for tt in range(NT):
            for n, (src, c0, g) in enumerate(((proj, 0, 12), (proj, 3 * wd, 12), (proj, 6 * wd, 4), (kv, 0, 4))):
                g0 = (0, 12, 24, 28)[n]
                jobs.append((src[:, tt, c0:c0 + g * HD].rearrange("p (g w) -> p g w", g=g), gf[:, tt, g0:g0 + g]))
        row_rsqrt(k, jobs, 1e-6)
        scale_groups(k, jobs)
        units = []
        at = 0
        for dst, h0, n, src, c0, gain in ((q_T, 0, 6, proj, 0, "qg_dil"), (k_T, 0, 6, proj, wd, "kg_dil"),
                                          (q_T, 6, 6, proj, 3 * wd, "qg_moba"), (k_T, 6, 6, proj, 4 * wd, "kg_moba"),
                                          (q_T, 12, 4, proj, 6 * wd, "qg_mem"), (k_T, 12, 4, kv, 0, "kg_mem")):
            for h in range(0, n, 2):
                trs = [lambda ps, a=a, tt=tt, src=src, c0=c0, h=h:
                       nc.tensor.transpose(ps[0:HD, a * S + tt * P:a * S + (tt + 1) * P],
                                           src[:, tt, c0 + (h + a) * HD:c0 + (h + a + 1) * HD], k.ident)
                       for a in range(2) for tt in range(NT)]

                def gained(eng, ps, dst=dst, h=h0 + h, gain=gain):
                    o = dst[:, h:h + 2, :].rearrange("p a b -> p (a b)")
                    if eng is nc.scalar:
                        return eng.activation(o, ps[0:HD, :], ACT.Copy, scale=k.col(gain, 0, HD))
                    return eng.tensor_scalar(o, ps[0:HD, :], k.col(gain, 0, HD),
                                             HD ** -0.5 if dst is q_T else 1.0, ALU.mult, ALU.mult)
                units.append((None, trs, "v" if dst is q_T else "a", [gained]))
        run_products(k, units)

        heads = []
        for h in range(H_MIX):
            if h < H_DIL:
                v = lambda kt, h=h: proj[:, kt, 2 * wd + h * HD:2 * wd + (h + 1) * HD]
                kind = ("alibi", (SLOPES[2 * h], masks[:, 0, :], masks[:, 2, :]))
            elif h < H_DIL + H_MOBA:
                g = h - H_DIL
                v = lambda kt, g=g: proj[:, kt, 5 * wd + g * HD:5 * wd + (g + 1) * HD]
                kind = ("alibi", (SLOPES[2 * g + 1], masks[:, 1, :], None))
            else:
                g = h - H_DIL - H_MOBA
                v = lambda kt, g=g: kv[:, kt, (H_MEM + g) * HD:(H_MEM + g + 1) * HD]
                kind = ("plain", None)
            heads.append(([q_T[:, h, :]], [k_T[:, h, :]], v, kind,
                          lambda tt, h=h: out[:, tt, h * HD:(h + 1) * HD]))
        attention(k, heads, HD)

        jobs = [(out[:, tt, c0:c0 + n].unsqueeze(1), gf[:, tt, i:i + 1])
                for tt in range(NT) for i, (c0, n) in enumerate(((0, wd), (wd, wd), (2 * wd, D - 2 * wd)))]
        row_rsqrt(k, jobs, 1e-6)
        scale_groups(k, jobs)
        outT = sb("mixed_T", [P, DC, S], ctx=c)
        turn(k, out, DC, outT, lambda ch: k.col("og_dil", ch))
        project_residual(k, outT, DC, tiles["w_out"], x, 1.0)

def top16(k, lists):
    v = k.nc.vector
    steps = [lambda a, b, t, i: v.max(t[:, 0:8], a),
             lambda a, b, t, i: v.max_index(i[:, 0:8], t[:, 0:8], a),
             lambda a, b, t, i: v.match_replace(b, t[:, 0:8], a, -3e38),
             lambda a, b, t, i: v.max(t[:, 8:16], b),
             lambda a, b, t, i: v.max_index(i[:, 8:16], t[:, 8:16], b)]
    for step in steps:
        for item in lists:
            step(*item).then_inc(k.dve_step.up(), 1)
        v.wait_ge(k.dve_step.sem, k.dve_step.count)

def peer_routing(k, hT, tiles, slots_T):
    nc, sb = k.nc, k.sb
    with ExitStack() as c:
        qT = sb("peer_queries_T", [P, 2 * PH, S], ctx=c)
        units = []
        for j in range(4):
            for m in range(4):
                units.append(feature_products(k, hT, DC, tiles["w_peer_q"] + j, 512, m * P, P,
                                              [(qT[:, 4 * j + m, :], 0, P)], "va"[m % 2]))
        run_products(k, units, (tiles["w_peer_q"], tiles["w_peer_q"] + 4))
        sub = sb("sub_keys_T", [P, 2, PH, PK], ctx=c)
        load_small(k, [(sub[:, n, :, :], k.dram[f"subkeys_T_{n + 1}"]) for n in range(2)])
        sc = sb("sub_scores", [P, 2, NT, PH, PK], ctx=c)
        units = []
        for side in range(2):
            for tt in range(NT):
                for hh in range(0, PH, 4):
                    prods = [lambda ps, h=h, side=side, tt=tt, hh=hh:
                             mm(k, ps[:, (h - hh) * PK:(h - hh + 1) * PK], qT[:, 2 * h + side, tt * P:(tt + 1) * P],
                                sub[:, side, h, :]) for h in range(hh, hh + 4)]
                    units.append((None, prods, "va"[tt], [copy_out(
                        k, sc[:, side, tt, hh:hh + 4, :].rearrange("p a b -> p (a b)"), P, 512)]))
        run_products(k, units)

        best = sb("best_keys", [P, NT, 2, PH, TOPK], ctx=c)
        place = sb("best_places", [P, NT, 2, PH, TOPK], U32, ctx=c)
        placef = sb("best_places_float", [P, NT, 2, PH, TOPK], ctx=c)
        pair = sb("pair_sums", [P, PH, TOPK * TOPK], ctx=c)
        spare = sb("spare", [P, 2 * PH * TOPK * TOPK], ctx=c)
        ps_top = sb("pair_best", [P, NT, PH, TOPK], ctx=c)
        ps_at = sb("pair_places", [P, NT, PH, TOPK], U32, ctx=c)
        digit = sb("pair_digits", [P, 2, PH * TOPK], U32, ctx=c)
        digitf = sb("pair_digits_float", [P, 2, PH * TOPK], ctx=c)
        rows = sb("slot_rows", [P, NT, 3, PH * TOPK], ctx=c)
        iota = sb("iota_16", [P, TOPK], ctx=c)
        tot = sb("gate_sums", [P, NT * PH], ctx=c)
        load_small(k, [(iota[:, :], k.const("iota")[:, 0:TOPK])])
        G = [P, PH * TOPK, TOPK]

        def route(dve):
            v = nc.vector
            for tt in range(NT):
                sp = spare[:, :].rearrange("p (s h n) -> p s h n", s=2, h=PH)
                top16(k, [(sc[:, s, tt, h, :], sp[:, s, h, 0:PK], best[:, tt, s, h, :], place[:, tt, s, h, :])
                          for s in range(2) for h in range(PH)])
                k.v(v.tensor_copy(placef[:, tt], place[:, tt]))
                for h in range(PH):
                    v.tensor_tensor(pair[:, h, :].rearrange("p (a b) -> p a b", a=TOPK),
                                    best[:, tt, 0, h, :].unsqueeze(2).to_broadcast([P, TOPK, TOPK]),
                                    best[:, tt, 1, h, :].unsqueeze(1).to_broadcast([P, TOPK, TOPK]),
                                    ALU.add).then_inc(k.dve_step.up(), 1)
                v.wait_ge(k.dve_step.sem, k.dve_step.count)
                top16(k, [(pair[:, h, :], sp[:, 0, h, :], ps_top[:, tt, h, :], ps_at[:, tt, h, :])
                          for h in range(PH)])
                at = ps_at[:, tt, :, :].rearrange("p h j -> p (h j)")
                k.v(v.tensor_scalar(digit[:, 0, :], at, 4, None, ALU.logical_shift_right))
                k.v(v.tensor_scalar(digit[:, 1, :], at, TOPK - 1, None, ALU.bitwise_and))
                k.v(v.tensor_copy(digitf[:, :, :], digit[:, :, :]))
                for s in range(2):
                    hot = spare[:, 0:PH * TOPK * TOPK].rearrange("p (j a) -> p j a", a=TOPK)
                    k.v(v.tensor_tensor(hot, digitf[:, s, :].unsqueeze(2).to_broadcast(G),
                                        iota[:, :].unsqueeze(1).to_broadcast(G), ALU.is_equal))
                    for h in range(PH):
                        hh = hot[:, h * TOPK:(h + 1) * TOPK, :]
                        v.tensor_tensor(hh, hh, placef[:, tt, s, h, :].unsqueeze(1).to_broadcast([P, TOPK, TOPK]),
                                        ALU.mult).then_inc(k.dve_step.up(), 1)
                    v.wait_ge(k.dve_step.sem, k.dve_step.count)
                    k.v(v.tensor_reduce(rows[:, tt, s, :], hot, AX, ALU.add))
                v.tensor_tensor(rows[:, tt, 2, :].rearrange("p (h j) -> p h j", h=PH), ps_top[:, tt, :, :],
                                ps_top[:, tt, :, 0:1].to_broadcast([P, PH, TOPK]),
                                ALU.subtract).then_inc(k.shift_ready.up(), 1)
            for tt in range(NT):
                dve.wait_ge(k.exps_ready.sem, k.exps_ready.at(tt + 1))
                e = rows[:, tt, 2, :].rearrange("p (h j) -> p h j", h=PH)
                t = tot[:, tt * PH:(tt + 1) * PH]
                k.v(v.tensor_reduce(t, e, AX, ALU.add))
                k.v(v.reciprocal(t, t))
                k.v(v.tensor_tensor(e, e, t.unsqueeze(2).to_broadcast([P, PH, TOPK]), ALU.mult))

        def exponentials(act):
            for tt in range(NT):
                act.wait_ge(k.shift_ready.sem, k.shift_ready.at(tt + 1))
                nc.scalar.activation(rows[:, tt, 2, :], rows[:, tt, 2, :],
                                     ACT.Exp).then_inc(k.exps_ready.up(), 1)

        memT = sb("memory_2_T", [P, DC, S], ctx=c)
        kv = [(sb("xa_k_T", [P, DC, S], ctx=c), sb("xa_v", [P, NT, D], ctx=c)) for _ in range(2)]
        load_small(k, [(memT[:, :, :], k.dram["mem_2_T"])])
        units = []
        for layer, (k_T, v_rows) in enumerate(kv):
            t0 = tiles["xa_kv"] + 4 * layer
            for j in range(2):
                for m in range(4):
                    units.append(feature_products(k, memT, DC, t0 + j, 512, m * P, P, [(k_T[:, 4 * j + m, :], 0, P)], "a"))
            for j in range(2):
                units += token_products(k, memT, DC, t0 + 2 + j, 512, 0, 512,
                                        lambda tt, j=j, v_rows=v_rows: v_rows[:, tt, 512 * j:512 * (j + 1)], "a")

        def store_kv(sp):
            for layer, (k_T, v_rows) in enumerate(kv):
                sp.wait_ge(k.act_evacuated.sem, k.act_evacuated.at(12 * (layer + 1)))
                sp.dma_start(k.dram["xa_k_T"][layer], k_T[:, :, :]).then_inc(k.rows_stored.up(16), 16)
                sp.dma_start(k.dram["xa_v"][layer], v_rows[:, :, :]).then_inc(k.rows_stored.up(16), 16)
            sp.wait_ge(k.rows_stored.sem, k.rows_stored.at(64))
        run_products(k, units, (tiles["xa_kv"], tiles["xa_kv"] + 8), (route, exponentials, store_kv))
        units = []
        for n in range(3):
            trs = [lambda ps, n=n, tt=tt: nc.tensor.transpose(ps[:, tt * P:(tt + 1) * P], rows[:, tt, n, :], k.ident)
                   for tt in range(NT)]
            units.append((None, trs, "va"[n % 2], [copy_out(k, slots_T[:, n, :], P, S)]))
        run_products(k, units)

def peer_gates(k, slots_T, gates, raw):
    nc = k.nc
    GRP = 4
    BUF = 4
    with ExitStack() as c:
        hot = k.sb("one_hots", [P, BUF, 2, GRP, P], ctx=c)
        iota = k.sb("iota_keys", [P, PK], ctx=c)
        load_small(k, [(iota[:, :], k.const("iota")[:, 0:PK])])
        turns = S // GRP // BUF

        with k.stage() as block:
            @block.sync
            def _(sp):
                for key in range(2):
                    for which in range(2):
                        load_key(k, sp, raw, which, key, key)

            def hots(dve, g, b, wait):
                if wait:
                    dve.wait_ge(k.products.sem, k.products.at(g - BUF + 1))
                for side, n in ((1, GRP - 1), (0, GRP)):
                    sh = [P, n, P]
                    ins = nc.vector.tensor_tensor(hot[:, b, side, 0:n, :],
                                                  slots_T[:, side, bass.ds(g * GRP, n)].unsqueeze(2).to_broadcast(sh),
                                                  iota[:, :].unsqueeze(1).to_broadcast(sh), ALU.is_equal)
                    if side:
                        ins.then_inc(k.onehots_ready.up(), 1)
                last = bass.ds(g * GRP + GRP - 1, 1)
                nc.vector.tensor_scalar(hot[:, b, 1, GRP - 1, :], iota[:, :], slots_T[:, 1, last],
                                        slots_T[:, 2, last], ALU.is_equal, ALU.mult).then_inc(k.more_onehots.up(), 1)

            def scale(act, g, b):
                act.wait_ge(k.onehots_ready.sem, k.onehots_ready.at(g + 1))
                for t in range(GRP - 1):
                    ins = nc.scalar.activation(hot[:, b, 1, t, :], hot[:, b, 1, t, :], ACT.Copy,
                                               scale=slots_T[:, 2, bass.ds(g * GRP + t, 1)])
                ins.then_inc(k.onehots_gated.up(), 1)

            def outer(pe, g, b, wait):
                pe.wait_ge(k.more_onehots.sem, k.more_onehots.at(g + 1))
                pe.wait_ge(k.onehots_gated.sem, k.onehots_gated.at(g + 1))
                if wait:
                    pe.wait_ge(k.gates_placed.sem, k.gates_placed.at(g - BUF + 1))
                for t in range(GRP):
                    last = mm(k, k.ps[:, b, t * P:(t + 1) * P], hot[:, b, 0, t, :], hot[:, b, 1, t, :])
                last.then_inc(k.products.up(), 1)

            def place(act, g, b):
                act.wait_ge(k.products.sem, k.products.at(g + 1))
                nc.scalar.activation(gates[:, :, bass.ds(g * GRP, GRP)],
                                     k.ps[:, b, :].rearrange("p (t n) -> p n t", t=GRP),
                                     ACT.Copy).then_inc(k.gates_placed.up(), 1)

            @block.vector
            def _(dve):
                for b in range(BUF):
                    hots(dve, b, b, False)
                with dve.Fori(1, turns) as i:
                    for b in range(BUF):
                        hots(dve, BUF * i + b, b, True)
                for sig in (k.onehots_ready, k.more_onehots):
                    sig.repeated(turns - 1, BUF)

            @block.tensor
            def _(pe):
                for b in range(BUF):
                    outer(pe, b, b, False)
                with pe.Fori(1, turns) as i:
                    for b in range(BUF):
                        outer(pe, BUF * i + b, b, True)
                k.products.repeated(turns - 1, BUF)

            @block.scalar
            def _(act):
                for b in range(BUF):
                    scale(act, b, b)
                    if b:
                        place(act, b - 1, b - 1)
                with act.Fori(1, turns) as i:
                    for b in range(BUF):
                        scale(act, BUF * i + b, b)
                        place(act, BUF * i + b - 1, (b - 1) % BUF)
                for sig in (k.onehots_gated, k.gates_placed):
                    sig.repeated(turns - 1, BUF)
                place(act, BUF * turns - 1, BUF - 1)

def load_key(k, sp, raw, which, key, b):
    src = k.dram[("peer_u_T", "peer_v_rows")[which]][bass.ds(key, 1)].rearrange("a p n -> p (a n)")
    sp.dma_start(raw[which][:, b, :], src).then_inc(k.key_landed[which][b], 16)

def peer_experts(k, gates, raw, hT_keep):
    nc = k.nc
    with ExitStack() as c, ExitStack() as c2:
        hT_high, hT_low = (k.sb(f"peer_input_{n}", [P, DC, S], F32R, ctx=c) for n in ("high", "low"))
        parts = [[k.sb(f"{m}_{n}", [P, 2, D], F32R, ctx=c) for n in ("high", "low")] for m in "uv"]
        hT = k.sb("peer_input_T_again", [P, DC, S], ctx=c2)
        load_small(k, [(hT[:, :, :], hT_keep)])
        with k.stage() as block:
            @block.scalar
            def _(act):
                nc.scalar.activation(hT_high[:, :, :], hT[:, :, :], ACT.Copy).then_inc(k.act_ready.up(), 1)

            @block.vector
            def _(dve):
                dve.wait_ge(k.act_ready.sem, k.act_ready.at(1))
                nc.vector.tensor_tensor(hT_low[:, :, :], hT[:, :, :], hT_high[:, :, :],
                                        ALU.subtract).then_inc(k.dve_step.up(), 1)
        c2.close()
        gelu, w = (k.sb(n, [P, 2, S], ctx=c) for n in ("gelu_out", "gated"))
        w_high, w_low = (k.sb(n, [P, 2, S], F32R, ctx=c) for n in ("gated_high", "gated_low"))
        peer_steps(k, gates, raw, parts, hT_high, hT_low, gelu, w, w_high, w_low)

def peer_steps(k, gates, raw, parts, hT_high, hT_low, gelu, w, w_high, w_low):
    nc = k.nc
    as_u = lambda t, b: t[:, b, :].rearrange("p (c e) -> p c e", c=DC)
    TURN = 4
    turns = PK // TURN
    FIRST, LAST = 0, turns - 1

    with k.stage() as block:
        def pre(pe, n, b, start):
            pe.wait_ge(k.u_low_ready.sem, k.u_low_ready.at(n + 1))
            if not start:
                pe.wait_ge(k.act_ready.sem, k.act_ready.at(n - 3))
            out = k.ps[:, 4 + b, 0:S]
            for ch in range(DC):
                high, low = (as_u(t, b % 2)[:, ch, :] for t in parts[0])
                h_high, h_low = hT_high[:, ch, :], hT_low[:, ch, :]
                mm(k, out, high, h_high, ch == 0, False)
                mm(k, out, high, h_low, False, False)
                last = mm(k, out, low, h_high, False, ch == DC - 1)
            last.then_inc(k.products.up(), 1)

        def post(pe, n, b, first_one, last_one):
            pe.wait_ge(k.v_low_ready.sem, k.v_low_ready.at(n + 1))
            pe.wait_ge(k.weights_gated.sem, k.weights_gated.at(n + 1))
            for tt in range(NT):
                tok = slice(tt * P, (tt + 1) * P)
                for half in range(2):
                    cols = slice(half * 512, (half + 1) * 512)
                    out = k.ps[:, 2 * tt + half, :]
                    v_high, v_low = (t[:, b % 2, cols] for t in parts[1])
                    mm(k, out, w_high[:, b % 2, tok], v_high, first_one, False)
                    mm(k, out, w_high[:, b % 2, tok], v_low, False, False)
                    last = mm(k, out, w_low[:, b % 2, tok], v_high, False, last_one)
            last.then_inc(k.down_products.up(), 1)

        def pe_turn(pe, i):
            for b in range(TURN):
                n = TURN * i + b
                if i is not LAST or b < 2:
                    pre(pe, n + 2, (b + 2) % TURN, i is FIRST and b < 2)
                post(pe, n, b, i is FIRST and b == 0, i is LAST and b == TURN - 1)

        def act_gelu(act, n, b, start):
            act.wait_ge(k.products.sem, k.products.at(n + 1))
            if not start:
                act.wait_ge(k.weights_gated.sem, k.weights_gated.at(n - 1))
            nc.scalar.activation(gelu[:, b % 2, :], k.ps[:, 4 + b, 0:S], ACT.Gelu).then_inc(k.act_ready.up(), 1)

        def high(act, which, n, i, b, start):
            act.wait_ge(k.key_landed[which][b % 2], 16 * (TURN // 2 * i + b // 2 + 1))
            used, ready = ((k.products, k.u_high_ready), (k.down_products, k.v_high_ready))[which]
            if not start:
                act.wait_ge(used.sem, used.at(n - 1))
            nc.scalar.activation(parts[which][0][:, b % 2, :], raw[which][:, b % 2, :],
                                 ACT.Copy).then_inc(ready.up(), 1)

        def low(dve, which, n, b):
            high_ready, ready = ((k.u_high_ready, k.u_low_ready), (k.v_high_ready, k.v_low_ready))[which]
            dve.wait_ge(high_ready.sem, high_ready.at(n + 1))
            part_high, part_low = parts[which]
            nc.vector.tensor_tensor(part_low[:, b % 2, :], raw[which][:, b % 2, :], part_high[:, b % 2, :],
                                    ALU.subtract).then_inc(ready.up(), 1)

        def gate(dve, n, b, start):
            dve.wait_ge(k.act_ready.sem, k.act_ready.at(n + 1))
            if not start:
                dve.wait_ge(k.down_products.sem, k.down_products.at(n - 1))
            g = gates[:, bass.ds(n, 1), :].rearrange("p a t -> p (a t)")
            nc.vector.tensor_tensor(w_high[:, b % 2, :], gelu[:, b % 2, :], g,
                                    ALU.mult).then_inc(k.dve_step.up(), 1)
            nc.vector.tensor_tensor(w[:, b % 2, :], gelu[:, b % 2, :], g, ALU.mult).then_inc(k.dve_step.up(), 1)
            dve.wait_ge(k.dve_step.sem, k.dve_step.at(2 * n + 2))
            nc.vector.tensor_tensor(w_low[:, b % 2, :], w[:, b % 2, :], w_high[:, b % 2, :],
                                    ALU.subtract).then_inc(k.weights_gated.up(), 1)

        def act_step(act, i, b):
            n = TURN * i + b
            later = lambda d: (i + (b + d) // TURN, (b + d) % TURN)
            if i is not LAST or b + 1 < TURN:
                i1, b1 = later(1)
                act_gelu(act, n + 1, b1, i is FIRST and b + 1 < 2)
                high(act, 1, n + 1, i1, b1, i is FIRST and b + 1 < 2)
            if i is not LAST or b + 3 < TURN:
                i3, b3 = later(3)
                high(act, 0, n + 3, i3, b3, i is FIRST and b + 3 < 2)

        def dve_step(dve, i, b):
            n = TURN * i + b
            if i is not LAST or b + 1 < TURN:
                gate(dve, n + 1, (b + 1) % TURN, i is FIRST and b + 1 < 2)
                low(dve, 1, n + 1, (b + 1) % TURN)
            if i is not LAST or b + 3 < TURN:
                low(dve, 0, n + 3, (b + 3) % TURN)

        @block.sync
        def _(sp):
            def reload(n, b):
                sp.wait_ge(k.u_low_ready.sem, k.u_low_ready.at(n + 1))
                load_key(k, sp, raw, 0, n + 2, b)
                sp.wait_ge(k.v_low_ready.sem, k.v_low_ready.at(n + 1))
                load_key(k, sp, raw, 1, n + 2, b)
            with sp.Fori(0, PK // 2 - 1) as i:
                for b in range(2):
                    reload(2 * i + b, b)

        @block.tensor
        def _(pe):
            pre(pe, 0, 0, True)
            pre(pe, 1, 1, True)
            pe_turn(pe, FIRST)
            with pe.Fori(1, LAST) as i:
                pe_turn(pe, i)
            for sig in (k.products, k.down_products):
                sig.repeated(turns - 2, TURN)
            pe_turn(pe, LAST)

        @block.scalar
        def _(act):
            high(act, 0, 0, 0, 0, True)
            high(act, 0, 1, 0, 1, True)
            act_gelu(act, 0, 0, True)
            high(act, 1, 0, 0, 0, True)
            high(act, 0, 2, 0, 2, False)
            for b in range(TURN):
                act_step(act, FIRST, b)
            with act.Fori(1, LAST) as i:
                for b in range(TURN):
                    act_step(act, i, b)
            for sig in (k.act_ready, k.u_high_ready, k.v_high_ready):
                sig.repeated(turns - 2, TURN)
            for b in range(TURN):
                act_step(act, LAST, b)

        @block.vector
        def _(dve):
            low(dve, 0, 0, 0)
            low(dve, 0, 1, 1)
            gate(dve, 0, 0, True)
            low(dve, 1, 0, 0)
            low(dve, 0, 2, 2)
            for b in range(TURN):
                dve_step(dve, FIRST, b)
            with dve.Fori(1, LAST) as i:
                for b in range(TURN):
                    dve_step(dve, i, b)
            for sig in (k.weights_gated, k.u_low_ready, k.v_low_ready):
                sig.repeated(turns - 2, TURN)
            k.dve_step.repeated(turns - 2, 2 * TURN)
            for b in range(TURN):
                dve_step(dve, LAST, b)
    k.stream.restart, k.stream.hold = k.stream.hold, None

def first_block(k, tiles):
    nc, sb = k.nc, k.sb
    keep, hT_keep = k.dram["x_rows"], k.dram["h_T"]
    with ExitStack() as c:
        x = sb("x", [P, NT, D], ctx=c)
        first_block_attention(k, x, tiles)
        hT = sb("peer_input_T", [P, DC, S], ctx=c)
        f = sb("x_factors", [P, NT], ctx=c)
        with ExitStack() as c2:
            y = sb("normed_x", [P, NT, D], ctx=c2)
            row_rsqrt(k, [(x[:, :, :], f[:, :])], 1e-6)
            with k.stage() as block:
                @block.vector
                def _(dve):
                    for tt in range(NT):
                        nc.vector.tensor_scalar(y[:, tt, :], x[:, tt, :], f[:, tt:tt + 1], None,
                                                ALU.mult).then_inc(k.dve_step.up(), 1)
            turn(k, y, DC, hT, lambda ch: k.col("g_ffn", ch))
        store(k, [(keep, x[:, :, :]), (hT_keep, hT[:, :, :])])
        slots_T = sb("slots_T", [P, 3, S], ctx=c)
        peer_routing(k, hT, tiles, slots_T)
        store(k, [(k.dram["slots"], slots_T[:, :, :])])
    k.ring_place.close()
    with ExitStack() as c:
        gates = sb("gates", [P, PK, S], ctx=c)
        raw = [sb(f"{n}_of_key", [P, 2, D], ctx=c) for n in "uv"]
        with ExitStack() as c2:
            slots_T = sb("slots_T_again", [P, 3, S], ctx=c2)
            load_small(k, [(slots_T[:, :, :], k.dram["slots"])])
            peer_gates(k, slots_T, gates, raw)
        peer_experts(k, gates, raw, hT_keep)
    k.place_ring()

def store(k, pairs, wait=True):
    with k.stage() as block:
        @block.scalar
        def _(act):
            for dst, src in pairs:
                act.dma_start(dst, src).then_inc(k.rows_stored.up(16), 16)
            if wait:
                act.wait_ge(k.rows_stored.sem, k.rows_stored.at(16 * len(pairs)))

def rwkv_and_gating(k, tiles, hT, cat_T):
    nc, sb = k.nc, k.sb
    W = RW_H * S
    with ExitStack() as c:
        AR = sb("rw_A_R", [64, RW_H, NCH, 2, CH], ctx=c)
        Bt = sb("rw_B_then_T", [64, W], ctx=c)
        Kt = sb("rw_K_then_T_T", [64, W], ctx=c)
        VN = sb("rw_V_rows", [64, NCH, RW_H, 64], ctx=c)
        sgl = sb("rw_gate_low", [P, S], ctx=c)
        decay_end = sb("rw_chunk_decay", [64, RW_H, NCH], ctx=c)
        bonus = sb("rw_bonus", [64, NCH * RW_H], ctx=c)
        pu = sb("sg_u", [P, NT, 512], ctx=c)
        pv = sb("sg_v", [P, NT, 512], ctx=c)
        hv = lambda t: t.rearrange("p (h t) -> p h t", h=RW_H)
        with ExitStack() as c2:
            r, kx, vx, ax, lw, cum, ex = (sb(n, [64, W], ctx=c2)[:, :] for n in
                                          ("rw_r", "rw_k", "rw_v", "rw_a", "rw_log_decay", "rw_cum", "rw_exp"))
            lora = sb("rw_lora", [64, 2, S], ctx=c2)
            low = sb("rw_lora_up", [64, 2, 512], ctx=c2)
            units = []
            t0 = tiles["ab_in"]
            for j, dst in enumerate((r, kx, vx)):
                for m in range(4):
                    d = hv(dst)
                    units.append(feature_products(k, hT, DC, t0 + j, 512, m * P, P,
                                                  [(d[:, 2 * m, :], 0, 64), (d[:, 2 * m + 1, :], 64, 64)],
                                                  "va"[m % 2]))
            units.append(feature_products(k, hT, DC, t0 + 3, 256, 0, P,
                                          [(lora[:, 0, :], 0, 64), (lora[:, 1, :], 64, 64)], "v"))
            units.append(feature_products(k, hT, DC, t0 + 3, 256, P, P, [(sgl[:, :], 0, P)], "a"))
            for j, dst in enumerate((pu, pv)):
                units += token_products(k, hT, DC, t0 + 4 + j, 512, 0, 512, lambda tt, dst=dst: dst[:, tt, :])
            run_products(k, units, (t0, t0 + 6))

            with k.stage() as block:
                @block.vector
                def _(dve):
                    v = nc.vector

                    def shift(dst, g, rows, mus):
                        d = dst.rearrange("p (g t) -> p g t", g=g)
                        e = (sg_tmp if rows == P else ex)[0:rows, 0:g * S].rearrange("p (g t) -> p g t", g=g)
                        k.v(v.tensor_tensor(e[:, :, 1:S], d[:, :, 0:S - 1], d[:, :, 1:S], ALU.subtract))
                        k.v(v.tensor_scalar(e[:, :, 0:1], d[:, :, 0:1], -1.0, None, ALU.mult))
                        for i in range(g):
                            v.scalar_tensor_tensor(out=d[:, i, :], in0=e[:, i, :], scalar=mus(i), in1=d[:, i, :],
                                                   op0=ALU.mult, op1=ALU.add).then_inc(k.dve_step.up(), 1)
                        v.wait_ge(k.dve_step.sem, k.dve_step.count)
                    sg_tmp = cat_T[:, 0, :]
                    for n, dst in enumerate((r, kx, vx)):
                        shift(dst, RW_H, 64, lambda i, n=n: k.col("mu_rkv", 8 * n + i, 64))
                    shift(lora[:, :, :].rearrange("p a t -> p (a t)"), 2, 64, lambda i: k.col("mu_rkv", 24 + i, 64))
                    shift(sgl[:, :], 1, P, lambda i: k.col("mu_g", 13))

                @block.scalar
                def _(act):
                    act.dma_start(low[:, 0, :], k.dram["rw_w2_2"].rearrange("a p n -> (a p) n")
                                  ).then_inc(k.small_loaded.up(16), 16)
                    act.dma_start(low[:, 1, :], k.dram["rw_a2_2"].rearrange("a p n -> (a p) n")
                                  ).then_inc(k.small_loaded.up(16), 16)
                    act.wait_ge(k.small_loaded.sem, k.small_loaded.at(32))
                    act.wait_ge(k.dve_step.sem, k.dve_step.count)
                    nc.scalar.activation(lora[:, 0, :], lora[:, 0, :], ACT.Tanh).then_inc(k.act_step.up(), 1)
                    nc.scalar.activation(sgl[:, :], sgl[:, :], ACT.Sigmoid).then_inc(k.act_step.up(), 1)

            def squashed(dst, h, name):
                def go(eng, ps):
                    return nc.scalar.activation(hv(dst)[:, h, :], ps[0:64, 0:S], ACT.Sigmoid,
                                                bias=k.col(name, h, 64))
                return go
            units = []
            for n, (dst, name) in enumerate(((lw, "w0"), (ax, "a0"))):
                for h in range(RW_H):
                    units.append((None, [lambda ps, n=n, h=h: mm(k, ps[0:64, 0:S], low[:, n, h * 64:(h + 1) * 64],
                                                                 lora[:, n, :])], "a", [squashed(dst, h, name)]))
            run_products(k, units)

            with ExitStack() as c3:
                reset = sb("rw_chunk_resets", [64, W], ctx=c3)
                load_small(k, [(reset[:, :], k.const("reset", 64))])
                with k.stage() as block:
                    @block.vector
                    def _(dve):
                        v = nc.vector
                        k.v(v.tensor_scalar(lw, lw, -math.exp(-0.5), None, ALU.mult))
                        k.v(v.tensor_tensor_scan(cum, reset[:, :], lw, 0.0, ALU.mult, ALU.add))
                        for h in range(RW_H):
                            v.tensor_scalar(hv(ex)[:, h, :], hv(kx)[:, h, :], k.col("k_k", h, 64), None,
                                            ALU.mult).then_inc(k.dve_step.up(), 1)
                        v.wait_ge(k.dve_step.sem, k.dve_step.count)
                        k.v(v.tensor_tensor(reset[:, :], ex, ex, ALU.mult))
                ones = sb("rw_ones", [64, 64], ctx=c3)
                load_small(k, [(ones[:, :], k.const("ones", 64)[:, 0:64])])
                run_products(k, [(None, [lambda ps, n=n: mm(k, ps[0:64, :], ones[:, :],
                                                            reset[:, n * 512:(n + 1) * 512])], "a",
                                  [lambda eng, ps, n=n: nc.scalar.activation(Bt[:, n * 512:(n + 1) * 512],
                                                                             ps[0:64, :], ACT.Sqrt)])
                                 for n in range(W // 512)])
                with k.stage() as block:
                    @block.vector
                    def _(dve):
                        v = nc.vector
                        k.v(v.tensor_scalar(Bt[:, :], Bt[:, :], 1e-12, None, ALU.max))
                        k.v(v.reciprocal(Bt[:, :], Bt[:, :]))
                        k.v(v.tensor_tensor(ex, ex, Bt[:, :], ALU.mult))
                        for h in range(RW_H):
                            v.tensor_scalar(hv(reset[:, :])[:, h, :], hv(ax)[:, h, :], 1.0, k.col("k_a", h, 64),
                                            ALU.subtract, ALU.mult).then_inc(k.dve_step.up(), 1)
                        v.wait_ge(k.dve_step.sem, k.dve_step.count)
                        k.v(v.scalar_tensor_tensor(out=kx, in0=reset[:, :], scalar=1.0, in1=kx,
                                                   op0=ALU.add, op1=ALU.mult))
                        k.v(v.tensor_tensor(reset[:, :], r, kx, ALU.mult))
                        v.tensor_tensor(lw, cum, lw, ALU.subtract).then_inc(k.shift_ready.up(), 1)
                        k.v(v.tensor_tensor(ax, ax, ex, ALU.mult))
                        dve.wait_ge(k.exps_ready.sem, k.exps_ready.at(1))
                        part = lambda i: AR[:, :, :, i, :].rearrange("p h c t -> p (h c) t")
                        ch = lambda t: t.rearrange("p (g t) -> p g t", t=CH)
                        k.v(v.scalar_tensor_tensor(out=part(0), in0=ch(ex), scalar=-1.0, in1=ch(lw),
                                                   op0=ALU.mult, op1=ALU.mult))
                        dve.wait_ge(k.exps_ready.sem, k.exps_ready.at(2))
                        k.v(v.tensor_tensor(Bt[:, :], ax, Kt[:, :], ALU.mult))
                        k.v(v.tensor_tensor(Kt[:, :], kx, Kt[:, :], ALU.mult))
                        dve.wait_ge(k.exps_ready.sem, k.exps_ready.at(3))
                        k.v(v.tensor_tensor(part(1), ch(r), ch(cum), ALU.mult))
                        k.v(v.tensor_copy(decay_end[:, :, :].rearrange("p h c -> p (h c)"),
                                          ch(cum)[:, :, CH - 1]))

                    @block.scalar
                    def _(act):
                        act.wait_ge(k.shift_ready.sem, k.shift_ready.at(1))
                        for out, src, s in ((lw, lw, 1.0), (Kt[:, :], cum, -1.0), (cum, cum, 1.0)):
                            nc.scalar.activation(out, src, ACT.Exp, scale=s).then_inc(k.exps_ready.up(), 1)
                units = []
                for n in range(2):
                    units.append((None, [lambda ps, i=i, n=n: mm(
                        k, ps[0:64, i:i + 1], hv(reset[:, :])[:, (16 * n + i) % RW_H,
                                                             (16 * n + i) // RW_H * CH:((16 * n + i) // RW_H + 1) * CH],
                        k.col("r_k", (16 * n + i) % RW_H, 64)) for i in range(16)], "v",
                        [copy_out(k, bonus[:, 16 * n:16 * n + 16], 64, 16)]))
                units += chunk_rows(k, vx, VN)
                run_products(k, units)

        with ExitStack() as c2:
            rows = sb("sg_norm_rows", [P, 2, 512], ctx=c2)
            wT = sb("sg_weights_T", [P, SG, P], ctx=c2)
            stt = sb("sg_sums", [P, NT * SG], ctx=c2)
            var = sb("sg_vars", [P, NT * SG], ctx=c2)
            sq = sb("sg_squares", [P, NT * SG, P], ctx=c2)
            z = pv[:, :, :].rearrange("p t (g n) -> p (t g) n", g=SG)
            bc = lambda t: t.unsqueeze(2).to_broadcast([P, NT * SG, P])
            with k.stage() as block:
                @block.scalar
                def _(act):
                    act.dma_start(rows[:, 0, :], k.dram["sg_ln_g_2"].rearrange("a g n -> (a g n)")
                                  .partition_broadcast(P)).then_inc(k.small_loaded.up(16), 16)
                    act.dma_start(rows[:, 1, :], k.dram["sg_ln_b_2"].rearrange("a g n -> (a g n)")
                                  .partition_broadcast(P)).then_inc(k.small_loaded.up(16), 16)
                    act.dma_start(wT[:, :, :], k.dram["sg_ws_T"]).then_inc(k.small_loaded.up(16), 16)
                    for t in (pv, pu):
                        nc.scalar.activation(t[:, :, :], t[:, :, :], ACT.Gelu_apprx_tanh
                                             ).then_inc(k.act_step.up(), 1)
                    act.wait_ge(k.shift_ready.sem, k.shift_ready.at(1))
                    nc.scalar.activation(var[:, :], var[:, :], ACT.Sqrt).then_inc(k.act_step.up(), 1)

                @block.gpsimd
                def _(pool):
                    pool.wait_ge(k.small_loaded.sem, k.small_loaded.at(48))
                    nc.gpsimd.affine_select(out=wT[:, :, :], in_=wT[:, :, :], pattern=[[0, SG], [1, P]],
                                            compare_op=ALU.is_ge, fill=0.0, base=0, channel_multiplier=-1
                                            ).then_inc(k.gated_ready.up(), 1)
                    pool.wait_ge(k.gated_ready.sem, k.gated_ready.at(1))

                @block.vector
                def _(dve):
                    v = nc.vector
                    dve.wait_ge(k.act_step.sem, k.act_step.at(2))
                    k.v(v.tensor_reduce(stt[:, :], z, AX, ALU.add))
                    k.v(v.tensor_scalar(stt[:, :], stt[:, :], 1.0 / P, None, ALU.mult))
                    k.v(v.tensor_tensor(z, z, bc(stt[:, :]), ALU.subtract))
                    k.v(v.tensor_tensor(sq[:, :, :], z, z, ALU.mult))
                    k.v(v.tensor_reduce(var[:, :], sq[:, :, :], AX, ALU.add))
                    v.tensor_scalar(var[:, :], var[:, :], 1.0 / P, 1e-5, ALU.mult,
                                    ALU.add).then_inc(k.shift_ready.up(), 1)
                    dve.wait_ge(k.small_loaded.sem, k.small_loaded.at(48))
                    dve.wait_ge(k.act_step.sem, k.act_step.at(3))
                    k.v(v.reciprocal(var[:, :], var[:, :]))
                    k.v(v.tensor_tensor(z, z, bc(var[:, :]), ALU.mult))
                    for tt in range(NT):
                        k.v(v.tensor_tensor(pv[:, tt, :], pv[:, tt, :], rows[:, 0, :], ALU.mult))
                        k.v(v.tensor_tensor(pv[:, tt, :], pv[:, tt, :], rows[:, 1, :], ALU.add))
            units = []
            for tt in range(NT):
                def gate(g, tt=tt):
                    def go(eng, ps):
                        col = slice(g * P, (g + 1) * P)
                        return nc.vector.scalar_tensor_tensor(out=pu[:, tt, col], in0=ps[:, col],
                                                              scalar=k.col("sg_b", g), in1=pu[:, tt, col],
                                                              op0=ALU.add, op1=ALU.mult)
                    return go
                units.append((None, [lambda ps, g=g, tt=tt: mm(k, ps[:, g * P:(g + 1) * P], wT[:, g, :],
                                                               pv[:, tt, g * P:(g + 1) * P]) for g in range(SG)],
                              "v", [gate(g) for g in range(SG)]))
            run_products(k, units)
        turn(k, pu, 4, cat_T[:, 4:8, :])

        BN = sb("rw_B_rows", [64, NCH, RW_H, 64], ctx=c)
        KN = sb("rw_K_rows", [64, NCH, RW_H, 64], ctx=c)
        LB = sb("rw_lower_B", [64, NCH * RW_H, 2 * CH], ctx=c)
        LK = sb("rw_lower_K", [64, NCH * RW_H, 2 * CH], ctx=c)
        X = sb("rw_level_product", [64, W], ctx=c)
        Lm = sb("rw_level_part", [64, W], ctx=c)
        lv = sb("rw_levels", [64, 6, CH], ctx=c)
        tri = sb("rw_triangles", [64, 2 * CH], ctx=c)
        load_small(k, [(lv[:, :, :].rearrange("p a b -> p (a b)"), k.const("levels", 64)), (tri[:, :], k.const("tri", 64))])
        units = chunk_rows(k, Bt[:, :], BN) + chunk_rows(k, Kt[:, :], KN)
        for src, dst in ((Bt, LB), (Kt, LK)):
            for g in range(8):
                def masked(eng, ps, dst=dst, g=g):
                    return nc.vector.tensor_tensor(dst[:, 4 * g:4 * g + 4, :],
                                                   ps[0:64, :].rearrange("p (a b) -> p a b", a=4),
                                                   tri[:, :].unsqueeze(1).to_broadcast([64, 4, 2 * CH]), ALU.mult)
                def prod(ps, a, src=src, g=g):
                    ci, h = divmod(4 * g + a, RW_H)
                    return mm(k, ps[0:64, a * P:(a + 1) * P], hv(src[:, :])[:, h, ci * CH:(ci + 1) * CH],
                              AR[:, h, ci, :, :].rearrange("p a t -> p (a t)"))
                units.append((None, [lambda ps, a=a, prod=prod: prod(ps, a) for a in range(4)], "v", [masked]))
        run_products(k, units)

        T, TT = Bt, Kt
        pairs = NCH * RW_H
        q = lambda t: t[:, :].rearrange("p (g n) -> p g n", g=pairs)
        with k.stage() as block:
            @block.vector
            def _(dve):
                v = nc.vector
                eye = k.ident[0:64, 0:64].unsqueeze(1).to_broadcast([64, pairs, 64])
                v.tensor_copy(q(T), eye).then_inc(k.dve_step.up(), 1)
                v.tensor_copy(q(TT), eye).then_inc(k.dve_step.up(), 1)
        for level in range(6):
            with k.stage() as block:
                @block.vector
                def _(dve):
                    nc.vector.tensor_tensor(q(Lm), LB[:, :, 0:CH],
                                            lv[:, level, :].unsqueeze(1).to_broadcast([64, pairs, CH]),
                                            ALU.mult).then_inc(k.dve_step.up(), 1)
            run_products(k, [(None, [lambda ps, i=i, g=g: mm(k, ps[0:64, i * 64:(i + 1) * 64], q(Lm)[:, 8 * g + i, :],
                                                             q(T)[:, 8 * g + i, :]) for i in range(8)], "va"[g % 2],
                              [copy_out(k, X[:, g * 512:(g + 1) * 512], 64, 512)]) for g in range(4)])

            def added(dst, g):
                def go(eng, ps):
                    d = dst[:, g * 512:(g + 1) * 512]
                    return nc.vector.tensor_tensor(d, d, ps[0:64, :], ALU.add)
                return go
            units = []
            for g in range(4):
                units.append((None, [lambda ps, i=i, g=g: mm(k, ps[0:64, i * 64:(i + 1) * 64], q(X)[:, 8 * g + i, :],
                                                             q(TT)[:, 8 * g + i, :]) for i in range(8)], "v", []))
                units.append((None, [lambda ps, i=i, g=g: mm(k, ps[0:64, i * 64:(i + 1) * 64], q(TT)[:, 8 * g + i, :],
                                                             q(X)[:, 8 * g + i, :]) for i in range(8)], "v",
                              [lambda eng, ps, g=g: added(T, g)(eng, ps),
                               lambda eng, ps, g=g: added(TT, g)(eng, k.ps[:, 2 * g, :])]))
            run_products(k, units)

        gn = sb("rw_gn_rows", [64, 2, 512], ctx=c)
        Y = sb("rw_y", [64, NCH, RW_H, 64], ctx=c)
        U = sb("rw_U", [64, 512], ctx=c)
        SA = sb("rw_SA", [64, 512], ctx=c)
        ST = sb("rw_state_T", [64, RW_H, 64], ctx=c)
        hs = lambda h: slice(h * 64, (h + 1) * 64)
        with k.stage() as block:
            @block.tensor
            def _(pe):
                for ci in range(NCH):
                    A = lambda h: AR[:, h, ci, 0, :]
                    R = lambda h: AR[:, h, ci, 1, :]
                    if ci:
                        pe.wait_ge(k.hidden_ready.sem, k.hidden_ready.at(2 * ci))
                    for h in range(RW_H):
                        if ci:
                            mm(k, k.ps[0:64, 0, hs(h)], A(h), ST[:, h, :], True, False)
                        last = mm(k, k.ps[0:64, 0, hs(h)], LK[:, ci * RW_H + h, 0:CH], VN[:, ci, h, :], not ci, True)
                    last.then_inc(k.products.up(), 1)
                    pe.wait_ge(k.act_ready.sem, k.act_ready.at(3 * ci + 1))
                    for h in range(RW_H):
                        last = mm(k, k.ps[0:64, 1, hs(h)], q(TT)[:, ci * RW_H + h, :], U[:, hs(h)])
                    last.then_inc(k.products.up(), 1)
                    pe.wait_ge(k.act_ready.sem, k.act_ready.at(3 * ci + 2))
                    for h in range(RW_H):
                        mm(k, k.ps[0:64, 2, hs(h)], BN[:, ci, h, :], SA[:, hs(h)], True, False)
                        last = mm(k, k.ps[0:64, 2, hs(h)], KN[:, ci, h, :], VN[:, ci, h, :], False, True)
                    last.then_inc(k.products.up(), 1)
                    for h in range(RW_H):
                        if ci:
                            mm(k, k.ps[0:64, 3, hs(h)], R(h), ST[:, h, :], True, False)
                        mm(k, k.ps[0:64, 3, hs(h)], LB[:, ci * RW_H + h, CH:2 * CH], SA[:, hs(h)], not ci, False)
                        last = mm(k, k.ps[0:64, 3, hs(h)], LK[:, ci * RW_H + h, CH:2 * CH], VN[:, ci, h, :], False, True)
                    last.then_inc(k.products.up(), 1)

            @block.scalar
            def _(act):
                act.dma_start(gn[:, 0, :], k.dram["rw_gn_g_2"].rearrange("a n -> (a n)").partition_broadcast(64)
                              ).then_inc(k.small_loaded.up(16), 16)
                act.dma_start(gn[:, 1, :], k.dram["rw_gn_b_2"].rearrange("a n -> (a n)").partition_broadcast(64)
                              ).then_inc(k.small_loaded.up(16), 16)
                act.wait_ge(k.small_loaded.sem, k.small_loaded.at(32))
                for ci in range(NCH):
                    for n, dst in enumerate((U[:, :], SA[:, :], Y[:, ci, :, :].rearrange("p h n -> p (h n)"))):
                        bank = (0, 1, 3)[n]
                        act.wait_ge(k.products.sem, k.products.at(4 * ci + (1, 2, 4)[n]))
                        nc.scalar.activation(dst, k.ps[0:64, bank, :], ACT.Copy).then_inc(k.act_ready.up(), 1)

            @block.vector
            def _(dve):
                v = nc.vector
                for ci in range(NCH):
                    flat = ST[:, :, :].rearrange("p h n -> p (h n)")
                    dve.wait_ge(k.products.sem, k.products.at(4 * ci + 4))
                    if ci:
                        v.tensor_tensor(flat, flat, k.ps[0:64, 2, :], ALU.add).then_inc(k.hidden_ready.up(), 1)
                    else:
                        v.tensor_copy(flat, k.ps[0:64, 2, :]).then_inc(k.hidden_ready.up(), 1)
                    v.wait_ge(k.hidden_ready.sem, k.hidden_ready.at(2 * ci + 1))
                    dve.wait_ge(k.act_ready.sem, k.act_ready.at(3 * ci + 3))
                    v.tensor_tensor(ST[:, :, :], ST[:, :, :], decay_end[:, :, ci:ci + 1].to_broadcast([64, RW_H, 64]),
                                    ALU.mult).then_inc(k.hidden_ready.up(), 1)

        with ExitStack() as c2:
            g2 = pu[:, 0, :]
            load_small(k, [(g2, k.dram["rw_g2_2"].rearrange("a p n -> (a p) n"))])
            mean = sb("rw_means", [64, pairs], ctx=c2)
            var = sb("rw_vars", [64, pairs], ctx=c2)
            y3 = Y[:, :, :, :].rearrange("p c h n -> p (c h) n")
            sq = q(X)
            bc = lambda t: t.unsqueeze(2).to_broadcast([64, pairs, 64])
            bonus_rows = VN[:, :, :, :].rearrange("p c h n -> p (c h) n")
            with k.stage() as block:
                @block.vector
                def _(dve):
                    v = nc.vector
                    k.v(v.tensor_reduce(mean[:, :], y3, AX, ALU.add))
                    k.v(v.tensor_scalar(mean[:, :], mean[:, :], 1.0 / RW_N, None, ALU.mult))
                    k.v(v.tensor_tensor(y3, y3, bc(mean[:, :]), ALU.subtract))
                    k.v(v.tensor_tensor(sq, y3, y3, ALU.mult))
                    k.v(v.tensor_reduce(var[:, :], sq, AX, ALU.add))
                    v.tensor_scalar(var[:, :], var[:, :], 1.0 / RW_N, 64e-5, ALU.mult,
                                    ALU.add).then_inc(k.shift_ready.up(), 1)
                    dve.wait_ge(k.act_step.sem, k.act_step.at(1))
                    k.v(v.reciprocal(var[:, :], var[:, :]))
                    k.v(v.tensor_tensor(y3, y3, bc(var[:, :]), ALU.mult))
                    yc = Y[:, :, :, :].rearrange("p c h n -> p c (h n)")
                    row = lambda n: gn[:, n, :].unsqueeze(1).to_broadcast([64, NCH, 512])
                    k.v(v.tensor_tensor(yc, yc, row(0), ALU.mult))
                    k.v(v.tensor_tensor(yc, yc, row(1), ALU.add))
                    dve.wait_ge(k.window_ready.sem, k.window_ready.at(1))
                    k.v(v.tensor_tensor(y3, y3, bonus_rows, ALU.add))

                @block.gpsimd
                def _(pool):
                    nc.gpsimd.tensor_tensor(bonus_rows, bonus_rows, bc(bonus[:, :]),
                                            ALU.mult).then_inc(k.window_ready.up(), 1)

                @block.scalar
                def _(act):
                    act.wait_ge(k.shift_ready.sem, k.shift_ready.at(1))
                    nc.scalar.activation(var[:, :], var[:, :], ACT.Sqrt).then_inc(k.act_step.up(), 1)

            def gated(ci):
                def go(eng, ps):
                    y = Y[:, ci, :, :].rearrange("p h n -> p (h n)")
                    return nc.vector.tensor_tensor(y, y, ps[0:64, :], ALU.mult)
                return go
            run_products(k, [(None, [lambda ps, ci=ci: mm(k, ps[0:64, :], sgl[:, ci * CH:(ci + 1) * CH], g2)],
                              "v", [gated(ci)]) for ci in range(NCH)])
            turn(k, Y[:, :, :, :].rearrange("p c h n -> p c (h n)"), 4, cat_T, None, CH, NCH)

def chunk_rows(k, src, dst):
    units = []
    for ci in range(NCH):
        trs = [lambda ps, h=h, ci=ci: k.nc.tensor.transpose(
            ps[0:64, h * 64:(h + 1) * 64], src[:, h * S + ci * CH:h * S + (ci + 1) * CH],
            k.ident[0:64, 0:64]) for h in range(RW_H)]
        units.append((None, trs, "va"[ci % 2],
                      [copy_out(k, dst[:, ci, :, :].rearrange("p h n -> p (h n)"), 64, 512)]))
    return units

def mla(k, x, hT, tiles, load_norm):
    nc, sb = k.nc, k.sb
    with ExitStack() as c:
        q_T = sb("mla_q_T", [MLA_QK, MLA_H, S], ctx=c)
        k_T = sb("mla_k_T", [MLA_QK, MLA_H, S], ctx=c)
        kv = sb("mla_kv", [P, NT, 2048], ctx=c)
        with ExitStack() as c2:
            p = sb("mla_p", [P, NT, 544], ctx=c2)
            low_T = sb("mla_low_T", [P, 4, S], ctx=c2)
            f = sb("mla_factors", [P, NT, 2], ctx=c2)
            t0 = tiles["mla_in"]
            units = token_products(k, hT, DC, t0, 512, 0, 512, lambda tt: p[:, tt, 0:512])
            units += token_products(k, hT, DC, t0 + 1, 32, 0, 32, lambda tt: p[:, tt, 512:544])
            run_products(k, units, (t0, t0 + 2))
            jobs = [(p[:, tt, 256 * i:256 * (i + 1)].unsqueeze(1), f[:, tt, i:i + 1])
                    for tt in range(NT) for i in range(2)]
            row_rsqrt(k, jobs, 1e-6)
            scale_groups(k, jobs)
            turn(k, p, 4, low_T, lambda ch: k.col("q_norm", ch))
            q = sb("mla_q", [P, NT, MLA_H * MLA_QK], ctx=c2)
            units = []
            for j in range(3):
                units += token_products(k, low_T[:, 0:2, :], 2, t0 + 2, 1536, 512 * j, 512,
                                        lambda tt, j=j: q[:, tt, 512 * j:512 * (j + 1)])
            for j in range(4):
                units += token_products(k, low_T[:, 2:4, :], 2, t0 + 3, 2048, 512 * j, 512,
                                        lambda tt, j=j: kv[:, tt, 512 * j:512 * (j + 1)])
            run_products(k, units, (t0 + 2, t0 + 4))
            half = MLA_ROPE // 2
            trig = sb("mla_cos_sin", [P, 2, NT, half], ctx=c2)
            tmp = sb("mla_rotated", [P, MLA_H + 1, 2 * half], ctx=c2)
            kf = sb("mla_k", [P, NT, MLA_H, MLA_QK], ctx=c2)
            load_small(k, [(trig[:, n, :, :].rearrange("p a b -> p (a b)"), k.const(s)) for n, s in enumerate(("cos", "sin"))])
            with k.stage() as block:
                @block.vector
                def _(dve):
                    v = nc.vector
                    for tt in range(NT):
                        qs = q[:, tt, :].rearrange("p (h w) -> p h w", h=MLA_H)[:, :, MLA_NOPE:]
                        ks = p[:, tt, 512:544].unsqueeze(1)
                        for a, n, t in ((qs, MLA_H, tmp[:, 0:MLA_H, :]), (ks, 1, tmp[:, MLA_H:, :])):
                            sh = [P, n, half]
                            cs = trig[:, 0, tt, :].unsqueeze(1).to_broadcast(sh)
                            sn = trig[:, 1, tt, :].unsqueeze(1).to_broadcast(sh)
                            a1, a2 = a[:, :, 0:half], a[:, :, half:]
                            k.v(v.tensor_tensor(t[:, :, 0:half], a2, sn, ALU.mult))
                            k.v(v.tensor_tensor(t[:, :, half:], a1, sn, ALU.mult))
                            k.v(v.tensor_tensor(a1, a1, cs, ALU.mult))
                            k.v(v.tensor_tensor(a2, a2, cs, ALU.mult))
                            k.v(v.tensor_tensor(a1, a1, t[:, :, 0:half], ALU.subtract))
                            k.v(v.tensor_tensor(a2, a2, t[:, :, half:], ALU.add))
                        v.tensor_copy(kf[:, tt, :, MLA_NOPE:], ks.to_broadcast([P, MLA_H, MLA_ROPE])
                                      ).then_inc(k.dve_step.up(), 1)
                        v.tensor_copy(kf[:, tt, :, 0:MLA_NOPE], kv[:, tt, :].rearrange(
                            "p (h w) -> p h w", h=MLA_H)[:, :, 0:MLA_NOPE]).then_inc(k.dve_step.up(), 1)
            units = []
            for src, dst, who, s in ((q, q_T, "v", MLA_QK ** -0.5), (kf, k_T, "a", None)):
                for h in range(0, MLA_H, 2):
                    def piece(tt, hh, src=src):
                        if src is q:
                            return q[:, tt, hh * MLA_QK:(hh + 1) * MLA_QK]
                        return kf[:, tt, hh, :]
                    trs = [lambda ps, a=a, tt=tt, h=h, piece=piece: nc.tensor.transpose(
                        ps[0:MLA_QK, a * S + tt * P:a * S + (tt + 1) * P], piece(tt, h + a), k.ident)
                        for a in range(2) for tt in range(NT)]
                    units.append((None, trs, who, [copy_out(k, dst[:, h:h + 2, :].rearrange("p a b -> p (a b)"),
                                                            MLA_QK, 512, s)]))
            run_products(k, units)
        out = sb("mla_out", [P, NT, D], ctx=c)
        mask = sb("mla_causal", [P, NT * S], ctx=c)
        load_small(k, [(mask[:, :], k.const("causal"))])
        attention(k, [([q_T[:, h, :]], [k_T[:, h, :]],
                       lambda kt, h=h: kv[:, kt, h * 128 + MLA_NOPE:(h + 1) * 128], ("masked", mask[:, :]),
                       lambda tt, h=h: out[:, tt, h * MLA_V:(h + 1) * MLA_V]) for h in range(MLA_H)], MLA_V)
        outT = sb("mla_out_T", [P, DC, S], ctx=c)
        load_norm()
        turn(k, out, DC, outT)
        project_residual(k, outT, DC, t0 + 4, x, ALPHA)

def cross_attention(k, x, hT, layer, tiles, load_norm):
    nc, sb = k.nc, k.sb
    t0 = tiles[f"xa{layer}"]
    with ExitStack() as c:
        q_T = sb("xa_q_T", [P, DC, S], ctx=c)
        k_T = sb("xa_k_T", [P, DC, S], ctx=c)
        v = sb("xa_v", [P, NT, D], ctx=c)
        out = sb("xa_out", [P, NT, D], ctx=c)
        load_small(k, [(k_T[:, :, :], k.dram["xa_k_T"][layer]), (v[:, :, :], k.dram["xa_v"][layer])], wait=False)
        units = []
        for j in range(2):
            for m in range(4):
                u = feature_products(k, hT, DC, t0 + j, 512, m * P, P, [(q_T[:, 4 * j + m, :], 0, P)], "va"[m % 2])
                units.append(u[:3] + ([copy_out(k, q_T[:, 4 * j + m, :], P, S, XA_D ** -0.5)],))
        run_products(k, units, (t0, t0 + 2))
        load_small(k, [])
        attention(k, [([q_T[:, 2 * h, :], q_T[:, 2 * h + 1, :]], [k_T[:, 2 * h, :], k_T[:, 2 * h + 1, :]],
                       lambda kt, h=h: v[:, kt, h * XA_D:(h + 1) * XA_D], ("plain", None),
                       lambda tt, h=h: out[:, tt, h * XA_D:(h + 1) * XA_D]) for h in range(XA_H)], XA_D)
        outT = sb("xa_out_T", [P, DC, S], ctx=c)
        load_norm()
        turn(k, out, DC, outT)
        project_residual(k, outT, DC, t0 + 2, x, ALPHA)

def moe(k, x, hT, layer, tiles, router, load_norm):
    nc, sb = k.nc, k.sb
    first = tiles[f"moe{layer}"]
    with ExitStack() as c:
        rows_T = sb("sorted_rows_T", [P, DC, PAIRS + P], ctx=c)
        outs_T = sb("sorted_outputs_T", [P, DC, PAIRS + P], ctx=c)
        spread = sb("gate_of_place", [P, NT, PAIRS], ctx=c)
        table = sb("window_table", [1, 2, WINDOWS + 1], U32, ctx=c)
        with ExitStack() as c2:
            NL = NG + NE
            w, bias, iota, ones = router
            lg = sb("router_logits", [P, NT, NL], ctx=c2)
            g8 = sb("group_logits", [P, NT, 8], ctx=c2)
            top = sb("router_top", [P, NT, 8], ctx=c2)
            at = sb("router_at", [P, NT, 8], U32, ctx=c2)
            atf = sb("router_at_float", [P, NT, 8], ctx=c2)
            neg = sb("router_neg", [P, NT, 1], ctx=c2)
            gsum = sb("router_sum", [P, NT, 1], ctx=c2)
            hot = sb("group_hot", [P, NT, NG], ctx=c2)
            off = sb("group_off", [P, NT, NG], ctx=c2)
            gexp = sb("group_exps", [P, NT, NG], ctx=c2)
            le = sb("expert_logits", [P, NT, NE], ctx=c2)
            e2 = sb("second_exp", [P, NT, 1], ctx=c2)
            g1 = sb("gate_first", [P, NT, 2], ctx=c2)
            one = sb("chosen", [P, 2, NT, NE], ctx=c2)
            both = sb("chosen_both", [P, NT, NE], ctx=c2)
            num = sb("expert_counts", [P, NE], ctx=c2)
            cum = sb("pairs_before", [P, NT, NE], ctx=c2)
            start = sb("expert_starts", [P, NE], ctx=c2)
            win = sb("expert_windows", [P, 4, NE], ctx=c2)
            hit = sb("window_hits", [1, 2, WINDOWS, NE], ctx=c2)
            tf = sb("window_table_float", [1, 2, WINDOWS + 1], ctx=c2)
            place = sb("pair_places_of_token", [P, 2, NT], ctx=c2)
            sel = sb("token_of_place", [P, NT, PAIRS], ctx=c2)
            half2 = sb("second_gate_of_place", [P, PAIRS], ctx=c2)
            run_products(k, [(None, [lambda ps, kk=kk, tt=tt: mm(k, ps[:, 0:NL], hT[:, kk, tt * P:(tt + 1) * P],
                                                                 w[:, kk, :], kk == 0, kk == DC - 1)
                                     for kk in range(DC)], "v",
                              [lambda eng, ps, tt=tt: nc.vector.tensor_tensor(lg[:, tt, :], ps[:, 0:NL], bias[:, :],
                                                                              ALU.add)]) for tt in range(NT)])
            with k.stage() as block:
                @block.vector
                def _(dve):
                    v = nc.vector
                    k.v(v.memset(g8[:, :, :], -3e38))
                    k.v(v.tensor_copy(g8[:, :, 0:NG], lg[:, :, 0:NG]))
                    for tt in range(NT):
                        k.v(v.max(top[:, tt, :], g8[:, tt, :]))
                        k.v(v.max_index(at[:, tt, :], top[:, tt, :], g8[:, tt, :]))
                    k.v(v.tensor_copy(atf[:, :, :], at[:, :, :]))
                    v.tensor_scalar(neg[:, :, :], top[:, :, 0:1], -1.0, None,
                                    ALU.mult).then_inc(k.shift_ready.up(), 1)
                    for tt in range(NT):
                        k.v(v.tensor_scalar(hot[:, tt, :], iota[:, 0:NG], atf[:, tt, 0:1], None, ALU.is_equal))
                    k.v(v.tensor_scalar(off[:, :, :], hot[:, :, :], 1.0, 1e30, ALU.subtract, ALU.mult))
                    for tt in range(NT):
                        e = le[:, tt, :].rearrange("p (g n) -> p g n", g=NG)
                        lt = lg[:, tt, NG:NL].rearrange("p (g n) -> p g n", g=NG)
                        bc = lambda t: t.unsqueeze(2).to_broadcast([P, NG, NPG])
                        k.v(v.tensor_tensor(e, lt, bc(hot[:, tt, :]), ALU.mult))
                        k.v(v.tensor_tensor(e, e, bc(off[:, tt, :]), ALU.add))
                        k.v(v.max(top[:, tt, :], le[:, tt, :]))
                        k.v(v.max_index(at[:, tt, :], top[:, tt, :], le[:, tt, :]))
                    k.v(v.tensor_copy(atf[:, :, :], at[:, :, :]))
                    v.tensor_tensor(e2[:, :, :], top[:, :, 1:2], top[:, :, 0:1],
                                    ALU.subtract).then_inc(k.shift_ready.up(), 1)
                    dve.wait_ge(k.exps_ready.sem, k.exps_ready.at(NT))
                    k.v(v.reciprocal(gsum[:, :, :], gsum[:, :, :]))
                    dve.wait_ge(k.exps_ready.sem, k.exps_ready.at(NT + 1))
                    k.v(v.tensor_scalar(g1[:, :, 0:1], e2[:, :, :], 1.0, None, ALU.add))
                    k.v(v.reciprocal(g1[:, :, 0:1], g1[:, :, 0:1]))
                    k.v(v.tensor_tensor(g1[:, :, 0:1], g1[:, :, 0:1], gsum[:, :, :], ALU.mult))
                    k.v(v.tensor_tensor(g1[:, :, 1:2], g1[:, :, 0:1], e2[:, :, :], ALU.mult))
                    for tt in range(NT):
                        for j in range(2):
                            k.v(v.tensor_scalar(one[:, j, tt, :], iota[:, 0:NE], atf[:, tt, j:j + 1], None,
                                                ALU.is_equal))
                    k.v(v.tensor_tensor(both[:, :, :], one[:, 0, :, :], one[:, 1, :, :], ALU.add))

                @block.scalar
                def _(act):
                    act.wait_ge(k.shift_ready.sem, k.shift_ready.at(1))
                    for tt in range(NT):
                        nc.scalar.activation(gexp[:, tt, :], lg[:, tt, 0:NG], ACT.Exp,
                                             bias=neg[:, tt, :], accum_out=gsum[:, tt, :]
                                             ).then_inc(k.exps_ready.up(), 1)
                    act.wait_ge(k.shift_ready.sem, k.shift_ready.at(2))
                    nc.scalar.activation(e2[:, :, :], e2[:, :, :], ACT.Exp).then_inc(k.exps_ready.up(), 1)
            run_products(k, [
                (None, [lambda ps, tt=tt: mm(k, ps[:, 0:NE], ones[:, 0, :], both[:, tt, :], tt == 0, tt == 1)
                        for tt in range(NT)], "v", [copy_out(k, num[:, :], P, NE)]),
                (None, [lambda ps: mm(k, ps[:, 0:NE], ones[:, 1, :], both[:, 0, :])], "v",
                 [copy_out(k, cum[:, 0, :], P, NE)]),
                (None, [lambda ps: mm(k, ps[:, 0:NE], ones[:, 0, :], both[:, 0, :], True, False),
                        lambda ps: mm(k, ps[:, 0:NE], ones[:, 1, :], both[:, 1, :], False, True)], "v",
                 [copy_out(k, cum[:, 1, :], P, NE)])])
            with k.stage() as block:
                @block.vector
                def _(dve):
                    v = nc.vector
                    k.v(v.tensor_tensor_scan(start[:, :], ones[:, 0, 0:NE], num[:, :], 0.0, ALU.mult, ALU.add))
                    k.v(v.tensor_tensor(start[:, :], start[:, :], num[:, :], ALU.subtract))
                    for tt in range(NT):
                        k.v(v.tensor_tensor(cum[:, tt, :], cum[:, tt, :], start[:, :], ALU.add))
                        for j in range(2):
                            k.v(v.tensor_tensor(both[:, j, :], one[:, j, tt, :], cum[:, tt, :], ALU.mult))
                            k.v(v.tensor_reduce(place[:, j, tt:tt + 1], both[:, j, :], AX, ALU.add))
                    k.v(v.tensor_scalar(win[:, 0, :], num[:, :], float(P), 1.0, ALU.is_gt, ALU.add))
                    k.v(v.tensor_tensor_scan(win[:, 2, :], ones[:, 0, 0:NE], win[:, 0, :], 0.0, ALU.mult, ALU.add))
                    k.v(v.tensor_tensor(win[:, 1, :], win[:, 2, :], win[:, 0, :], ALU.subtract))
                    k.v(v.scalar_tensor_tensor(out=win[:, 3, :], in0=win[:, 1, :], scalar=-float(P),
                                               in1=start[:, :], op0=ALU.mult, op1=ALU.add))
                    sh = [1, WINDOWS, NE]
                    w_ids = iota[0:1, 0:WINDOWS].unsqueeze(2).to_broadcast(sh)
                    per_e = lambda t: t.unsqueeze(1).to_broadcast(sh)
                    h0, h1 = hit[:, 0, :, :], hit[:, 1, :, :]
                    k.v(v.tensor_tensor(h0, w_ids, per_e(win[0:1, 1, :]), ALU.is_ge))
                    k.v(v.tensor_tensor(h1, w_ids, per_e(win[0:1, 2, :]), ALU.is_lt))
                    k.v(v.tensor_tensor(h0, h0, h1, ALU.mult))
                    k.v(v.tensor_tensor(h1, h0, per_e(iota[0:1, 0:NE]), ALU.mult))
                    k.v(v.tensor_reduce(tf[:, 0, 0:WINDOWS], h1, AX, ALU.add))
                    k.v(v.tensor_tensor(h1, h0, per_e(win[0:1, 3, :]), ALU.mult))
                    k.v(v.tensor_reduce(tf[:, 1, 0:WINDOWS], h1, AX, ALU.add))
                    k.v(v.scalar_tensor_tensor(out=tf[:, 1, 0:WINDOWS], in0=iota[0:1, 0:WINDOWS], scalar=float(P),
                                               in1=tf[:, 1, 0:WINDOWS], op0=ALU.mult, op1=ALU.add))
                    for j in range(2):
                        k.v(v.tensor_copy(tf[:, j, WINDOWS:WINDOWS + 1], win[0:1, 2, NE - 1:NE]))
                    k.v(v.tensor_copy(table[:, :, :], tf[:, :, :]))
                    for tt in range(NT):
                        k.v(v.tensor_scalar(half2[:, :], iota[:, :], place[:, 0, tt:tt + 1], None, ALU.is_equal))
                        k.v(v.scalar_tensor_tensor(out=sel[:, tt, :], in0=iota[:, :], scalar=place[:, 1, tt:tt + 1],
                                                   in1=half2[:, :], op0=ALU.is_equal, op1=ALU.add))
                        k.v(v.tensor_scalar(spread[:, tt, :], iota[:, :], place[:, 0, tt:tt + 1], g1[:, tt, 0:1],
                                            ALU.is_equal, ALU.mult))
                        k.v(v.tensor_scalar(half2[:, :], iota[:, :], place[:, 1, tt:tt + 1], g1[:, tt, 1:2],
                                            ALU.is_equal, ALU.mult))
                        k.v(v.tensor_tensor(spread[:, tt, :], spread[:, tt, :], half2[:, :], ALU.add))

                @block.gpsimd
                def _(pool):
                    nc.gpsimd.memset(rows_T[:, :, PAIRS:], 0.0).then_inc(k.act_step.up(), 1)
                    pool.wait_ge(k.act_step.sem, k.act_step.at(1))
            run_products(k, [(None, [lambda ps, tt=tt, ch=ch: mm(k, ps, x[:, tt, ch * P:(ch + 1) * P], sel[:, tt, :],
                                                                 tt == 0, tt == 1) for tt in range(NT)],
                              "va"[ch % 2], [copy_out(k, rows_T[:, ch, 0:PAIRS], P, PAIRS)]) for ch in range(DC)])
        with ExitStack() as c2:
            main_windows(k, first, layer, rows_T, outs_T, table, c2)
        load_norm()
        with ExitStack() as c2:
            late_windows(k, layer, rows_T, outs_T, table, c2)
        outs = sb("sorted_outputs", [P, PAIRS // P, D], ctx=c)
        back = sb("gate_of_place_T", [P, PAIRS // P, S], ctx=c)
        units = []
        for pc in range(PAIRS // P):
            units.append((None, [lambda ps, pc=pc, tt=tt: nc.tensor.transpose(
                ps[:, tt * P:(tt + 1) * P], spread[:, tt, pc * P:(pc + 1) * P], k.ident) for tt in range(NT)],
                "v", [copy_out(k, back[:, pc, :], P, S)]))
            for hf in range(2):
                units.append((None, [lambda ps, pc=pc, hf=hf, n=n: nc.tensor.transpose(
                    ps[:, n * P:(n + 1) * P], outs_T[:, 4 * hf + n, pc * P:(pc + 1) * P], k.ident)
                    for n in range(4)], "va"[hf], [copy_out(k, outs[:, pc, 512 * hf:512 * (hf + 1)], P, 512)]))
        run_products(k, units)
        run_products(k, [(None, [lambda ps, pc=pc, tt=tt, hf=hf: mm(
            k, ps, back[:, pc, tt * P:(tt + 1) * P], outs[:, pc, 512 * hf:512 * (hf + 1)], pc == 0,
            pc == PAIRS // P - 1) for pc in range(PAIRS // P)], "v",
            [residual(k, x, ALPHA, 512 * hf, 512)(tt)]) for tt in range(NT) for hf in range(2)])

def expert_part(k, flat, part):
    return flat.rearrange("p (c n) -> p c n", c=FF // P if part == 2 else DC)

def expert_source(k, layer, part, expert):
    return k.dram["moe_parts"][part][layer, bass.ds(expert, 1)].rearrange("a (c p) n -> p (a c) n", p=P)

def into_features(k, ps, w, rows):
    for m in range(FF // P):
        for ch in range(DC):
            last = mm(k, ps[:, m * P:(m + 1) * P], w[:, ch, m * P:(m + 1) * P], rows[:, ch, :], ch == 0, ch == DC - 1)
    return last

def out_of_features(k, ps2, w, hidden):
    for d in range(DC):
        for m in range(FF // P):
            last = mm(k, ps2[:, d // 4, (d % 4) * P:(d % 4 + 1) * P], w[:, m, d * P:(d + 1) * P],
                      hidden[:, m * P:(m + 1) * P], m == 0, m == FF // P - 1)
    return last

def main_windows(k, first, layer, rows_T, outs_T, table, c):
    nc, sb = k.nc, k.sb
    window = sb("window_rows_T", [P, 2, DC, P], ctx=c)
    silu = sb("silu_out", [P, 2, FF], ctx=c)
    hid = sb("expert_hidden", [P, 2, FF], ctx=c)
    TURN = 4
    turns = NE // TURN
    start_of = lambda eng, w: eng.value_load(table[0:1, 1, bass.ds(w, 1)], min_val=0, max_val=PAIRS)

    with k.stage() as block:
        LEFT = 3 * TURN - 3
        FIRST, LAST = 0, turns - 1

        def weights(pe, i, q):
            if q < 0 or (i is LAST and q > LEFT):
                tile, later = first + (q + 2 if q < 0 else 3 * NE - 1), 0
            else:
                tile, later = first + 2 + q, 3 * TURN // SLOTS * 16 * i
            pe.wait_ge(k.stream.landed[tile % SLOTS].sem, 16 * (tile // SLOTS + 1) + later)
            return expert_part(k, k.ring[:, tile % SLOTS, :], 2 if q >= 0 and q % 3 == 2 else (q + 2 if q < 0 else q % 3))

        def ups(pe, i, e, start, q):
            n = TURN * i + e
            pe.wait_ge(k.window_ready.sem, k.window_ready.at(n + 1))
            for part, ready, read in ((0, k.gate_products, k.silu_ready), (1, k.up_products, k.gated_ready)):
                w = weights(pe, i, q + part)
                if not start:
                    pe.wait_ge(read.sem, read.at(n - 1))
                into_features(k, k.ps[:, 2 * (e % 2) + part, :], w,
                              window[:, e % 2, :, :]).then_inc(ready.up(), 1)

        def downs(pe, i, e, start):
            n = TURN * i + e
            w = weights(pe, i, 3 * e + 2)
            pe.wait_ge(k.gated_ready.sem, k.gated_ready.at(n + 1))
            if not start:
                pe.wait_ge(k.dve_evacuated.sem, k.dve_evacuated.at(n - 1))
                pe.wait_ge(k.act_evacuated.sem, k.act_evacuated.at(n - 1))
            b = 4 + 2 * (e % 2)
            out_of_features(k, k.ps[:, b:b + 2, :], w, hid[:, e % 2, :]).then_inc(k.down_products.up(), 1)

        def pe_turn(pe, i, first_turn, last_turn):
            for e in range(TURN):
                if e < TURN - 1 or not last_turn:
                    ups(pe, i, e + 1, first_turn and e + 1 < 2, 3 * e)
                downs(pe, i, e, first_turn and e < 2)

        def place(eng, n, b, half, done, ordered=True):
            at = start_of(eng, n)
            eng.wait_ge(k.down_products.sem, k.down_products.at(n + 1))
            if ordered:
                eng.wait_ge(done.sem, done.at(n))
            dst = outs_T[:, 4 * half:4 * half + 4, bass.ds(at, P)]
            src = k.ps[:, 4 + 2 * b + half, :].rearrange("p (d n) -> p d n", d=4)
            ins = eng.tensor_copy(dst, src) if half == 0 else eng.activation(dst, src, ACT.Copy)
            ins.then_inc(done.up(), 1)

        def act_turn(act, i, start):
            for e in range(TURN):
                n = TURN * i + e
                act.wait_ge(k.gate_products.sem, k.gate_products.at(n + 1))
                if not (start and e < 2):
                    act.wait_ge(k.gated_ready.sem, k.gated_ready.at(n - 1))
                nc.scalar.activation(silu[:, e % 2, :], k.ps[:, 2 * (e % 2), :],
                                     ACT.Silu).then_inc(k.silu_ready.up(), 1)
                if not (start and e == 0):
                    place(act, n - 1, (e + 1) % 2, 1, k.act_evacuated, not (start and e == 1))

        def dve_turn(dve, i, start):
            for e in range(TURN):
                n = TURN * i + e
                dve.wait_ge(k.silu_ready.sem, k.silu_ready.at(n + 1))
                dve.wait_ge(k.up_products.sem, k.up_products.at(n + 1))
                if not (start and e < 2):
                    dve.wait_ge(k.down_products.sem, k.down_products.at(n - 1))
                nc.vector.tensor_tensor(hid[:, e % 2, :], silu[:, e % 2, :], k.ps[:, 2 * (e % 2) + 1, :],
                                        ALU.mult).then_inc(k.gated_ready.up(), 1)
                if not (start and e == 0):
                    place(dve, n - 1, (e + 1) % 2, 0, k.dve_evacuated, not (start and e == 1))

        def pool_turn(pool, i, start):
            for e in range(TURN):
                n = TURN * i + e
                at = start_of(pool, n)
                if not (start and e < 2):
                    pool.wait_ge(k.up_products.sem, k.up_products.at(n - 1))
                nc.gpsimd.tensor_copy(window[:, e % 2, :, :],
                                      rows_T[:, :, bass.ds(at, P)]).then_inc(k.window_ready.up(), 1)

        @block.sync
        def _(sp):
            def expert_of(w):
                return sp.value_load(table[0:1, 0, bass.ds(w, 1)], min_val=0, max_val=NE - 1)

            def load(t, expert, part):
                slot = (first + t) % SLOTS
                sp.dma_start(expert_part(k, k.ring[:, slot, :], part),
                             expert_source(k, layer, part, expert)).then_inc(k.stream.landed[slot].sem, 16)

            def used(i, q):
                e, part = divmod(q, 3)
                done = (k.gate_products, k.up_products, k.down_products)[part]
                sp.wait_ge(done.sem, done.at(TURN * i + e + (1 if part == 2 else 2)))

            def fill(i, q, tile):
                e, part = divmod(q, 3)
                expert = expert_of(TURN * i + e + (0 if part == 2 else 1))
                before = q - SLOTS
                if i is LAST and q > LEFT:
                    used(i, LEFT - SLOTS)
                elif before >= 0:
                    used(i, before)
                elif i is not FIRST:
                    used(i - 1, before + 3 * TURN)
                elif before >= -2:
                    done = (k.gate_products, k.up_products)[before + 2]
                    sp.wait_ge(done.sem, done.at(1))
                load(tile, expert, part)

            for q in range(3 * TURN):
                fill(FIRST, q, 2 + q)
            with sp.Fori(1, turns - 1) as i:
                for q in range(3 * TURN):
                    fill(i, q, 2 + q)
            for q in range(LEFT):
                fill(LAST, q, 2 + q)
            fill(LAST, 3 * TURN - 1, 3 * NE - 1)
            k.stream.issued = first + 3 * NE
            for q in (LEFT - 3, LEFT - 2, LEFT - 1, 3 * TURN - 1):
                used(LAST, q)
                if k.stream.issued < len(k.stream.sources):
                    k.stream.load(sp, k.stream.issued)
                    k.stream.issued += 1

        @block.gpsimd
        def _(pool):
            pool_turn(pool, 0, True)
            with pool.Fori(1, turns) as i:
                pool_turn(pool, i, False)
            k.window_ready.repeated(turns - 1, TURN)

        @block.tensor
        def _(pe):
            ups(pe, 0, 0, True, -2)
            pe_turn(pe, 0, True, False)
            with pe.Fori(1, turns - 1) as i:
                pe_turn(pe, i, False, False)
            for sig in (k.gate_products, k.up_products, k.down_products):
                sig.repeated(turns - 2, TURN)
            pe_turn(pe, LAST, False, True)

        @block.scalar
        def _(act):
            act_turn(act, 0, True)
            with act.Fori(1, turns) as i:
                act_turn(act, i, False)
            for sig in (k.silu_ready, k.act_evacuated):
                sig.repeated(turns - 1, TURN)
            place(act, NE - 1, 1, 1, k.act_evacuated)

        @block.vector
        def _(dve):
            dve_turn(dve, 0, True)
            with dve.Fori(1, turns) as i:
                dve_turn(dve, i, False)
            for sig in (k.gated_ready, k.dve_evacuated):
                sig.repeated(turns - 1, TURN)
            place(dve, NE - 1, 1, 0, k.dve_evacuated)

def late_windows(k, layer, rows_T, outs_T, table, c):
    nc, sb = k.nc, k.sb
    w_sb = sb("late_weights", [P, 3, SLOT], ctx=c)
    window = sb("late_rows_T", [P, DC, P], ctx=c)
    silu = sb("late_silu", [P, FF], ctx=c)
    hid = sb("late_hidden", [P, FF], ctx=c)
    landed, rows_in, up, silu_in, gated, down, placed_v, placed_a = (
        nc.alloc_semaphore(name=f"late_{n}_{layer}") for n in
        ("landed", "rows_in", "up", "silu_in", "gated", "down", "placed_v", "placed_a"))
    late = range(WINDOWS - NE)

    def exists(eng, n):
        count = eng.value_load(table[0:1, 0, WINDOWS:WINDOWS + 1], min_val=NE, max_val=WINDOWS)
        return eng.If(count > NE + n)

    start_of = lambda eng, n: eng.value_load(table[0:1, 1, NE + n:NE + n + 1], min_val=0, max_val=PAIRS)

    with k.stage() as block:
        @block.sync
        def _(sp):
            for n in late:
                with exists(sp, n):
                    if n:
                        sp.wait_ge(down, n)
                    expert = sp.value_load(table[0:1, 0, NE + n:NE + n + 1], min_val=0, max_val=NE - 1)
                    for part in range(3):
                        sp.dma_start(expert_part(k, w_sb[:, part, :], part),
                                     expert_source(k, layer, part, expert)).then_inc(landed, 16)
                    sp.wait_ge(landed, 48 * (n + 1))

        @block.gpsimd
        def _(pool):
            for n in late:
                with exists(pool, n):
                    if n:
                        pool.wait_ge(down, n)
                    nc.gpsimd.tensor_copy(window[:, :, :], rows_T[:, :, bass.ds(start_of(pool, n), P)]
                                          ).then_inc(rows_in, 1)
                    pool.wait_ge(rows_in, n + 1)

        @block.tensor
        def _(pe):
            for n in late:
                with exists(pe, n):
                    pe.wait_ge(landed, 48 * (n + 1))
                    pe.wait_ge(rows_in, n + 1)
                    into_features(k, k.ps[:, 0, :], expert_part(k, w_sb[:, 0, :], 0), window)
                    into_features(k, k.ps[:, 1, :], expert_part(k, w_sb[:, 1, :], 1), window).then_inc(up, 1)
                    pe.wait_ge(gated, n + 1)
                    if n:
                        pe.wait_ge(placed_v, n)
                        pe.wait_ge(placed_a, n)
                    out_of_features(k, k.ps[:, 2:4, :], expert_part(k, w_sb[:, 2, :], 2), hid).then_inc(down, 1)

        @block.scalar
        def _(act):
            for n in late:
                with exists(act, n):
                    act.wait_ge(up, n + 1)
                    nc.scalar.activation(silu[:, :], k.ps[:, 0, :], ACT.Silu).then_inc(silu_in, 1)
                    act.wait_ge(down, n + 1)
                    nc.scalar.activation(outs_T[:, 4:8, bass.ds(start_of(act, n), P)],
                                         k.ps[:, 3, :].rearrange("p (d n) -> p d n", d=4),
                                         ACT.Copy).then_inc(placed_a, 1)
                    act.wait_ge(placed_a, n + 1)

        @block.vector
        def _(dve):
            for n in late:
                with exists(dve, n):
                    dve.wait_ge(silu_in, n + 1)
                    nc.vector.tensor_tensor(hid[:, :], silu[:, :], k.ps[:, 1, :], ALU.mult).then_inc(gated, 1)
                    dve.wait_ge(down, n + 1)
                    nc.vector.tensor_copy(outs_T[:, 0:4, bass.ds(start_of(dve, n), P)],
                                          k.ps[:, 2, :].rearrange("p (d n) -> p d n", d=4)).then_inc(placed_v, 1)
                    dve.wait_ge(placed_v, n + 1)

def add_banks(k, x, alpha):
    with k.stage() as block:
        @block.vector
        def _(dve):
            for tt in range(NT):
                for half in range(2):
                    xs = x[:, tt, half * 512:(half + 1) * 512]
                    k.nc.vector.scalar_tensor_tensor(out=xs, in0=xs, scalar=alpha, in1=k.ps[:, 2 * tt + half, :],
                                                     op0=ALU.mult, op1=ALU.add).then_inc(k.dve_step.up(), 1)

def second_block(k, tiles, out):
    nc, sb = k.nc, k.sb
    keep = k.dram["x_rows"]
    with ExitStack() as c:
        cat_T = sb("mixed_2_T", [P, DC, S], ctx=c)
        with ExitStack() as c2:
            x = sb("x_first", [P, NT, D], ctx=c2)
            load_small(k, [(x[:, :, :], keep)])
            add_banks(k, x, 1.0)
            store(k, [(keep, x[:, :, :])], wait=False)
            turn(k, x, DC, cat_T)
            store(k, [])
        rwkv_and_gating(k, tiles, cat_T, cat_T)
        x = sb("x_second", [P, NT, D], ctx=c)
        gb = sb("ln_gain_bias", [P, 2, D], ctx=c)

        def load_rows(n, layer):
            load_small(k, [(gb[:, j, :], k.dram[f"ln{n}_{m}_2"][layer].partition_broadcast(P))
                           for j, m in enumerate("gb")], wait=False)
        NL = NG + NE
        router = (sb("router_weights", [P, DC, NL], ctx=c), sb("router_bias", [P, NL], ctx=c),
                  sb("router_iota", [P, PAIRS], ctx=c),
                  sb("router_ones", [P, 2, P], ctx=c))

        def load_router(layer):
            w, bias, iota, ones = router
            load_small(k, [(w[:, :, 0:NG], k.dram["moe_w_group_2"][layer].rearrange("(c p) n -> p c n", p=P)),
                           (w[:, :, NG:NL], k.dram["moe_w_expert_2"][layer].rearrange("(c p) n -> p c n", p=P)),
                           (bias[:, 0:NG], k.dram["moe_b_group_2"][layer].partition_broadcast(P)),
                           (bias[:, NG:NL], k.dram["moe_b_expert_2"][layer].partition_broadcast(P)),
                           (iota[:, :], k.const("iota")[:, 0:PAIRS]),
                           (ones[:, 0, :], k.const("ones")), (ones[:, 1, :], k.const("before"))], wait=False)
        load_small(k, [(x[:, :, :], keep)], wait=False)
        load_rows(1, 0)
        load_small(k, [])
        project_residual(k, cat_T, DC, tiles["ab_out"], x, ALPHA)
        hT = sb("h_T", [P, DC, S], ctx=c)
        for layer in range(2):
            if layer == 1:
                mla(k, x, hT, tiles, lambda: load_rows(1, 1))
            layer_norm(k, x, gb)
            turn(k, x, DC, hT)
            cross_attention(k, x, hT, layer, tiles, lambda: (load_rows(2, layer), load_router(layer)))
            layer_norm(k, x, gb)
            turn(k, x, DC, hT)
            moe(k, x, hT, layer, tiles, router, lambda: load_rows(3, layer))
            layer_norm(k, x, gb)
            if layer == 0:
                turn(k, x, DC, hT)
        store(k, [(out.rearrange("a (t p) d -> p (a t) d", p=P), x[:, :, :])])

def build(nc, dram, out):
    with ExitStack() as ctx:
        k = Kernel(nc, dram, ctx)

        def columns(w, width=512):
            n = w.shape[1]
            v = w.rearrange("(c p) n -> p c n", p=P)
            return [v[:, :, j:min(j + width, n)] for j in range(0, n, width)]

        def wt(name, layer=0):
            return dram[name][layer]
        st, tiles = k.stream, {}
        tiles["w_in"] = st.add(columns(wt("w_in")))
        tiles["w_mem_kv"] = st.add(columns(wt("w_mem_kv")))
        tiles["w_out"] = st.add(columns(wt("w_out")))
        tiles["w_peer_q"] = st.add(columns(wt("w_peer_q")))
        for layer in range(2):
            tiles.setdefault("xa_kv", st.add(columns(wt("xa_wkv_2", layer))))
        st.hold = len(st.sources)
        w = wt("ab_w_in_2")
        tiles["ab_in"] = st.add(columns(w[:, 0:1536]) + columns(w[:, 1536:1792]) + columns(w[:, 1792:2816]))
        tiles["ab_out"] = st.add(columns(wt("ab_w_out_2")))

        def tail(layer):
            tiles[f"xa{layer}"] = st.add(columns(wt("xa_wq_2", layer)) + columns(wt("xa_wo_2", layer)))
            parts = []
            for e in range(NE):
                for m in k.dram["moe_parts"]:
                    parts += columns(m[layer, e], 1024)
            tiles[f"moe{layer}"] = st.add(parts[0:2] + [None] * (len(parts) - 2))
        tail(0)
        tiles["mla_in"] = st.add(columns(wt("mla_w_in_2")) + columns(wt("mla_wq_b_2"), 2048)
                                 + columns(wt("mla_wkv_b_2"), 2048) + columns(wt("mla_w_out_2")))
        tail(1)
        first_block(k, tiles)
        second_block(k, tiles, out)

PLAIN = ["x", "mem", "w_in", "w_mem_kv", "w_out", "w_peer_q", "ab_w_in_2", "rw_w2_2", "rw_a2_2", "rw_g2_2",
         "rw_gn_g_2", "rw_gn_b_2", "sg_ln_g_2", "sg_ln_b_2", "ab_w_out_2", "mla_w_in_2", "mla_wq_b_2",
         "mla_wkv_b_2", "mla_w_out_2", "ln1_g_2", "ln1_b_2", "xa_wq_2", "xa_wkv_2", "xa_wo_2", "ln2_g_2",
         "ln2_b_2", "moe_w_group_2", "moe_b_group_2", "moe_w_expert_2", "moe_b_expert_2", "moe_w_gate_2",
         "moe_w_up_2", "moe_w_down_2", "ln3_g_2", "ln3_b_2"]

def laid_out(inputs):
    a = {n: np.ascontiguousarray(inputs[n]) for n in PLAIN}
    for n in (1, 2):
        a[f"subkeys_T_{n}"] = np.ascontiguousarray(np.asarray(inputs[f"peer_subkeys_{n}"])[0].transpose(2, 0, 1))
    u = np.asarray(inputs["peer_u"])[0].reshape(PK, PK, DC, P).transpose(1, 3, 2, 0)
    a["peer_u_T"] = np.ascontiguousarray(u).reshape(PK, P, D)
    a["peer_v_rows"] = np.ascontiguousarray(np.asarray(inputs["peer_v"])[0].reshape(PK, PK, D).transpose(1, 0, 2))
    a["sg_ws_T"] = np.ascontiguousarray(np.asarray(inputs["sg_ws_2"])[0].transpose(2, 0, 1))
    a["mem_2_T"] = np.ascontiguousarray(np.asarray(inputs["mem_2"])[0].T.reshape(DC, P, S).transpose(1, 0, 2))
    cols = []
    for name, src, rows, n in vector_columns():
        m = np.asarray(inputs[src]).reshape(n, rows).T
        cols.append(np.concatenate([m, np.zeros((P - rows, n), m.dtype)], 0))
    a["columns"] = np.ascontiguousarray(np.concatenate(cols, 1))
    a["consts"] = shape_constants()[1]
    return a

def kernel(**inputs):
    import concourse.bacc as bacc
    from concourse.bass_utils import run_bass_kernel_spmd

    nc = bacc.Bacc("TRN2", target_bir_lowering=False, num_devices=1)
    arrays = laid_out(inputs)
    dram = {n: nc.dram_tensor(f"in_{n}", a.shape, F32, kind="ExternalInput").ap() for n, a in arrays.items()}
    for n, shape in (("x_rows", [P, NT, D]), ("h_T", [P, DC, S]), ("slots", [P, 3, S]),
                     ("xa_k_T", [2, P, DC, S]), ("xa_v", [2, P, NT, D])):
        dram[n] = nc.dram_tensor(n, shape, F32, kind="Internal").ap()
    dram["moe_parts"] = [dram["moe_w_gate_2"], dram["moe_w_up_2"], dram["moe_w_down_2"]]
    out = nc.dram_tensor("out_rows", [1, S, D], F32, kind="ExternalOutput").ap()
    build(nc, dram, out)
    r = run_bass_kernel_spmd(nc, [{f"in_{n}": a for n, a in arrays.items()}], core_ids=[0])
    return r.results[0]["out_rows"]
```
